# Optimizing a Trainium2 kernel written in Bass

```python
import math
import jax, jax.numpy as jnp
from jax import lax
import numpy as np

D_MODEL = 1024
BATCH = 1
SEQ = 512
DEPTH = 1

HEAD_DIM = 64
N_SB = 4
N_MOBA = 4
N_FOX = 4
N_DSA = 4
BRANCH_W = 4 * HEAD_DIM
N_BRANCH = 4
Q_BLOCK = 128
MOBA_BLOCK = 256
MOBA_TOPK = 3
MOBA_Q_CHUNK = 32
DSA_TOPK = 256
IDX_HEADS = 8
IDX_DIM = 32
T5_BUCKETS = 32
T5_MAX_DIST = 128
D_FF = 2816
CONV_W = 3
RMS_EPS = 1e-6
NEG_BIG = -1e30

IN_SIZES = (
    [BRANCH_W] * 3
    + [BRANCH_W] * 3
    + [BRANCH_W] * 3 + [N_FOX]
    + [BRANCH_W, HEAD_DIM, HEAD_DIM]
    + [IDX_HEADS * IDX_DIM, IDX_DIM, IDX_HEADS]
)
P_IN = int(sum(IN_SIZES))
IN_SPLITS = tuple(int(v) for v in np.cumsum(IN_SIZES)[:-1])


def rmsnorm(x, g):
    xf = x.astype(jnp.float32)
    y = xf * lax.rsqrt(jnp.mean(xf * xf, axis=-1, keepdims=True) + RMS_EPS)
    return (y * g.astype(jnp.float32)).astype(x.dtype)

def to_heads(t, n):
    b, s, _ = t.shape
    return t.reshape(b, s, n, HEAD_DIM).transpose(0, 2, 1, 3)

def merge_heads(o):
    b, h, s, d = o.shape
    return o.transpose(0, 2, 1, 3).reshape(b, s, h * d)

def t5_bucket(n):
    n = jnp.maximum(n, 0)
    max_exact = T5_BUCKETS // 2
    nf = jnp.maximum(n, 1).astype(jnp.float32)
    large = max_exact + (jnp.log(nf / max_exact) / math.log(T5_MAX_DIST / max_exact)
                         * (T5_BUCKETS - max_exact)).astype(jnp.int32)
    large = jnp.minimum(large, T5_BUCKETS - 1)
    return jnp.where(n < max_exact, n, large)

def stick_breaking_attention(q, k, v):
    s_len = q.shape[2]
    scale = HEAD_DIM ** -0.5
    outs = []
    for i in range(s_len // Q_BLOCK):
        t0, t1 = i * Q_BLOCK, (i + 1) * Q_BLOCK
        z = jnp.einsum('bhqd,bhkd->bhqk', q[:, :, t0:t1], k[:, :, :t1]).astype(jnp.float32) * scale
        strict = jnp.arange(t1)[None, :] < jnp.arange(t0, t1)[:, None]
        log_neg = jnp.where(strict, jax.nn.log_sigmoid(-z), 0.0)
        excl = lax.cumsum(log_neg, axis=3, reverse=True) - log_neg
        w = jnp.where(strict, jnp.exp(jax.nn.log_sigmoid(z) + excl), 0.0)
        outs.append(jnp.einsum('bhqk,bhkd->bhqd', w.astype(v.dtype), v[:, :, :t1]))
    return jnp.concatenate(outs, axis=2)

def forgetting_attention(q, k, v, f_logit):
    s_len = q.shape[2]
    scale = HEAD_DIM ** -0.5
    c = jnp.cumsum(jax.nn.log_sigmoid(f_logit.astype(jnp.float32)), axis=1).transpose(0, 2, 1)
    outs = []
    for i in range(s_len // Q_BLOCK):
        t0, t1 = i * Q_BLOCK, (i + 1) * Q_BLOCK
        logits = jnp.einsum('bhqd,bhkd->bhqk', q[:, :, t0:t1], k[:, :, :t1]).astype(jnp.float32) * scale
        logits = logits + c[:, :, t0:t1, None] - c[:, :, None, :t1]
        causal = jnp.arange(t1)[None, :] <= jnp.arange(t0, t1)[:, None]
        p = jax.nn.softmax(jnp.where(causal, logits, NEG_BIG), axis=-1)
        outs.append(jnp.einsum('bhqk,bhkd->bhqd', p.astype(v.dtype), v[:, :, :t1]))
    return jnp.concatenate(outs, axis=2)

def moba_attention(q, k, v, bias_table):
    b, h, s_len, d = q.shape
    scale = HEAD_DIM ** -0.5
    nb = -(-s_len // MOBA_BLOCK)
    pad = nb * MOBA_BLOCK - s_len
    kp = jnp.pad(k, ((0, 0), (0, 0), (0, pad), (0, 0)))
    vp = jnp.pad(v, ((0, 0), (0, 0), (0, pad), (0, 0)))
    kb = kp.reshape(b, h, nb, MOBA_BLOCK, d)
    vb = vp.reshape(b, h, nb, MOBA_BLOCK, d)
    kmean = jnp.mean(kb.astype(jnp.float32), axis=3).astype(k.dtype)
    topk = min(MOBA_TOPK, nb)
    table_t = bias_table.T
    bi = jnp.arange(b)[:, None, None, None]
    hi = jnp.arange(h)[None, :, None, None]

    def chunk(ci):
        t0 = ci * MOBA_Q_CHUNK
        qc = lax.dynamic_slice_in_dim(q, t0, MOBA_Q_CHUNK, axis=2)
        tpos = t0 + jnp.arange(MOBA_Q_CHUNK)
        own = t0 // MOBA_BLOCK
        gate = jnp.einsum('bhqd,bhnd->bhqn', qc, kmean).astype(jnp.float32)
        past = jnp.arange(nb) < own
        gate = jnp.where(past, gate, -jnp.inf)
        _, gidx = lax.top_k(gate, topk)
        sel_valid = gidx < own
        ks = kb[bi, hi, gidx]
        vs = vb[bi, hi, gidx]
        s_sel = jnp.einsum('bhqd,bhqnkd->bhqnk', qc, ks).astype(jnp.float32) * scale
        kpos = gidx[..., None] * MOBA_BLOCK + jnp.arange(MOBA_BLOCK)
        bucket = t5_bucket(tpos[None, None, :, None, None] - kpos)
        s_sel = s_sel + table_t[hi[..., None], bucket].astype(jnp.float32)
        s_sel = jnp.where(sel_valid[..., None], s_sel, NEG_BIG)
        ko = lax.dynamic_slice_in_dim(kp, own * MOBA_BLOCK, MOBA_BLOCK, axis=2)
        vo = lax.dynamic_slice_in_dim(vp, own * MOBA_BLOCK, MOBA_BLOCK, axis=2)
        kpos_own = own * MOBA_BLOCK + jnp.arange(MOBA_BLOCK)
        dist_own = tpos[:, None] - kpos_own[None, :]
        s_own = jnp.einsum('bhqd,bhkd->bhqk', qc, ko).astype(jnp.float32) * scale
        s_own = s_own + table_t[:, t5_bucket(dist_own)].astype(jnp.float32)[None]
        s_own = jnp.where(dist_own >= 0, s_own, NEG_BIG)
        logits = jnp.concatenate([s_sel.reshape(b, h, MOBA_Q_CHUNK, topk * MOBA_BLOCK), s_own], axis=-1)
        p = jax.nn.softmax(logits, axis=-1).astype(v.dtype)
        p_sel = p[..., :topk * MOBA_BLOCK].reshape(b, h, MOBA_Q_CHUNK, topk, MOBA_BLOCK)
        p_own = p[..., topk * MOBA_BLOCK:]
        return (jnp.einsum('bhqnk,bhqnkd->bhqd', p_sel, vs)
                + jnp.einsum('bhqk,bhkd->bhqd', p_own, vo))

    out = lax.map(chunk, jnp.arange(s_len // MOBA_Q_CHUNK))
    return out.transpose(1, 2, 0, 3, 4).reshape(b, h, s_len, d)

def dsa_attention(q, k, v, q_idx, k_idx, w_idx, bias_table):
    b, h, s_len, d = q.shape
    scale = HEAD_DIM ** -0.5
    ksel = min(DSA_TOPK, s_len // 4)
    table_t = bias_table.T
    bi = jnp.arange(b)[:, None, None]
    outs = []
    for i in range(s_len // Q_BLOCK):
        t0, t1 = i * Q_BLOCK, (i + 1) * Q_BLOCK
        kk = min(ksel, t1)
        tpos = jnp.arange(t0, t1)
        isc = jax.nn.relu(jnp.einsum('bqhe,bke->bqhk', q_idx[:, t0:t1], k_idx[:, :t1]))
        isc = jnp.einsum('bqh,bqhk->bqk', w_idx[:, t0:t1], isc).astype(jnp.float32)
        admissible = jnp.arange(t1)[None, :] <= tpos[:, None]
        _, idx = lax.top_k(jnp.where(admissible, isc, -jnp.inf), kk)
        dist = tpos[None, :, None] - idx
        ks = k[bi, idx]
        vs = v[bi, idx]
        logits = jnp.einsum('bhqd,bqkd->bhqk', q[:, :, t0:t1], ks).astype(jnp.float32) * scale
        logits = logits + table_t[:, t5_bucket(dist)].transpose(1, 0, 2, 3).astype(jnp.float32)
        logits = jnp.where((dist >= 0)[:, None], logits, NEG_BIG)
        p = jax.nn.softmax(logits, axis=-1).astype(v.dtype)
        outs.append(jnp.einsum('bhqk,bqkd->bhqd', p, vs))
    return jnp.concatenate(outs, axis=2)

def token_mixer(xn, w_in, fox_b_f, t5_bias, w_gate, w_branch, w_out):
    b, s_len, _ = xn.shape
    proj = xn @ w_in
    (sb_q, sb_k, sb_v, mb_q, mb_k, mb_v, fx_q, fx_k, fx_v, fx_f,
     ds_q, ds_k, ds_v, ix_q, ix_k, ix_w) = jnp.split(proj, IN_SPLITS, axis=-1)
    o_sb = stick_breaking_attention(to_heads(sb_q, N_SB), to_heads(sb_k, N_SB), to_heads(sb_v, N_SB))
    o_mb = moba_attention(to_heads(mb_q, N_MOBA), to_heads(mb_k, N_MOBA), to_heads(mb_v, N_MOBA),
                          t5_bias[:, :N_MOBA])
    o_fx = forgetting_attention(to_heads(fx_q, N_FOX), to_heads(fx_k, N_FOX), to_heads(fx_v, N_FOX),
                                fx_f + fox_b_f)
    o_ds = dsa_attention(to_heads(ds_q, N_DSA), ds_k, ds_v,
                         ix_q.reshape(b, s_len, IDX_HEADS, IDX_DIM), ix_k, ix_w, t5_bias[:, N_MOBA:])
    branches = (o_sb, o_mb, o_fx, o_ds)
    mixed = None
    for i in range(N_BRANCH):
        y = jax.nn.sigmoid(xn @ w_gate[i]) * (merge_heads(branches[i]) @ w_branch[i])
        mixed = y if mixed is None else mixed + y
    return mixed @ w_out

def conv_ffn(xn, w_up, conv_w, conv_b, w_down):
    s_len = xn.shape[1]
    hdn = xn @ w_up
    hp = jnp.pad(hdn, ((0, 0), (CONV_W - 1, 0), (0, 0)))
    acc = conv_b
    for j in range(CONV_W):
        acc = acc + conv_w[j] * hp[:, j:j + s_len]
    g, u = jnp.split(acc, 2, axis=-1)
    return (jax.nn.gelu(g, approximate=False) * u) @ w_down

def first_inputs(seed: int = 0) -> dict:
    key = jax.random.key(seed)
    ks = jax.random.split(key, 14)
    nrm = jax.random.normal
    f32 = jnp.float32
    return {
        "x": nrm(ks[0], (BATCH, SEQ, D_MODEL), f32),
        "norm_mix_g": 1.0 + 0.02 * nrm(ks[1], (DEPTH, D_MODEL), f32),
        "norm_ffn_g": 1.0 + 0.02 * nrm(ks[2], (DEPTH, D_MODEL), f32),
        "norm_final_g": 1.0 + 0.02 * nrm(ks[3], (D_MODEL,), f32),
        "w_in": nrm(ks[4], (DEPTH, D_MODEL, P_IN), f32) * D_MODEL ** -0.5,
        "fox_b_f": 1.0 + 0.1 * nrm(ks[5], (DEPTH, N_FOX), f32),
        "t5_bias": 0.5 * nrm(ks[6], (T5_BUCKETS, N_MOBA + N_DSA), f32),
        "w_gate": nrm(ks[7], (DEPTH, N_BRANCH, D_MODEL, D_MODEL), f32) * D_MODEL ** -0.5,
        "w_branch": nrm(ks[8], (DEPTH, N_BRANCH, BRANCH_W, D_MODEL), f32) * BRANCH_W ** -0.5,
        "w_out": nrm(ks[9], (DEPTH, D_MODEL, D_MODEL), f32) * D_MODEL ** -0.5,
        "w_up": nrm(ks[10], (DEPTH, D_MODEL, 2 * D_FF), f32) * D_MODEL ** -0.5,
        "conv_w": nrm(ks[11], (DEPTH, CONV_W, 2 * D_FF), f32) * CONV_W ** -0.5,
        "conv_b": 0.01 * nrm(ks[12], (DEPTH, 2 * D_FF), f32),
        "w_down": nrm(ks[13], (DEPTH, D_FF, D_MODEL), f32) * D_FF ** -0.5,
    }

def first_block(x, norm_mix_g, norm_ffn_g, norm_final_g, w_in, fox_b_f, t5_bias,
              w_gate, w_branch, w_out, w_up, conv_w, conv_b, w_down):
    for l in range(DEPTH):
        x = x + token_mixer(rmsnorm(x, norm_mix_g[l]), w_in[l], fox_b_f[l], t5_bias,
                            w_gate[l], w_branch[l], w_out[l])
        x = x + conv_ffn(rmsnorm(x, norm_ffn_g[l]), w_up[l], conv_w[l], conv_b[l], w_down[l])
    return rmsnorm(x, norm_final_g)


DEPTH_2 = 2

MIX_WIDTH = D_MODEL
N_GROUPS = 4
GROUP_WIDTH = MIX_WIDTH // N_GROUPS
EPS = 1e-6
ROPE_THETA = 10000.0

MLA_HEADS = 4
MLA_NOPE = 64
MLA_ROPE = 32
MLA_V = GROUP_WIDTH // MLA_HEADS
MLA_Q_LORA = 256
MLA_KV_LORA = 128
ATTN_BLOCK = 128

SG_HEADS = 4
SG_CHUNK = 128
SG_HALF = GROUP_WIDTH

HG_HEADS = 4
HG_KEY = 128
HG_VAL = GROUP_WIDTH // HG_HEADS
HG_CHUNK = 64

RET_HEADS = 4
RET_QK = 64
RET_V = GROUP_WIDTH // RET_HEADS
RET_CHUNK = 128

PLE_DIM = 256

IN_SPLITS_2 = (MLA_Q_LORA, MLA_KV_LORA, MLA_ROPE,
             SG_HALF, SG_HALF,
             HG_HEADS * HG_KEY, HG_HEADS * HG_KEY, HG_HEADS * HG_VAL, HG_HEADS * HG_VAL,
             RET_HEADS * RET_QK, RET_HEADS * RET_QK, RET_HEADS * RET_V, RET_HEADS * RET_V)
IN_WIDTH = sum(IN_SPLITS_2)


def rmsnorm_2(x, g):
    xf = x.astype(jnp.float32)
    y = xf * lax.rsqrt(jnp.mean(xf * xf, axis=-1, keepdims=True) + EPS)
    return (y * g.astype(jnp.float32)).astype(x.dtype)

def layernorm(x, g):
    xf = x.astype(jnp.float32)
    xc = xf - jnp.mean(xf, axis=-1, keepdims=True)
    y = xc * lax.rsqrt(jnp.mean(xc * xc, axis=-1, keepdims=True) + EPS)
    return (y * g.astype(jnp.float32)).astype(x.dtype)

def swiglu(x, w_gate, w_up, w_down):
    return (jax.nn.silu(x @ w_gate) * (x @ w_up)) @ w_down

def rope(x, positions):
    d = x.shape[-1]
    inv = ROPE_THETA ** (-jnp.arange(0, d, 2, dtype=jnp.float32) / d)
    ang = positions.astype(jnp.float32)[..., None] * inv
    cos = jnp.cos(ang)[:, :, None, :]
    sin = jnp.sin(ang)[:, :, None, :]
    x1, x2 = jnp.split(x.astype(jnp.float32), 2, axis=-1)
    return jnp.concatenate([x1 * cos - x2 * sin, x1 * sin + x2 * cos], axis=-1).astype(x.dtype)

def mla_mixer(c_q, c_kv, k_pe, positions, q_norm, w_uq, kv_norm, w_ukv):
    B, S, _ = c_q.shape
    q = (rmsnorm_2(c_q, q_norm) @ w_uq).reshape(B, S, MLA_HEADS, MLA_NOPE + MLA_ROPE)
    q = jnp.concatenate([q[..., :MLA_NOPE], rope(q[..., MLA_NOPE:], positions)], axis=-1)
    kv = (rmsnorm_2(c_kv, kv_norm) @ w_ukv).reshape(B, S, MLA_HEADS, MLA_NOPE + MLA_V)
    k_rot = rope(k_pe[:, :, None, :], positions)
    k = jnp.concatenate([kv[..., :MLA_NOPE],
                         jnp.broadcast_to(k_rot, (B, S, MLA_HEADS, MLA_ROPE))], axis=-1)
    v = kv[..., MLA_NOPE:]
    scale = (MLA_NOPE + MLA_ROPE) ** -0.5
    nb = S // ATTN_BLOCK
    qb = (q * scale).reshape(B, nb, ATTN_BLOCK, MLA_HEADS, MLA_NOPE + MLA_ROPE).transpose(1, 0, 3, 2, 4)
    kh = k.transpose(0, 2, 1, 3)
    vh = v.transpose(0, 2, 1, 3)
    key_idx = jnp.arange(S)

    def query_block(args):
        q_blk, bi = args
        s = jnp.einsum('bhqd,bhkd->bhqk', q_blk, kh).astype(jnp.float32)
        q_idx = bi * ATTN_BLOCK + jnp.arange(ATTN_BLOCK)
        s = jnp.where(key_idx[None, :] <= q_idx[:, None], s, -jnp.inf)
        pr = jax.nn.softmax(s, axis=-1).astype(vh.dtype)
        return jnp.einsum('bhqk,bhkd->bhqd', pr, vh)

    o = lax.map(query_block, (qb, jnp.arange(nb)))
    return o.transpose(1, 0, 3, 2, 4).reshape(B, S, MLA_HEADS * MLA_V)

def spatial_gating_mixer(z_u, z_v, ln_g, w_s, b_s):
    B, S, _ = z_u.shape
    u = jax.nn.gelu(z_u, approximate=False)
    v = layernorm(jax.nn.gelu(z_v, approximate=False), ln_g)
    n = S // SG_CHUNK
    vh = v.reshape(B, n, SG_CHUNK, SG_HEADS, SG_HALF // SG_HEADS)
    causal = jnp.tril(jnp.ones((SG_CHUNK, SG_CHUNK), dtype=bool))
    w = jnp.where(causal[None], w_s, 0.0).astype(v.dtype)
    mixed = jnp.einsum('hts,bnshd->bnthd', w, vh) + b_s.T[None, None, :, :, None]
    return u * mixed.reshape(B, S, SG_HALF)

def hgrn2_mixer(q, f, i, g, lb, norm_g):
    B, S, _ = q.shape
    f32 = jnp.float32
    forget = lb + (1.0 - lb) * jax.nn.sigmoid(f.astype(f32))
    log_f = jnp.log(forget)
    k = 1.0 - forget
    n = S // HG_CHUNK

    def chunks(t, d):
        return t.astype(f32).reshape(B, n, HG_CHUNK, HG_HEADS, d).transpose(1, 0, 3, 2, 4)

    qc, kc, gc = chunks(q, HG_KEY), chunks(k, HG_KEY), chunks(log_f, HG_KEY)
    vc = chunks(i, HG_VAL)
    causal = jnp.tril(jnp.ones((HG_CHUNK, HG_CHUNK), dtype=bool))[None, None, :, :, None]

    def step(state, inp):
        qt, kt, vt, gt = inp
        b = jnp.cumsum(gt, axis=2)
        diff = jnp.where(causal, b[:, :, :, None, :] - b[:, :, None, :, :], -jnp.inf)
        scores = jnp.einsum('bhtk,bhtsk,bhsk->bhts', qt, jnp.exp(diff), kt)
        o = (jnp.einsum('bhts,bhsv->bhtv', scores, vt)
             + jnp.einsum('bhtk,bhkv->bhtv', qt * jnp.exp(b), state))
        b_last = b[:, :, -1:, :]
        new_state = (jnp.exp(b_last[:, :, 0, :])[..., None] * state
                     + jnp.einsum('bhsk,bhsv->bhkv', kt * jnp.exp(b_last - b), vt))
        return new_state, o

    state0 = jnp.zeros((B, HG_HEADS, HG_KEY, HG_VAL), f32)
    _, o = lax.scan(step, state0, (qc, kc, vc, gc))
    o = o.transpose(1, 0, 3, 2, 4).reshape(B, S, HG_HEADS, HG_VAL)
    o = o * lax.rsqrt(jnp.mean(o * o, axis=-1, keepdims=True) + EPS) * norm_g.astype(f32).reshape(HG_HEADS, HG_VAL)
    gate = jax.nn.silu(g.astype(f32)).reshape(B, S, HG_HEADS, HG_VAL)
    return (o * gate).reshape(B, S, HG_HEADS * HG_VAL).astype(q.dtype)

def retention_mixer(q, k, v, g, positions, norm_g):
    B, S, _ = q.shape
    f32 = jnp.float32
    H, C = RET_HEADS, RET_CHUNK
    n = S // C
    qr = rope(q.reshape(B, S, H, RET_QK), positions).astype(f32)
    kr = rope(k.reshape(B, S, H, RET_QK), positions).astype(f32) * (RET_QK ** -0.5)
    vr = v.reshape(B, S, H, RET_V).astype(f32)

    def chunks(t):
        return t.reshape(B, n, C, H, t.shape[-1]).transpose(0, 3, 1, 2, 4)

    qh, kh, vh = chunks(qr), chunks(kr), chunks(vr)
    lg = jnp.log1p(-jnp.power(2.0, -(5.0 + jnp.arange(H, dtype=f32))))
    pos = jnp.arange(C, dtype=f32)
    rel = pos[:, None] - pos[None, :]
    decay = jnp.where(rel >= 0, jnp.exp(jnp.maximum(rel, 0.0)[None] * lg[:, None, None]), 0.0)
    scores = jnp.einsum('bhntd,bhnsd->bhnts', qh, kh) * decay[None, :, None]
    o = jnp.einsum('bhnts,bhnse->bhnte', scores, vh)
    k_dec = kh * jnp.exp((C - 1.0 - pos)[None, :] * lg[:, None])[None, :, None, :, None]
    kv = jnp.einsum('bhnsd,bhnse->bhnde', k_dec, vh)
    cidx = jnp.arange(n, dtype=f32)
    gap = cidx[:, None] - 1.0 - cidx[None, :]
    cross = jnp.where(gap >= 0, jnp.exp(C * jnp.maximum(gap, 0.0)[None] * lg[:, None, None]), 0.0)
    state = jnp.einsum('hnm,bhmde->bhnde', cross, kv)
    q_dec = qh * jnp.exp((pos + 1.0)[None, :] * lg[:, None])[None, :, None, :, None]
    o = o + jnp.einsum('bhntd,bhnde->bhnte', q_dec, state)
    o = o.transpose(0, 2, 3, 1, 4).reshape(B, S, H, RET_V)
    oc = o - jnp.mean(o, axis=-1, keepdims=True)
    o = oc * lax.rsqrt(jnp.mean(oc * oc, axis=-1, keepdims=True) + EPS) * norm_g.astype(f32).reshape(H, RET_V)
    gate = jax.nn.silu(g.astype(f32)).reshape(B, S, H, RET_V)
    return (o * gate).reshape(B, S, H * RET_V).astype(q.dtype)

def second_inputs(seed: int = 0) -> dict:
    key = jax.random.key(seed)
    ks = iter(jax.random.split(key, 40))
    f32 = jnp.float32

    def nrm(shape, scale):
        return jax.random.normal(next(ks), shape, f32) * scale

    def gain(shape):
        return 1.0 + 0.01 * jax.random.normal(next(ks), shape, f32)

    L, D = DEPTH_2, D_MODEL
    return {
        'x': nrm((BATCH, SEQ, D), 1.0),
        'p': nrm((DEPTH_2, BATCH, SEQ, PLE_DIM), 1.0),
        'positions': jnp.broadcast_to(jnp.arange(SEQ, dtype=jnp.int32), (BATCH, SEQ)),
        'ffn1_norm': gain((L, D)),
        'ffn1_w_gate': nrm((L, D, D_FF), D ** -0.5),
        'ffn1_w_up': nrm((L, D, D_FF), D ** -0.5),
        'ffn1_w_down': nrm((L, D_FF, D), D_FF ** -0.5),
        'mix_norm': gain((L, D)),
        'w_in': nrm((L, D, IN_WIDTH), D ** -0.5),
        'mla_q_norm': gain((L, MLA_Q_LORA)),
        'mla_w_uq': nrm((L, MLA_Q_LORA, MLA_HEADS * (MLA_NOPE + MLA_ROPE)), MLA_Q_LORA ** -0.5),
        'mla_kv_norm': gain((L, MLA_KV_LORA)),
        'mla_w_ukv': nrm((L, MLA_KV_LORA, MLA_HEADS * (MLA_NOPE + MLA_V)), MLA_KV_LORA ** -0.5),
        'sg_ln': gain((L, SG_HALF)),
        'sg_w_s': nrm((L, SG_HEADS, SG_CHUNK, SG_CHUNK), 0.5 * SG_CHUNK ** -0.5),
        'sg_b_s': 1.0 + nrm((L, SG_HEADS, SG_CHUNK), 0.1),
        'hg_lb_logits': nrm((L, HG_HEADS * HG_KEY), 1.0),
        'hg_norm': gain((L, HG_HEADS * HG_VAL)),
        'ret_norm': gain((L, RET_HEADS * RET_V)),
        'w_out': nrm((L, MIX_WIDTH, D), MIX_WIDTH ** -0.5),
        'ffn2_norm': gain((L, D)),
        'ffn2_w_gate': nrm((L, D, D_FF), D ** -0.5),
        'ffn2_w_up': nrm((L, D, D_FF), D ** -0.5),
        'ffn2_w_down': nrm((L, D_FF, D), D_FF ** -0.5),
        'ple_norm': gain((L, D)),
        'ple_w_proj': nrm((L, PLE_DIM, D), PLE_DIM ** -0.5),
        'ple_w_gate': nrm((L, D, D), D ** -0.5),
        'final_norm': gain((D,)),
    }

def second_block(x, p, positions, ffn1_norm, ffn1_w_gate, ffn1_w_up, ffn1_w_down,
              mix_norm, w_in, mla_q_norm, mla_w_uq, mla_kv_norm, mla_w_ukv,
              sg_ln, sg_w_s, sg_b_s, hg_lb_logits, hg_norm, ret_norm, w_out,
              ffn2_norm, ffn2_w_gate, ffn2_w_up, ffn2_w_down,
              ple_norm, ple_w_proj, ple_w_gate, final_norm):
    split_points = np.cumsum(IN_SPLITS_2)[:-1].tolist()
    lb_all = jnp.cumsum(jax.nn.softmax(hg_lb_logits.astype(jnp.float32), axis=0), axis=0)
    lb_all = lb_all - lb_all[0:1]
    h = x
    for l in range(DEPTH_2):
        h = h + 0.5 * swiglu(rmsnorm_2(h, ffn1_norm[l]), ffn1_w_gate[l], ffn1_w_up[l], ffn1_w_down[l])
        z = rmsnorm_2(h, mix_norm[l]) @ w_in[l]
        (c_q, c_kv, k_pe, z_u, z_v, hq, hf, hi, hg,
         rq, rk, rv, rg) = jnp.split(z, split_points, axis=-1)
        y_a = mla_mixer(c_q, c_kv, k_pe, positions, mla_q_norm[l], mla_w_uq[l], mla_kv_norm[l], mla_w_ukv[l])
        y_b = spatial_gating_mixer(z_u, z_v, sg_ln[l], sg_w_s[l], sg_b_s[l])
        y_c = hgrn2_mixer(hq, hf, hi, hg, lb_all[l], hg_norm[l])
        y_d = retention_mixer(rq, rk, rv, rg, positions, ret_norm[l])
        h = h + jnp.concatenate([y_a, y_b, y_c, y_d], axis=-1) @ w_out[l]
        h = h + 0.5 * swiglu(rmsnorm_2(h, ffn2_norm[l]), ffn2_w_gate[l], ffn2_w_up[l], ffn2_w_down[l])
        gate = jax.nn.sigmoid(rmsnorm_2(h, ple_norm[l]) @ ple_w_gate[l])
        h = h + (p[l] @ ple_w_proj[l]) * gate
    return rmsnorm_2(h, final_norm)


_first_inputs = second_inputs


def second_inputs(seed=0):
    import zlib

    import numpy as np

    out = dict(_first_inputs(seed))
    spreads = {}
    factors = {'ffn1_norm': 8.0,
     'mix_norm': 4.967,
     'mla_q_norm': 8.0,
     'mla_kv_norm': 8.0,
     'sg_ln': 8.0,
     'hg_norm': 8.0,
     'ret_norm': 8.0,
     'ffn2_norm': 8.0,
     'ple_norm': 8.0,
     'final_norm': 5.601}
    for name, (base, spread) in spreads.items():
        noise = np.random.default_rng([zlib.crc32(name.encode()), seed]).standard_normal(out[name].shape)
        drawn = base * np.exp(spread * noise) if base else spread * noise
        out[name] = __import__('jax').numpy.asarray(drawn.astype(out[name].dtype))
    for name, factor in factors.items():
        out[name] = (out[name] * factor).astype(out[name].dtype)
    return out


_narrow_inputs = second_inputs


def second_inputs(seed=0):
    out = dict(_narrow_inputs(seed))
    wider = {'mla_q_norm': 3.6,
     'mla_kv_norm': 3.42,
     'sg_ln': 12.0,
     'sg_b_s': 5.27,
     'hg_norm': 6.34,
     'ret_norm': 6.73,
     'ffn2_norm': 3.96,
     'ple_norm': 12.0,
     'final_norm': 6.28}
    for name, times in wider.items():
        mean = out[name].mean()
        out[name] = (mean + times * (out[name] - mean)).astype(out[name].dtype)
    return out


def setup_inputs(seed=0):
    out = dict(first_inputs(seed))
    for name, value in second_inputs(seed + 1).items():
        if name != "x":
            out[name + "_2"] = value
    return out


def reference(
    x, norm_mix_g, norm_ffn_g, norm_final_g, w_in, fox_b_f, t5_bias, w_gate, w_branch, w_out,
    w_up, conv_w, conv_b, w_down, p_2, positions_2, ffn1_norm_2, ffn1_w_gate_2, ffn1_w_up_2,
    ffn1_w_down_2, mix_norm_2, w_in_2, mla_q_norm_2, mla_w_uq_2, mla_kv_norm_2, mla_w_ukv_2,
    sg_ln_2, sg_w_s_2, sg_b_s_2, hg_lb_logits_2, hg_norm_2, ret_norm_2, w_out_2, ffn2_norm_2,
    ffn2_w_gate_2, ffn2_w_up_2, ffn2_w_down_2, ple_norm_2, ple_w_proj_2, ple_w_gate_2,
    final_norm_2,
):
    x = first_block(
        x, norm_mix_g, norm_ffn_g, norm_final_g, w_in, fox_b_f, t5_bias, w_gate, w_branch,
        w_out, w_up, conv_w, conv_b, w_down,
    )
    return second_block(
        x, p_2, positions_2, ffn1_norm_2, ffn1_w_gate_2, ffn1_w_up_2, ffn1_w_down_2, mix_norm_2,
        w_in_2, mla_q_norm_2, mla_w_uq_2, mla_kv_norm_2, mla_w_ukv_2, sg_ln_2, sg_w_s_2,
        sg_b_s_2, hg_lb_logits_2, hg_norm_2, ret_norm_2, w_out_2, ffn2_norm_2, ffn2_w_gate_2,
        ffn2_w_up_2, ffn2_w_down_2, ple_norm_2, ple_w_proj_2, ple_w_gate_2, final_norm_2,
    )


_drawn_inputs = setup_inputs


def setup_inputs(seed=0):
    import zlib

    import numpy as np

    out = dict(_drawn_inputs(seed))
    spreads = {}
    factors = {}
    for name, (base, spread) in spreads.items():
        noise = np.random.default_rng([zlib.crc32(name.encode()), seed]).standard_normal(out[name].shape)
        drawn = base * np.exp(spread * noise) if base else spread * noise
        out[name] = __import__('jax').numpy.asarray(drawn.astype(out[name].dtype))
    for name, factor in factors.items():
        out[name] = (out[name] * factor).astype(out[name].dtype)
    return out
```

```python
from contextlib import ExitStack

import numpy as np

import concourse.bass as bass
from concourse import mybir

F32 = mybir.dt.float32
I32 = mybir.dt.int32
ACT = mybir.ActivationFunctionType
ALU = mybir.AluOpType
AX = mybir.AxisListType

P = 128
S = 512
TT = S // P
D = 1024
DC = D // P
FF = 2816
FC = FF // P
HD = 64
NH = 4
LAYERS = 2
EPS = 1e-6
NEG = -1e30
GONE = -3e38
TOPK = 128
KEYS = 128
PLE = 256
MLA_D = 96
TWO_PI = 2.0 * float(np.pi)
LEVELS = [64, 32, 16, 8, 4, 2, 1]

A_COLS = dict(sbq=0, sbk=256, sbv=512, mbq=768, mbk=1024, mbv=1280, fxq=1536, fxk=1792, fxv=2048,
              fxf=2304, dsq=2308, dsk=2564, dsv=2628, ixq=2692, ixk=2948, ixw=2980)
B_COLS = dict(cq=0, ckv=256, zu=416, zv=672, hq=928, hf=1440, hi=1952, hg=2208,
              rq=2464, rk=2720, rv=2976, rg=3232)
A_ROWS = dict(mix=0, ffn=8, fin1=16, fin2=24, conv_b=32)
A_NROWS = 32 + 2 * FC
L_ROWS = dict(ffn1=0, mix=8, q=16, kv=18, sg=19, lb=21, hg=25, ret=27, ffn2=29, ple=37)
L_NROWS = 45


def t5_bucket(n):
    n = np.maximum(n, 0)
    large = 16 + (np.log(np.maximum(n, 1) / 16.0) / np.log(8.0) * 16).astype(np.int64)
    return np.where(n < 16, n, np.minimum(large, 31))


def constants():
    p = np.arange(P)
    c = {}
    c["ident"] = np.eye(P)
    c["flip"] = np.eye(P)[::-1]
    c["causal"] = np.where(p[None, :] > p[:, None], NEG, 0.0)
    c["strict"] = np.where(p[None, :] >= p[:, None], NEG, 0.0)
    swap = np.zeros((P, P))
    swap[p, p // 64 * 64 + (p % 64 + 32) % 64] = 1.0
    c["swap"] = swap
    swap32 = np.zeros((P, P))
    swap32[64 + np.arange(32), 64 + (np.arange(32) + 16) % 32] = 1.0
    c["swap32"] = swap32
    c["group"] = np.where(p[:, None] // 64 == p[None, :] // 64, 1.0 / 64, 0.0)
    lev = [(p[None, :] // m % 2 == 1) & (p[:, None] // m == p[None, :] // m - 1) for m in LEVELS]
    lev.append(p[:, None] == p[None, :])
    c["levels"] = np.concatenate([x.astype(float) for x in lev], 1)
    c["tril"] = (p[:, None] <= p[None, :]).astype(float)
    c["resets"] = np.tile((np.arange(S) % P != 0).astype(float), (P, 1))
    onehot = np.zeros((P, 640))
    onehot[t5_bucket(511 - np.arange(640)), np.arange(640)] = 1.0
    c["onehot"] = onehot
    f32 = np.float32
    inv64 = (f32(10000.0) ** (-np.arange(0, 64, 2, dtype=f32) / f32(64))).astype(f32)
    inv32 = (f32(10000.0) ** (-np.arange(0, 32, 2, dtype=f32) / f32(32))).astype(f32)
    cols = np.zeros((P, 4))
    cols[:, 0] = inv64[p % 32]
    cols[:, 1] = np.where(p % 64 < 32, -1.0, 1.0)
    cols[:, 2] = inv32[p % 16]
    cols[:, 3] = np.where(p % 32 < 16, -1.0, 1.0)
    c["cols"] = cols
    headsel = np.zeros((P, 2, P))
    for h in range(NH):
        headsel[h, h // 2, (h % 2) * 64:(h % 2) * 64 + 64] = 1.0
    c["headsel"] = headsel.reshape(P, -1)
    pick = np.zeros((P, 2, NH, P))
    for h in range(NH):
        pick[h, 0, h, :] = 1.0
        pick[h, 1, h, :] = -1.0
    c["pick"] = pick.reshape(P, -1)
    return {k: np.asarray(v, np.float32) for k, v in c.items()}


def decays():
    p, u = np.arange(P)[:, None], np.arange(S)[None, :]
    f32 = np.float32
    lg = np.log1p(-np.power(f32(2.0), -(f32(5.0) + np.arange(NH, dtype=f32)))).astype(f32)
    d = [np.where(u >= p, np.exp(np.maximum(u - p, 0).astype(f32) * g), 0.0) for g in lg]
    return np.concatenate(d, 1).astype(f32)


CONST_AT = {}
_n = 0
for _name, _a in constants().items():
    CONST_AT[_name] = (_n, _a.shape[1])
    _n += _a.shape[1]
CONST_N = _n


class Book:

    def __init__(self, known=None):
        self.marks = {}
        self.body = {}
        self.trips = {}
        self.known = known


class Count:

    def __init__(self, book, sem, name, unit=1):
        self.book, self.sem, self.name, self.unit = book, sem, name, unit
        self.n = 0
        self.loops = []

    def enter(self, loop):
        self.loops.append((loop, self.n))

    def leave(self, trips):
        loop, start = self.loops.pop()
        self.book.body[loop, self.name] = self.n - start
        self.book.trips[loop] = trips
        self.n = start + (self.n - start) * trips

    def up(self, *what):
        self.n += self.unit
        if what:
            assert what not in self.book.marks, what
            self.book.marks[what] = (self.sem, self.name, self.n, tuple(x for x, _ in self.loops))
        return self.sem, self.unit


class Engine(Count):

    def __init__(self, book, sem, name):
        super().__init__(book, sem, name)
        self.regs = {}
        self.others = []
        self.slabs = [[], []]
        self.slab_no = 0

    def begin(self, loop, reg):
        self.regs[loop] = reg
        for c in (self, *self.others):
            c.enter(loop)

    def end(self, loop, trips):
        for c in (self, *self.others):
            c.leave(trips)
        del self.regs[loop]

    def value(self, sem_name, n, loops, prev=None):
        known = self.book.known
        v, terms = n, []
        for loop in loops:
            stride = known.body[loop, sem_name] if known else 0
            if loop in self.regs:
                terms.append((self.regs[loop], stride))
                if loop == prev:
                    v -= stride
            elif known:
                v += stride * (known.trips[loop] - 1)
        for reg, stride in terms:
            if stride:
                v = reg * stride + v
        return v

    def at(self, *what, prev=None):
        known = self.book.known
        if known is None:
            return self.sem, 1
        _, name, n, loops = known.marks[what]
        return self.book.sems[name], self.value(name, n, loops, prev)

    def last(self):
        return self.sem, self.value(self.name, self.n, [x for x, _ in self.loops])


class Fori:

    def __init__(self, e, eng, loop, trips):
        self.e, self.loop, self.trips = e, loop, trips
        self.inner = eng.Fori(0, trips)

    def __enter__(self):
        reg = self.inner.__enter__()
        self.e.begin(self.loop, reg)
        return reg

    def __exit__(self, *a):
        self.e.end(self.loop, self.trips)
        return self.inner.__exit__(*a)


def program(nc, x, out, k, scratch, book):
    ctx = ExitStack()

    def sb(name, shape, dt=F32):
        return ctx.enter_context(nc.sbuf_tensor(name, shape, dt))

    def sem(name):
        return ctx.enter_context(nc.semaphore(name))

    h = sb("h", [P, DC, S])
    xn = sb("xn", [P, DC, S])
    ring = sb("ring", [P, 2, FC * 256])
    const = sb("const", [P, CONST_N])
    pcol = sb("pcol", [P, A_NROWS // 4 * 4])
    convw = sb("convw", [P, 3, 2 * FC])
    lcol = sb("lcol", [P, LAYERS * L_NROWS])
    lbs = sb("lbs", [P, LAYERS, 2, NH])
    cur = sb("cur", [P, L_NROWS + 8])
    ones = sb("ones", [P, 3, P])
    nrm = sb("nrm", [P, 3, S])
    stat = sb("stat", [P, 2, 4])
    eps = sb("eps", [P, 1])
    arena = sb("arena", [P, 26200])

    def C(name, rows=slice(0, P)):
        a, n = CONST_AT[name]
        return const[rows, a:a + n]

    spot = [0]

    def area(n, at=None):
        if at is not None:
            spot[0] = at
        a = spot[0]
        spot[0] += n
        assert spot[0] <= 26200, spot[0]
        return arena[:, a:a + n]

    def chunks(a, n=2):
        return a.rearrange("p (c t) -> p c t", c=n)

    xraw = area(4096, 8192).rearrange("p (i d) -> p i d", i=TT)
    rows_a = area(P)
    rows_c = area(3 * P).rearrange("p (j q) -> p j q", j=3)
    rows_l = area(P)
    t5_in = area(8)
    t5_rev = area(640)
    t5_rows = area(4096, 14200).rearrange("p (h u) -> p h u", h=8)
    sbo = chunks(area(1024, 0))
    sbq, sbk, mbq = chunks(area(1024)), chunks(area(1024)), chunks(area(1024))
    mixed = chunks(arena[:, spot[0]:spot[0] + 4096], DC)
    mbk, fxq, fxk, dsq = (chunks(area(1024)) for _ in range(4))
    sbv, mbv, fxv = (area(1024).rearrange("p (i d) -> p i d", i=TT) for _ in range(3))
    dsk = area(512)
    ixq = chunks(area(1024))
    ixk = area(512)
    dsv = area(TT * 72).rearrange("p (i d) -> p i d", i=TT)
    cum = area(512)
    prob = chunks(area(1024))
    probT = chunks(area(1024))
    soft = chunks(area(1024))
    sel = chunks(area(1536), 3)
    gates = chunks(area(1024), 2)
    top8 = area(8)
    one512 = area(512)
    zlog = area(512)
    bias = area(4096, 22000).rearrange("p (h u) -> p h u", h=8)
    branch_out = [sbo, sbq, sbk, mbq]
    hidden = chunks(area(FC * S, 0), FC)
    padded = chunks(area(4 * 514), 4)
    conv = chunks(area(4 * S), 4)
    silu = chunks(area(2 * S), 2)
    decay = area(NH * S, 22000).rearrange("p (h u) -> p h u", h=NH)
    rope = area(4 * S).rearrange("p (h u) -> p h u", h=4)
    pos_i = area(S, 17000)
    rtmp = chunks(area(4 * S), 4)
    cq = chunks(area(1024, 0))
    ckv = area(512)
    zu, zv = chunks(area(1024)), area(1024).rearrange("p (i d) -> p i d", i=TT)
    hq, hS, hk = chunks(area(2048), 4), chunks(area(2048), 4), chunks(area(2048), 4)
    hi = area(1024).rearrange("p (i d) -> p i d", i=TT)
    hgate = chunks(area(1024))
    rq, rk = chunks(area(1024)), chunks(area(1024))
    rv = area(1024).rearrange("p (i d) -> p i d", i=TT)
    rgate = chunks(area(1024))
    mv = area(1024).rearrange("p (i d) -> p i d", i=TT)
    sgw = area(512).rearrange("p (h s) -> p h s", h=NH)
    sgwT = area(512).rearrange("p (h s) -> p h s", h=NH)
    sgb = area(P)
    sgbb = chunks(area(256))
    sgst = area(TT * 8).rearrange("p (i d) -> p i d", i=TT)
    scratch_at = spot[0]
    lprob, lprobT = chunks(area(1024)), chunks(area(1024))
    gn = chunks(area(1024))
    mla_end = spot[0]
    kh = hk
    qh = xn[:, 0:NH, :]
    off = area(768, scratch_at)
    kd = area(512)
    kv3 = area(384)
    dend = area(4)
    hE, hQ, hK = xn[:, 0:2, :], xn[:, 2:4, :], xn[:, 4:6, :]
    scT, qd = xn[:, 6, :], xn[:, 7, :]
    assert max(mla_end, spot[0]) <= 22000, (mla_end, spot[0])
    pin = area(1024, 0).rearrange("p (i d) -> p i d", i=TT)
    pT = chunks(area(1024))
    sg8 = chunks(area(1024))
    outrow = area(4096, 0).rearrange("p (i d) -> p i d", i=TT)

    bank = [ctx.enter_context(nc.psum_tensor(f"bank{i}", [P, S], F32)) for i in range(8)]
    SC, PT, OB = bank[4:6], bank[6], bank[7]

    names = ["tensor_done", "vector_done", "scalar_done", "slab0", "slab1", "loads", "spills", "stores"]
    book.sems = {n: sem(n) for n in names}
    T = Engine(book, book.sems["tensor_done"], "tensor_done")
    V = Engine(book, book.sems["vector_done"], "vector_done")
    A = Engine(book, book.sems["scalar_done"], "scalar_done")
    Q = Engine(book, book.sems["stores"], "stores")
    slab_in = [Count(book, book.sems[f"slab{s}"], f"slab{s}", 16) for s in range(2)]
    loads = Count(book, book.sems["loads"], "loads", 16)
    spills = Count(book, book.sems["spills"], "spills", 16)
    Q.unit = 16
    Q.others = [*slab_in, loads]
    A.others = [spills]

    block = ctx.enter_context(nc.Block())

    ident = C("ident")

    @block.sync
    def _(sp):
        def load(dst, src, *what):
            sp.dma_start(dst, src).then_inc(*loads.up(*what))

        def rowload(dst, src, n):
            load(dst[0:n, :], src.rearrange("(c q) -> c q", q=P))

        slabs = [[], []]
        turn = [0]

        def slab(key, parts):
            s = turn[0] % 2
            turn[0] += 1
            for older, prev in slabs[s]:
                sp.wait_ge(*Q.at("gemm", *older, prev=prev))
            for i, (dst, src) in enumerate(parts):
                up = slab_in[s].up(*(("slab", *key) if i == len(parts) - 1 else ()))
                sp.dma_start(dst(ring[:, s, :]), src).then_inc(*up)
            slabs[s] = [(key, None)]

        def cols(w, c0, n, at=0, width=256, kc=DC):
            def dst(r):
                return r[:, 0:kc * width].rearrange("p (k c) -> p k c", k=kc)[:, :, at:at + n]
            return dst, w.rearrange("(k p) c -> p k c", p=P)[:, :, bass.ds(c0, n)]

        def half(w, c0, lo, hi, kc):
            def dst(r):
                return r[:, 0:kc * 256].rearrange("p (k c) -> p k c", k=kc)[:, lo:hi, :]
            return dst, w.rearrange("(k p) c -> p k c", p=P)[:, lo:hi, bass.ds(c0, 256)]

        def full(w, c0, kc=DC):
            return [half(w, c0, 0, kc // 2, kc), half(w, c0, kc // 2, kc, kc)]

        load(xraw, x.rearrange("(i p) d -> p i d", p=P), "x")
        load(const[:, :], k["const"])
        rowload(rows_a, k["norm_mix_g"][0], 8)
        rowload(rows_a[8:16], k["norm_ffn_g"][0], 8)
        rowload(rows_a[16:24], k["norm_final_g"], 8)
        rowload(rows_a[24:32], k["final_norm_2"], 8)
        rowload(rows_a[32:76], k["conv_b"][0], 2 * FC)
        for j in range(3):
            rowload(rows_c[:, j, :], k["conv_w"][0, j], 2 * FC)
        for l in range(LAYERS):
            for name, at, n in (("ffn1_norm_2", 0, 8), ("mix_norm_2", 8, 8), ("mla_q_norm_2", 16, 2),
                                ("mla_kv_norm_2", 18, 1), ("sg_ln_2", 19, 2), ("hg_lb_logits_2", 21, 4),
                                ("hg_norm_2", 25, 2), ("ret_norm_2", 27, 2), ("ffn2_norm_2", 29, 8),
                                ("ple_norm_2", 37, 8)):
                rowload(rows_l[l * L_NROWS + at:], k[name][l], n)
        load(t5_in[0:32, :], k["t5_bias"])
        load(cur[0:4, 49:50], k["fox_b_f"].rearrange("a h -> h a"), "params")

        w = k["w_in"][0]
        for name in ("sbq", "sbk", "sbv", "mbq", "mbk", "mbv", "fxq", "fxk", "fxv", "dsq"):
            slab((name,), full(w, A_COLS[name]))
        slab(("ix",), [cols(w, A_COLS["ixq"], 256)])
        slab(("dskv",), [cols(w, A_COLS["dsk"], 128), cols(w, A_COLS["ixw"], 8, 128)])
        slab(("ixkf",), [cols(w, A_COLS["ixk"], 32), cols(w, A_COLS["fxf"], 4, 32)])
        gate_w = k["w_gate"][0]
        branch_w = k["w_branch"][0]

        def gate_slab(key, gw, bw, c0):
            def gate_dst(r):
                return r[:, 0:DC * P].rearrange("p (k c) -> p k c", k=DC)

            def branch_dst(r):
                return r[:, DC * P:(DC + 2) * P].rearrange("p (k c) -> p k c", k=2)
            slab(key, [(gate_dst, gw.rearrange("(k p) c -> p k c", p=P)[:, :, bass.ds(c0, P)]),
                       (branch_dst, bw.rearrange("(k p) c -> p k c", p=P)[:, :, bass.ds(c0, P)])])

        def loop(name, trips, keys):
            f = Fori(Q, sp, name, trips)
            for i, key in enumerate(keys):
                slabs[(turn[0] + i) % 2] = [(key, name)]
            return f

        with loop("gates", DC, [("gate", 2), ("gate", 3)]) as it:
            for b in range(4):
                gate_slab(("gate", b), gate_w[b], branch_w[b], it * P)

        def proj(tag, w):
            with loop(tag, 2, [(tag, 0), (tag, 1)]) as it:
                for j in range(2):
                    slab((tag, j), full(w, it * 512 + j * 256))

        def ffn(tag, w_gate, w_up, w_down):
            with loop(tag + "u", FC // 2, [(tag + "u", 0), (tag + "u", 1)]) as it:
                for j in range(2):
                    slab((tag + "u", j), [cols(w_gate, it * 256 + j * P, P), cols(w_up, it * 256 + j * P, P, P)])
            with loop(tag + "d", 2, [(tag + "d", 0), (tag + "d", 1)]) as it:
                for j in range(2):
                    slab((tag + "d", j), full(w_down, it * 512 + j * 256, FC))

        proj("out", k["w_out"][0])
        up = k["w_up"][0]
        sp.wait_ge(*Q.at("evac", "gate", 3))
        load(pos_i[:, :].bitcast(I32), k["positions_2"].to_broadcast([P, S]), "pos")
        load(decay, k["decay"].rearrange("p (h u) -> p h u", h=NH), "decay")
        ffn("c", up[:, 0:FF], up[:, FF:2 * FF], k["w_down"][0])

        with loop("layer", LAYERS, [("ple", 0), ("ple", 1)]) as l:
            def at_layer(name):
                a = k[name + "_2"][bass.ds(l, 1)]
                while len(a.shape) > 2:
                    a = a.rearrange("a b c -> (a b) c") if len(a.shape) == 3 else a.rearrange("a b c d -> (a b) c d")
                return a

            ffn("f", at_layer("ffn1_w_gate"), at_layer("ffn1_w_up"), at_layer("ffn1_w_down"))
            w = at_layer("w_in")
            slab(("cq",), full(w, B_COLS["cq"]))
            slab(("ckv",), [cols(w, B_COLS["ckv"], 160)])
            sp.wait_ge(*Q.at("evac", "fd", 1))
            load(sgw, at_layer("sg_w_s").rearrange("(h t) s -> t h s", h=NH))
            load(sgb[0:NH, :], at_layer("sg_b_s"), "sg")
            for name, n in (("hf", 2), ("hq", 2), ("hi", 1), ("hg", 1), ("zu", 1), ("zv", 1),
                            ("rq", 1), ("rk", 1), ("rv", 1), ("rg", 1)):
                for j in range(n):
                    slab((name, j), full(w, B_COLS[name] + 256 * j))
            for j in range(2):
                slab(("uq", j), [cols(at_layer("mla_w_uq"), 192 * j, 192, 0, 192, 2)])
            ukv = at_layer("mla_w_ukv").rearrange("p (h c) -> p h c", h=NH)
            slab(("uk",), [(lambda r: r[:, 0:256].rearrange("p (h c) -> p h c", h=NH), ukv[:, :, 0:HD])])
            slab(("uv",), [(lambda r: r[:, 0:256].rearrange("p (h c) -> p h c", h=NH), ukv[:, :, HD:P])])
            proj("lout", at_layer("w_out"))
            ffn("g", at_layer("ffn2_w_gate"), at_layer("ffn2_w_up"), at_layer("ffn2_w_down"))
            sp.wait_ge(*Q.at("evac", "gd", 1))
            load(pin, at_layer("p").rearrange("(i q) d -> q i d", q=P), "pin")
            pg, pp = at_layer("ple_w_gate"), at_layer("ple_w_proj")
            with loop("ple", DC // 2, [("ple", 0), ("ple", 1)]) as it:
                for j in range(2):
                    gate_slab(("ple", j), pg, pp, it * 256 + j * P)

        sp.wait_ge(*Q.at("out_ready"))
        sp.dma_start(out.rearrange("(i p) d -> p i d", p=P), outrow).then_inc(*Q.up("stored"))
        sp.wait_ge(*Q.last())

    @block.tensor
    def _(pe):
        slabs = [[], []]
        turn = [0]

        def slab_start(key):
            s = turn[0] % 2
            turn[0] += 1
            pe.wait_ge(*T.at("slab", *key))
            for older, prev in slabs[s]:
                pe.wait_ge(*T.at("evac", *older, prev=prev))
            slabs[s] = [(key, None)]
            return s

        def loop(name, trips, keys):
            f = Fori(T, pe, name, trips)
            for i, key in enumerate(keys):
                slabs[(turn[0] + i) % 2] = [(key, name)]
            return f

        def hold():
            pe.matmul(PT[:, 0:4], ident, ident[:, 0:4], start=True, stop=True)

        def gemm_fm(key, rhs, outs, width=256, ready=None):
            s = slab_start(key)
            kc = len(rhs)
            for n, (b, lo, hi, c0, at) in enumerate(outs):
                w = ring[:, s, at:at + kc * width].rearrange("p (k c) -> p k c", k=kc)
                for i in range(kc):
                    if ready and n == 0:
                        pe.wait_ge(*T.at(*ready, i))
                    ins = pe.matmul(bank[2 * s + b][lo:hi, :], w[:, i, c0:c0 + hi - lo], rhs[i],
                                    start=(i == 0), stop=(i == kc - 1))
            ins.then_inc(*T.up("gemm", *key))

        def gemm_tm(key, lhs, n=256, c0=0, width=256, extra=None):
            s = slab_start(key)
            kc = len(lhs)
            w = ring[:, s, 0:kc * width].rearrange("p (k c) -> p k c", k=kc)
            if extra:
                extra(s, w)
            per = TT // 2 if n == 256 else TT
            for i in range(TT):
                b = i // per if n == 256 else 1
                for j in range(kc):
                    ins = pe.matmul(bank[2 * s + b][:, (i % per) * n:(i % per) * n + n], lhs[j][:, i * P:i * P + P],
                                    w[:, j, c0:c0 + n], start=(j == 0), stop=(j == kc - 1))
            ins.then_inc(*T.up("gemm", *key))

        pair = [(0, 0, P, 0, 0), (1, 0, P, P, 0)]
        xk = [xn[:, i, :] for i in range(DC)]

        def norm(tag, src, one):
            for i, a in enumerate(src):
                pe.wait_ge(*T.at("sq", tag, i))
                ins = pe.matmul(SC[0][:, :], ones[:, one, :], a, start=(i == 0), stop=(i == len(src) - 1))
            ins.then_inc(*T.up("ms", tag))

        def group_norm(tag, c, centred):
            if centred:
                pe.wait_ge(*T.at("gin", tag, c))
                pe.matmul(PT[:, :], C("group"), gn[:, 0, :], start=True, stop=True).then_inc(*T.up("gmean", tag, c))
            pe.wait_ge(*T.at("gsq", tag, c))
            pe.matmul(PT[:, :], C("group"), gn[:, 1, :], start=True, stop=True).then_inc(*T.up("gms", tag, c))

        def attention(tag, score, value, mode):
            def scores(u):
                hh, i = u // TT, u % TT
                if u >= 2:
                    pe.wait_ge(*T.at("score_used", tag, u - 2))
                score(SC[u % 2], hh, i).then_inc(*T.up("score", tag, u))

            scores(0)
            scores(1)
            for u in range(NH * TT):
                hh, i = u // TT, u % TT
                pe.wait_ge(*T.at("prob", tag, u))
                if u >= 1:
                    pe.wait_ge(*T.at("probT", tag, u - 1))
                p = (prob if mode == 1 else lprob)[:, u % 2, :]
                pt = (probT if mode == 1 else lprobT)[:, u % 2, :]
                for j in range(i + 1):
                    ins = pe.transpose(PT[:, j * P:j * P + P], p[:, j * P:j * P + P], ident)
                ins.then_inc(*T.up("turned", tag, u))
                if u + 2 < NH * TT:
                    scores(u + 2)
                pe.wait_ge(*T.at("probT", tag, u))
                r = hh % 2 * HD
                for j in range(i + 1):
                    ins = pe.matmul(OB[r:r + HD, i * P:i * P + P], value(hh, j), pt[:, j * P:j * P + P],
                                    start=(j == 0), stop=(j == i))
                ins.then_inc(*T.up("pv", tag, u))

        pe.wait_ge(*T.at("params"))
        for c in range(DC):
            if c >= 2:
                pe.wait_ge(*T.at("x_in", c - 2))
            for i in range(TT):
                ins = pe.transpose(SC[c % 2][:, i * P:i * P + P], xraw[:, i, c * P:c * P + P], ident)
            ins.then_inc(*T.up("x_turned", c))
        pe.transpose(PT[:, 0:A_NROWS], rows_a[0:A_NROWS, :], ident[0:A_NROWS, 0:A_NROWS])
        for j in range(3):
            pe.transpose(PT[:, 128 + 44 * j:172 + 44 * j], rows_c[0:44, j, :], ident[0:44, 0:44])
        n = LAYERS * L_NROWS
        pe.transpose(PT[:, 264:264 + n], rows_l[0:n, :], ident[0:n, 0:n]).then_inc(*T.up("cols_turned"))
        pe.matmul(OB[0:8, :], t5_in[0:32, :], C("onehot", slice(0, 32))[:, 0:512], start=True, stop=True)\
            .then_inc(*T.up("t5a"))
        pe.wait_ge(*T.at("cols_in"))
        pe.matmul(PT[0:8, 0:128], t5_in[0:32, :], C("onehot", slice(0, 32))[:, 512:640], start=True, stop=True)\
            .then_inc(*T.up("t5b"))
        pe.wait_ge(*T.at("x_in", DC - 1))
        norm("mix", xk, 0)
        for name in ("sbq", "sbk", "sbv", "mbq", "mbk", "mbv", "fxq", "fxk", "fxv", "dsq"):
            if name[2] == "v":
                gemm_tm((name,), xk)
            else:
                gemm_fm((name,), xk, pair, ready=("xn", "mix") if name == "sbq" else None)
        gemm_fm(("ix",), xk, pair)

        def dsk_twice(s, w):
            for r in (0, HD):
                for i in range(DC):
                    pe.matmul(bank[2 * s][r:r + HD, :], w[:, i, 0:HD], xk[i], start=(i == 0), stop=(i == DC - 1))
        gemm_tm(("dskv",), xk, 72, HD, 256, dsk_twice)
        gemm_fm(("ixkf",), xk, [(0, 32 * r, 32 * r + 32, 0, 0) for r in range(4)] + [(1, 0, 4, 32, 0)])
        pe.wait_ge(*T.at("t5_rows"))
        pe.wait_ge(*T.at("rstd", "mix"))
        for i in range(8):
            if i >= 2:
                pe.wait_ge(*T.at("bias", i - 2))
            pe.matmul(SC[i % 2][:, :], C("flip"), t5_rows[:, i, :], start=True, stop=True).then_inc(*T.up("flip", i))

        def heads(a, hh):
            return a[hh % 2 * HD:hh % 2 * HD + HD, hh // 2, :]

        def diagonal(o, i, mask):
            return pe.matmul(o[:, i * P:i * P + P], ident, C(mask), start=False, stop=True)

        def qk(o, q, kk, i):
            pe.matmul(o[:, 0:(i + 1) * P], q[:, i * P:i * P + P], kk[:, 0:(i + 1) * P], start=True, stop=False)

        def score_sb(o, hh, i):
            qk(o, heads(sbq, hh), heads(sbk, hh), i)
            return diagonal(o, i, "strict")

        def score_mb(o, hh, i):
            qk(o, heads(mbq, hh), heads(mbk, hh), i)
            return diagonal(o, i, "causal")

        def score_fx(o, hh, i):
            qk(o, heads(fxq, hh), heads(fxk, hh), i)
            pick = C("pick", slice(0, NH)).rearrange("p (g h q) -> p g h q", g=2, h=NH)
            for j in range(i + 1):
                pe.matmul(o[:, j * P:j * P + P], cum[0:NH, i * P:i * P + P], pick[:, 0, hh, :], start=False, stop=False)
            pe.matmul(o[:, 0:(i + 1) * P], pick[:, 1, hh, :], cum[0:NH, 0:(i + 1) * P], start=False, stop=False)
            return diagonal(o, i, "causal")

        def score_ds(o, hh, i):
            r = slice(hh % 2 * HD, hh % 2 * HD + HD)
            pe.matmul(o[:, 0:(i + 1) * P], dsq[r, hh // 2, i * P:i * P + P], dsk[r, 0:(i + 1) * P], start=True, stop=False)
            if i == 0:
                return diagonal(o, i, "causal")
            return pe.matmul(o[:, 0:(i + 1) * P], ident, sel[:, i - 1, 0:(i + 1) * P], start=False, stop=True)

        pe.wait_ge(*T.at("bias", 7))
        pe.wait_ge(*T.at("evac", "ixkf"))
        pe.wait_ge(*T.at("t5_kept"))
        attention("sb", score_sb, lambda hh, j: sbv[:, j, hh * HD:hh * HD + HD], 1)
        pe.wait_ge(*T.at("o", "sb", 1))
        attention("mb", score_mb, lambda hh, j: mbv[:, j, hh * HD:hh * HD + HD], 1)
        pe.wait_ge(*T.at("o", "mb", 1))
        pe.wait_ge(*T.at("cum"))
        attention("fx", score_fx, lambda hh, j: fxv[:, j, hh * HD:hh * HD + HD], 1)
        pe.wait_ge(*T.at("o", "fx", 1))
        n = 0
        for i in range(1, TT):
            for hh in range(8):
                if n >= 2:
                    pe.wait_ge(*T.at("ix_used", n - 2))
                r = slice(hh % 4 * 32, hh % 4 * 32 + 32)
                pe.matmul(SC[n % 2][:, 0:(i + 1) * P], ixq[r, hh // 4, i * P:i * P + P], ixk[r, 0:(i + 1) * P],
                          start=True, stop=True).then_inc(*T.up("ix_score", n))
                n += 1
        pe.wait_ge(*T.at("sel", TT - 2))
        attention("ds", score_ds, lambda hh, j: dsv[:, j, 0:HD], 1)
        pe.wait_ge(*T.at("o", "ds", 1))

        def gate_slab(key, rhs2):
            s = slab_start(key)
            w = ring[:, s, 0:(DC + 2) * P].rearrange("p (k c) -> p k c", k=DC + 2)
            for i in range(DC):
                pe.matmul(bank[2 * s][:, :], w[:, i, :], xk[i], start=(i == 0), stop=(i == DC - 1))
            for i in range(2):
                ins = pe.matmul(bank[2 * s + 1][:, :], w[:, DC + i, :], rhs2[i], start=(i == 0), stop=(i == 1))
            ins.then_inc(*T.up("gemm", *key))

        with loop("gates", DC, [("gate", 2), ("gate", 3)]):
            for b in range(4):
                gate_slab(("gate", b), [branch_out[b][:, 0, :], branch_out[b][:, 1, :]])

        def proj(tag, rhs, ready):
            pe.wait_ge(*T.at(*ready))
            hold()
            with loop(tag, 2, [(tag, 0), (tag, 1)]):
                for j in range(2):
                    gemm_fm((tag, j), rhs, pair)

        def ffn(tag, normed):
            pe.wait_ge(*T.at("xn", normed, DC - 1))
            hold()
            with loop(tag + "u", FC // 2, [(tag + "u", 0), (tag + "u", 1)]):
                for j in range(2):
                    gemm_fm((tag + "u", j), xk, pair)
            pe.wait_ge(*T.at(*(("hidden", "c", 1) if tag == "c" else ("evac", tag + "u", 1))))
            hold()
            with loop(tag + "d", 2, [(tag + "d", 0), (tag + "d", 1)]):
                for j in range(2):
                    gemm_fm((tag + "d", j), [hidden[:, i, :] for i in range(FC)], pair)

        proj("out", [mixed[:, i, :] for i in range(DC)], ("evac", "gate", 3))
        norm("ffn", xk, 0)
        ffn("c", "ffn")
        norm("fin1", xk, 0)

        with loop("layer", LAYERS, [("ple", 0), ("ple", 1)]):
            norm("f1", xk, 0)
            ffn("f", "f1")
            norm("lm", xk, 0)
            pe.wait_ge(*T.at("xn", "lm", DC - 1))
            hold()
            gemm_fm(("cq",), xk, pair)
            gemm_fm(("ckv",), xk, [(0, 0, P, 0, 0), (1, 64, 96, P, 0)])
            for name, n in (("hf", 2), ("hq", 2), ("hi", 1), ("hg", 1), ("zu", 1), ("zv", 1),
                            ("rq", 1), ("rk", 1), ("rv", 1), ("rg", 1)):
                for j in range(n):
                    if name in ("hi", "zv", "rv"):
                        gemm_tm((name, j), xk)
                    else:
                        gemm_fm((name, j), xk, pair)
            norm("q", [lprob[:, i, :] for i in range(2)], 1)
            pe.wait_ge(*T.at("rstd", "q"))
            norm("kv", [lprobT[:, 0, :]], 2)
            pe.wait_ge(*T.at("xn", "q", 1))
            for j in range(2):
                gemm_fm(("uq", j), [cq[:, i, :] for i in range(2)],
                        [(0, 0, MLA_D, 0, 0), (1, 0, MLA_D, MLA_D, 0)], width=192)
            pe.wait_ge(*T.at("xn", "kv", 0))
            gemm_fm(("uk",), [ckv], pair)
            gemm_tm(("uv",), [ckv])
            swap32 = C("swap32", slice(64, 96))
            for n in range(NH + 1):
                src = qh[64:96, n, :] if n < NH else kh[64:96, 0, :]
                if n == 0:
                    pe.wait_ge(*T.at("rstd", "kv"))
                    pe.wait_ge(*T.at("evac", "uq", 1))
                if n >= 2:
                    pe.wait_ge(*T.at("rot_used", n - 2))
                pe.matmul(SC[n % 2][:, :], swap32, src, start=True, stop=True).then_inc(*T.up("swapped", n))
            pe.wait_ge(*T.at("sg"))
            for i in range(NH):
                ins = pe.transpose(PT[:, i * P:i * P + P], sgw[:, i, :], ident)
            ins.then_inc(*T.up("sgw_turned"))
            hs = C("headsel", slice(0, NH)).rearrange("p (c q) -> p c q", c=2)
            for c in range(2):
                ins = pe.matmul(OB[:, c * P:c * P + P], hs[:, c, :], sgb[0:NH, :], start=True, stop=True)
            ins.then_inc(*T.up("sgb_spread"))
            pe.wait_ge(*T.at("sgwT"))
            pe.wait_ge(*T.at("sgbb"))
            for c in range(2):
                dst = PT if c == 0 else OB
                for hh in (2 * c, 2 * c + 1):
                    r = hh % 2 * HD
                    for i in range(TT):
                        ins = pe.matmul(dst[r:r + HD, i * P:i * P + P], zv[:, i, hh * HD:hh * HD + HD],
                                        sgwT[:, hh, :], start=True, stop=True)
                ins.then_inc(*T.up("sg_mixed", c))
            pe.wait_ge(*T.at("sg_out", 1))

            def score_mla(o, hh, i):
                qk(o, qh[0:MLA_D, hh, :], kh[0:MLA_D, hh, :], i)
                return diagonal(o, i, "causal")

            pe.wait_ge(*T.at("evac", "uv"))
            attention("ml", score_mla, lambda hh, j: mv[:, j, hh * HD:hh * HD + HD], 2)
            pe.wait_ge(*T.at("o", "ml", 1))
            for n in range(4):
                src = (rq, rk)[n // 2][:, n % 2, :]
                if n >= 2:
                    pe.wait_ge(*T.at("ret_rot", n - 2))
                pe.matmul(SC[n % 2][:, :], C("swap"), src, start=True, stop=True).then_inc(*T.up("ret_swap", n))
            pe.wait_ge(*T.at("ret_rot", 3))

            def ret_scores(u):
                hh, j = u // TT, u % TT
                if u >= 2:
                    pe.wait_ge(*T.at("ret_w", u - 2))
                pe.matmul(SC[u % 2][:, 0:S - j * P], heads(rk, hh)[:, j * P:j * P + P], heads(rq, hh)[:, j * P:S],
                          start=True, stop=True).then_inc(*T.up("ret_score", u))

            ret_scores(0)
            for u in range(NH * TT):
                hh, j = u // TT, u % TT
                if u + 1 < NH * TT:
                    ret_scores(u + 1)
                pe.wait_ge(*T.at("ret_w", u))
                if u == 2 * TT:
                    pe.wait_ge(*T.at("gin", "r", 0))
                r = hh % 2 * HD
                pe.matmul(OB[r:r + HD, j * P:S], rv[:, j, hh * HD:hh * HD + HD], lprob[:, u % 2, 0:S - j * P],
                          start=(j == 0), stop=(j == TT - 1)).then_inc(*T.up("ret_pv", u))
                if u in (2 * TT - 1, 4 * TT - 1):
                    c = u // (2 * TT)
                    group_norm("r", c, True)
            n = 0
            for hh in range(NH):
                r = hh % 2 * HD
                for lv in range(len(LEVELS) + 1):
                    if lv < len(LEVELS):
                        pe.wait_ge(*T.at("lvl_k", hh, lv))
                        kk, qq = hK[:, lv % 2, :], hQ[:, lv % 2, :]
                    else:
                        pe.wait_ge(*T.at("lvl_used", n - 2))
                        kk, qq = hk[:, hh, :], hq[:, hh, :]
                    for i in range(TT):
                        ins = pe.matmul(SC[n % 2][:, i * P:i * P + P], kk[:, i * P:i * P + P], qq[:, i * P:i * P + P],
                                        start=True, stop=True)
                    ins.then_inc(*T.up("lvl", n))
                    n += 1
                pe.wait_ge(*T.at("kv3", hh))
                kvs = kv3.rearrange("p (c t) -> p c t", c=3)
                blocks = [(1, kd[:, 0:P]), (2, kd[:, P:2 * P]), (3, kd[:, 2 * P:3 * P]), (2, kvs[:, 0, :]),
                          (3, kvs[:, 1, :]), (3, kvs[:, 2, :])]
                for b, (i, kk) in enumerate(blocks):
                    if b == 4:
                        pe.wait_ge(*T.at("offs", hh, 0))
                    ins = pe.matmul(PT[:, b % 4 * P:b % 4 * P + P], kk, qd[:, i * P:i * P + P], start=True, stop=True)
                    if b in (3, 5):
                        ins.then_inc(*T.up("off", hh, b // 4))
                where = {(1, 0): 0, (2, 1): 1, (3, 2): 2, (2, 0): 3, (3, 1): 4, (3, 0): 5}
                pe.wait_ge(*T.at("offs", hh, 1))
                pe.wait_ge(*T.at("lvl_used", n - 1))
                for i in range(TT):
                    for j in range(i + 1):
                        w = scT[:, i * P:i * P + P] if i == j else off[:, where[i, j] * P:where[i, j] * P + P]
                        ins = pe.matmul(OB[r:r + HD, i * P:i * P + P], hi[:, j, hh * HD:hh * HD + HD], w,
                                        start=(j == 0), stop=(j == i))
                ins.then_inc(*T.up("hg_pv", hh))
                if hh % 2 == 1:
                    group_norm("h", hh // 2, False)
            pe.wait_ge(*T.at("gout", "h", 1))
            parts = [cq, zu, hgate, rgate]
            proj("lout", [a[:, c, :] for a in parts for c in range(2)], ("gout", "h", 1))
            norm("f2", xk, 0)
            ffn("g", "f2")
            norm("pl", xk, 0)
            pe.wait_ge(*T.at("rstd", "pl"))
            pe.wait_ge(*T.at("pin"))
            for c in range(2):
                for i in range(TT):
                    ins = pe.transpose(SC[c][:, i * P:i * P + P], pin[:, i, c * P:c * P + P], ident)
                ins.then_inc(*T.up("p_turned", c))
            pe.wait_ge(*T.at("pT"))
            hold()
            pe.wait_ge(*T.at("xn", "pl", DC - 1))
            hold()
            with loop("ple", DC // 2, [("ple", 0), ("ple", 1)]):
                for j in range(2):
                    gate_slab(("ple", j), [pT[:, 0, :], pT[:, 1, :]])

        norm("fin", xk, 0)
        pe.wait_ge(*T.at("rstd", "fin"))
        for c in range(DC):
            pe.wait_ge(*T.at("xn", "fin", c))
            if c >= 2:
                pe.wait_ge(*T.at("out_row", c - 2))
            for i in range(TT):
                ins = pe.transpose(SC[c % 2][:, i * P:i * P + P], xn[:, c, i * P:i * P + P], ident)
            ins.then_inc(*T.up("out_turned", c))

    @block.scalar
    def _(act):
        def copy_pair(key, dst, scale=1.0, f=ACT.Copy):
            s = evac_start(key)
            for b in range(2):
                ins = act.activation(dst[b], bank[2 * s + b][:, :], f, scale=scale)
                ins.then_inc(*A.up(*(("evac", *key) if b == 1 else ())))

        turn = [0]

        def evac_start(key):
            s = turn[0] % 2
            turn[0] += 1
            act.wait_ge(*A.at("gemm", *key))
            return s

        def norm(tag, src, dst, ready=None):
            for i, a in enumerate(src):
                if ready:
                    act.wait_ge(*A.at(*ready, i))
                act.activation(dst[i], a, ACT.Square).then_inc(*A.up("sq", tag, i))
            root("msx", tag)

        def root(*what):
            act.wait_ge(*A.at(*what))
            act.activation(nrm[:, 1, :], nrm[:, 0, :], ACT.Sqrt).then_inc(*A.up("rt", *what[1:]))

        hk8 = [h[:, i, :] for i in range(DC)]
        xk = [xn[:, i, :] for i in range(DC)]

        def two(a):
            return [a[:, 0, :], a[:, 1, :]]

        def two_tm(a):
            return [a[:, 2 * b:2 * b + 2, :].rearrange("p i d -> p (i d)") for b in range(2)]

        def attention(tag, odst, mode, biased):
            pr, pt = (prob, probT) if mode == 1 else (lprob, lprobT)

            def expo(u):
                n = (u % TT + 1) * P
                act.wait_ge(*A.at("negmax", tag, u))
                src = pr[:, u % 2, 0:n] if biased else SC[u % 2][:, 0:n]
                if not biased and u >= 2:
                    act.wait_ge(*A.at("turned", tag, u - 2))
                act.activation(pr[:, u % 2, 0:n], src, ACT.Exp, bias=stat[:, u % 2, 1:2],
                               accum_out=stat[:, u % 2, 2:3])\
                    .then_inc(*A.up(*(("expo", tag, u) if biased else ("score_used", tag, u))))

            def copy_turned(u):
                n = (u % TT + 1) * P
                act.wait_ge(*A.at("turned", tag, u))
                act.activation(pt[:, u % 2, 0:n], PT[:, 0:n], ACT.Copy).then_inc(*A.up("probT", tag, u))

            expo(0)
            for u in range(NH * TT):
                if u + 1 < NH * TT:
                    expo(u + 1)
                copy_turned(u)
                if u % (2 * TT) == 2 * TT - 1:
                    c = u // (2 * TT)
                    act.wait_ge(*A.at("pv", tag, u))
                    act.activation(odst[:, c, :], OB[:, :], ACT.Copy).then_inc(*A.up("o", tag, c))

        def stick_breaking():
            def soft3(u):
                n = (u % TT + 1) * P
                a = soft[:, u % 2, 0:n]
                act.wait_ge(*A.at("score", "sb", u))
                if u >= 2:
                    act.wait_ge(*A.at("score_used", "sb", u - 2))
                act.activation(a, SC[u % 2][:, 0:n], ACT.Abs).then_inc(*A.up())
                act.wait_ge(*A.last())
                act.activation(a, a, ACT.Exp, scale=-1.0).then_inc(*A.up())
                act.wait_ge(*A.last())
                act.activation(a, a, ACT.Ln, bias=1.0).then_inc(*A.up("soft", u))

            soft3(0)
            for u in range(NH * TT):
                n = (u % TT + 1) * P
                if u + 1 < NH * TT:
                    soft3(u + 1)
                act.wait_ge(*A.at("score_used", "sb", u))
                act.activation(prob[:, u % 2, 0:n], prob[:, u % 2, 0:n], ACT.Exp).then_inc(*A.up("prob", "sb", u))
                act.wait_ge(*A.at("turned", "sb", u))
                act.activation(probT[:, u % 2, 0:n], PT[:, 0:n], ACT.Copy).then_inc(*A.up("probT", "sb", u))
                if u % (2 * TT) == 2 * TT - 1:
                    c = u // (2 * TT)
                    act.wait_ge(*A.at("pv", "sb", u))
                    act.activation(sbo[:, c, :], OB[:, :], ACT.Copy).then_inc(*A.up("o", "sb", c))

        for c in range(DC):
            act.wait_ge(*A.at("x_turned", c))
            act.activation(h[:, c, :], SC[c % 2][:, :], ACT.Copy).then_inc(*A.up("x_in", c))
        act.wait_ge(*A.at("cols_turned"))
        n = LAYERS * L_NROWS
        act.activation(pcol[:, 0:A_NROWS], PT[:, 0:A_NROWS], ACT.Copy).then_inc(*A.up())
        act.activation(convw.rearrange("p j c -> p (j c)"), PT[:, 128:128 + 6 * FC], ACT.Copy).then_inc(*A.up())
        act.activation(lcol[:, :], PT[:, 264:264 + n], ACT.Copy).then_inc(*A.up("cols_in"))
        act.wait_ge(*A.at("lb_in"))
        act.activation(nrm[:, 2, 0:8], nrm[:, 2, 0:8], ACT.Exp).then_inc(*A.up("lb_exp"))
        norm("mix", hk8, xk, ("x_in",))
        act.wait_ge(*A.at("t5a"))
        act.activation(t5_rev[0:8, 0:512], OB[0:8, :], ACT.Copy).then_inc(*A.up())
        act.wait_ge(*A.at("t5b"))
        act.activation(t5_rev[0:8, 512:640], PT[0:8, 0:128], ACT.Copy).then_inc(*A.up("t5_kept"))
        act.wait_ge(*A.last())
        act.dma_start(scratch, t5_rev[0:8, :]).then_inc(*spills.up("t5_out"))
        act.wait_ge(*A.at("t5_out"))
        toeplitz = bass.AP(tensor=scratch.tensor, offset=0, ap=[[1, P], [640, 8], [1, 512]])
        act.dma_start(t5_rows, toeplitz).then_inc(*spills.up("t5_rows"))
        q8 = HD ** -0.5
        for name, dst, kind in (("sbq", sbq, "q"), ("sbk", sbk, "k"), ("sbv", sbv, "v"), ("mbq", mbq, "q"),
                                ("mbk", mbk, "k"), ("mbv", mbv, "v"), ("fxq", fxq, "q"), ("fxk", fxk, "k"),
                                ("fxv", fxv, "v"), ("dsq", dsq, "q")):
            copy_pair((name,), two_tm(dst) if kind == "v" else two(dst), q8 if kind == "q" else 1.0)
        copy_pair(("ix",), two(ixq))
        s = evac_start(("dskv",))
        act.activation(dsk, bank[2 * s][:, :], ACT.Copy).then_inc(*A.up())
        act.activation(dsv.rearrange("p i d -> p (i d)"), bank[2 * s + 1][:, 0:TT * 72], ACT.Copy)\
            .then_inc(*A.up("evac", "dskv"))
        s = evac_start(("ixkf",))
        act.activation(ixk, bank[2 * s][:, :], ACT.Copy).then_inc(*A.up())
        act.activation(zlog[0:NH, :], bank[2 * s + 1][0:NH, :], ACT.Copy).then_inc(*A.up("evac", "ixkf"))
        for i in range(8):
            act.wait_ge(*A.at("flip", i))
            act.activation(bias[:, i, :], SC[i % 2][:, :], ACT.Copy).then_inc(*A.up("bias", i))
        act.wait_ge(*A.at("zlog"))
        a = soft[0:NH, 0, :]
        act.activation(a, zlog[0:NH, :], ACT.Abs).then_inc(*A.up())
        act.wait_ge(*A.last())
        act.activation(a, a, ACT.Exp, scale=-1.0).then_inc(*A.up())
        act.wait_ge(*A.last())
        act.activation(a, a, ACT.Ln, bias=1.0).then_inc(*A.up("zsoft"))
        act.wait_ge(*A.at("cum"))
        stick_breaking()
        attention("mb", sbq, 1, True)
        attention("fx", sbk, 1, False)
        n = 0
        for i in range(1, TT):
            for hh in range(8):
                act.wait_ge(*A.at("ix_score", n))
                if n >= 2:
                    act.wait_ge(*A.at("ix_added", n - 2))
                act.activation(soft[:, n % 2, 0:(i + 1) * P], SC[n % 2][:, 0:(i + 1) * P], ACT.Relu)\
                    .then_inc(*A.up("ix_used", n))
                n += 1
        attention("ds", mbq, 1, True)

        with Fori(A, act, "gates", DC):
            for b in range(4):
                s = evac_start(("gate", b))
                if b >= 2:
                    act.wait_ge(*A.at("evac", "gate", b - 2))
                act.activation(gates[:, b % 2, :], bank[2 * s][:, :], ACT.Sigmoid).then_inc(*A.up("gate_on", b))

        def silu_loop(tag, dst):
            with Fori(A, act, tag + "u", FC // 2):
                for j in range(2):
                    s = evac_start((tag + "u", j))
                    act.activation(dst[:, j, :], bank[2 * s][:, :], ACT.Silu).then_inc(*A.up("silu", tag, j))

        def sincos():
            for n in range(4):
                act.wait_ge(*A.at("angle", n))
                act.activation(rope[:, n, :], rtmp[:, n, :], ACT.Sin).then_inc(*A.up("sin", n))

        turn[0] += 2 * 2
        act.wait_ge(*A.at("evac", "out", 1))
        norm("ffn", hk8, xk)
        sincos()
        act.wait_ge(*A.at("pad_zero"))
        with Fori(A, act, "cu", FC // 2):
            for j in range(2):
                s = evac_start(("cu", j))
                act.wait_ge(*A.at("hidden", "c", j, prev="cu"))
                act.activation(padded[:, 2 * j, 2:514], bank[2 * s][:, :], ACT.Copy).then_inc(*A.up())
                act.activation(padded[:, 2 * j + 1, 2:514], bank[2 * s + 1][:, :], ACT.Copy)\
                    .then_inc(*A.up("evac", "cu", j))
                act.wait_ge(*A.at("conv_g", j))
                act.activation(silu[:, j, :], conv[:, 2 * j, :], ACT.Gelu).then_inc(*A.up("gelu", j))
        turn[0] += 4
        act.wait_ge(*A.at("evac", "cd", 1))
        norm("fin1", hk8, xk)

        with Fori(A, act, "layer", LAYERS):
            act.wait_ge(*A.at("xn", "fin1", DC - 1))
            act.wait_ge(*A.at("evac", "ple", 1, prev="layer"))
            norm("f1", hk8, xk)
            silu_loop("f", silu)
            turn[0] += 4
            act.wait_ge(*A.at("evac", "fd", 1))
            norm("lm", hk8, xk)
            copy_pair(("cq",), two(cq))
            s = evac_start(("ckv",))
            act.activation(ckv, bank[2 * s][:, :], ACT.Copy).then_inc(*A.up())
            act.activation(kh[64:96, 0, :], bank[2 * s + 1][64:96, :], ACT.Copy).then_inc(*A.up("evac", "ckv"))
            for j in range(2):
                copy_pair(("hf", j), [hS[:, 2 * j, :], hS[:, 2 * j + 1, :]], f=ACT.Sigmoid)
            for j in range(2):
                copy_pair(("hq", j), [hq[:, 2 * j, :], hq[:, 2 * j + 1, :]])
            copy_pair(("hi", 0), two_tm(hi))
            copy_pair(("hg", 0), two(hgate), f=ACT.Silu)
            copy_pair(("zu", 0), two(zu), f=ACT.Gelu)
            copy_pair(("zv", 0), two_tm(zv), f=ACT.Gelu)
            copy_pair(("rq", 0), two(rq))
            copy_pair(("rk", 0), two(rk), q8)
            copy_pair(("rv", 0), two_tm(rv))
            copy_pair(("rg", 0), two(rgate), f=ACT.Silu)
            norm("q", two(cq), two(lprob))
            norm("kv", [ckv], [lprobT[:, 0, :]])
            for j in range(2):
                s = evac_start(("uq", j))
                for b in range(2):
                    ins = act.activation(qh[0:MLA_D, 2 * j + b, :], bank[2 * s + b][0:MLA_D, :], ACT.Copy,
                                         scale=MLA_D ** -0.5)
                    ins.then_inc(*A.up(*(("evac", "uq", j) if b else ())))
            s = evac_start(("uk",))
            for hh in range(NH):
                ins = act.activation(kh[0:HD, hh, :], bank[2 * s + hh // 2][hh % 2 * HD:hh % 2 * HD + HD, :], ACT.Copy)
                ins.then_inc(*A.up(*(("evac", "uk") if hh == 3 else ())))
            copy_pair(("uv",), two_tm(mv))
            act.wait_ge(*A.at("sgvar"))
            act.activation(sgst[:, :, 3], sgst[:, :, 2], ACT.Sqrt).then_inc(*A.up("sgroot"))
            act.wait_ge(*A.at("sgb_spread"))
            act.activation(sgbb.rearrange("p c t -> p (c t)"), OB[:, 0:2 * P], ACT.Copy).then_inc(*A.up("sgbb"))
            attention("ml", cq, 2, False)

            def group_in(tag, c, last_pv, centred):
                act.wait_ge(*A.at(*last_pv))
                act.activation(gn[:, 0, :], OB[:, :], ACT.Copy).then_inc(*A.up("gin", tag, c))
                act.wait_ge(*(A.at("gcentred", tag, c) if centred else A.last()))
                act.activation(gn[:, 1, :], gn[:, 0, :], ACT.Square).then_inc(*A.up("gsq", tag, c))
                root("gx", tag, c)

            for c in range(2):
                if c:
                    act.wait_ge(*A.at("gout", "r", c - 1))
                group_in("r", c, ("ret_pv", 2 * TT * (c + 1) - 1), True)
            for hh in range(NH):
                act.wait_ge(*A.at("forget", hh))
                act.activation(hS[:, hh, :], hS[:, hh, :], ACT.Ln).then_inc(*A.up("logf", hh))
            for hh in range(NH):
                act.wait_ge(*A.at("tail", hh))
                act.activation(hE[:, 0, :], hE[:, 0, :], ACT.Exp).then_inc(*A.up())
                act.activation(hE[:, 1, :], hS[:, hh, :], ACT.Exp).then_inc(*A.up())
                ends = hS[:, hh, :].rearrange("p (n m) -> p n m", n=TT)[:, :, P - 1]
                act.activation(dend, ends, ACT.Exp).then_inc(*A.up("head_exp", hh))
                for lv in range(len(LEVELS)):
                    act.wait_ge(*A.at("lvl_d", hh, lv))
                    act.activation(hE[:, lv % 2, :], hE[:, lv % 2, :], ACT.Exp).then_inc(*A.up("lvl_e", hh, lv))
                act.wait_ge(*A.at("off", hh, 0))
                act.activation(off[:, 0:512], PT[:, :], ACT.Copy).then_inc(*A.up("offs", hh, 0))
                act.wait_ge(*A.at("off", hh, 1))
                act.activation(off[:, 512:768], PT[:, 0:256], ACT.Copy).then_inc(*A.up("offs", hh, 1))
                if hh % 2:
                    if hh == 3:
                        act.wait_ge(*A.at("gout", "h", 0))
                    group_in("h", hh // 2, ("hg_pv", hh), False)
            turn[0] += 4
            act.wait_ge(*A.at("evac", "lout", 1))
            norm("f2", hk8, xk)
            silu_loop("g", silu)
            turn[0] += 4
            act.wait_ge(*A.at("evac", "gd", 1))
            norm("pl", hk8, xk)
            for c in range(2):
                act.wait_ge(*A.at("p_turned", c))
                act.activation(pT[:, c, :], SC[c][:, :], ACT.Copy).then_inc(*A.up(*(("pT",) if c else ())))
            with Fori(A, act, "ple", DC // 2):
                for j in range(2):
                    s = evac_start(("ple", j))
                    act.wait_ge(*A.at("evac", "ple", j, prev="ple"))
                    act.activation(sg8[:, j, :], bank[2 * s][:, :], ACT.Sigmoid).then_inc(*A.up("ple_on", j))

        act.wait_ge(*A.at("evac", "ple", 1))
        norm("fin", hk8, xk)
        for c in range(DC):
            act.wait_ge(*A.at("out_turned", c))
            dst = outrow[:, :, c * P:c * P + P]
            act.activation(dst, SC[c % 2][:, :].rearrange("p (i d) -> p i d", i=TT), ACT.Copy)\
                .then_inc(*A.up("out_row", c))
        act.wait_ge(*A.last())
        act.activation(stat[:, 0, 3:4], outrow[:, 0, 0:1], ACT.Copy).then_inc(*A.up("out_ready"))

    @block.vector
    def _(v):
        turn = [13]

        def evac_start(key):
            s = turn[0] % 2
            turn[0] += 1
            v.wait_ge(*V.at("gemm", *key))
            return s

        def last():
            v.wait_ge(*V.last())

        def tt(out, a, b, op, *what):
            v.tensor_tensor(out, a, b, op).then_inc(*V.up(*what))

        def ts(out, a, s1, s2, op0, op1, *what):
            if op1 is None:
                v.tensor_scalar(out, a, s1, None, op0).then_inc(*V.up(*what))
            else:
                v.tensor_scalar(out, a, s1, s2, op0, op1).then_inc(*V.up(*what))

        def stt(out, a, s, b, op0, op1, *what):
            v.scalar_tensor_tensor(out=out, in0=a, scalar=s, in1=b, op0=op0, op1=op1).then_inc(*V.up(*what))

        def newton(x, y, t, *what):
            v.reciprocal(y, y).then_inc(*V.up())
            last()
            tt(t, x, y, ALU.mult)
            last()
            tt(t, t, y, ALU.mult)
            last()
            ts(t, t, -0.5, 1.5, ALU.mult, ALU.add)
            last()
            tt(y, y, t, ALU.mult, *what)
            last()

        def rstd(psum, ms, x, tag):
            v.wait_ge(*V.at(*ms))
            last()
            ts(nrm[:, 0, :], psum, EPS, None, ALU.add, None, x, *tag)
            v.wait_ge(*V.at("rt", *tag))
            newton(nrm[:, 0, :], nrm[:, 1, :], nrm[:, 2, :], "rstd", *tag)

        def norm(tag, src, dst, g):
            rstd(SC[0][:, :], ("ms", tag), "msx", (tag,))
            for i, a in enumerate(src):
                stt(dst[i], a, g[:, i:i + 1], nrm[:, 1, :], ALU.mult, ALU.mult, "xn", tag, i)

        hk8 = [h[:, i, :] for i in range(DC)]
        xk = [xn[:, i, :] for i in range(DC)]

        def attention(tag, mode, table):
            pr = prob if mode == 1 else lprob

            def peak(u):
                hh, i = u // TT, u % TT
                n = (i + 1) * P
                v.wait_ge(*V.at("score", tag, u))
                last()
                if table is not None:
                    if u >= 2:
                        v.wait_ge(*V.at("turned", tag, u - 2))
                    v.tensor_tensor_reduce(pr[:, u % 2, 0:n], SC[u % 2][:, 0:n], bias[:, table + hh, S - n:S], 1.0, GONE,
                                           ALU.add, ALU.max, stat[:, u % 2, 0:1])\
                        .then_inc(*V.up("score_used", tag, u))
                else:
                    v.tensor_reduce(stat[:, u % 2, 0:1], SC[u % 2][:, 0:n], AX.X, ALU.max).then_inc(*V.up())
                last()
                ts(stat[:, u % 2, 1:2], stat[:, u % 2, 0:1], -1.0, None, ALU.mult, None, "negmax", tag, u)

            peak(0)
            for u in range(NH * TT):
                n = (u % TT + 1) * P
                if u + 1 < NH * TT:
                    peak(u + 1)
                v.wait_ge(*V.at(*(("expo", tag, u) if table is not None else ("score_used", tag, u))))
                v.reciprocal(stat[:, u % 2, 3:4], stat[:, u % 2, 2:3]).then_inc(*V.up())
                last()
                ts(pr[:, u % 2, 0:n], pr[:, u % 2, 0:n], stat[:, u % 2, 3:4], None, ALU.mult, None, "prob", tag, u)

        v.memset(ones[:, 0, :], 1.0 / D).then_inc(*V.up())
        v.memset(ones[:, 1, :], 1.0 / 256).then_inc(*V.up())
        v.memset(ones[:, 2, :], 1.0 / 128).then_inc(*V.up())
        v.wait_ge(*V.at("cols_in"))
        a0, a1 = (lcol[:, l * L_NROWS + 21:l * L_NROWS + 25] for l in range(LAYERS))
        e0, e1, m, r = (nrm[:, 2, 4 * i:4 * i + 4] for i in range(4))
        tt(m, a0, a1, ALU.max)
        last()
        tt(e0, a0, m, ALU.subtract)
        tt(e1, a1, m, ALU.subtract, "lb_in")
        v.wait_ge(*V.at("lb_exp"))
        tt(m, e0, e1, ALU.add)
        last()
        v.reciprocal(r, m).then_inc(*V.up())
        last()
        tt(e0, e0, r, ALU.mult)
        tt(e1, e1, r, ALU.mult)
        last()
        tt(m, e0, e1, ALU.add)
        v.memset(lbs[:, 0, 0, :], 0.0).then_inc(*V.up())
        v.memset(lbs[:, 0, 1, :], 1.0).then_inc(*V.up())
        last()
        tt(lbs[:, 1, 0, :], m, e0, ALU.subtract)
        last()
        ts(lbs[:, 1, 1, :], lbs[:, 1, 0, :], -1.0, 1.0, ALU.mult, ALU.add)

        norm("mix", hk8, xk, pcol[:, A_ROWS["mix"]:])
        v.wait_ge(*V.at("bias", 7))
        v.memset(one512, 1.0).then_inc(*V.up())
        z = zlog[0:NH, :]
        ts(z, z, cur[0:NH, 49:50], None, ALU.add, None, "zlog")
        v.wait_ge(*V.at("zsoft"))
        last()
        stt(z, z, 0.0, soft[0:NH, 0, :], ALU.min, ALU.subtract)
        last()
        v.tensor_tensor_scan(cum[0:NH, :], one512[0:NH, :], z, 0.0, ALU.mult, ALU.add).then_inc(*V.up("cum"))
        for u in range(NH * TT):
            n = (u % TT + 1) * P
            sp, pr, z = soft[:, u % 2, 0:n], prob[:, u % 2, 0:n], SC[u % 2][:, 0:n]
            v.wait_ge(*V.at("soft", u))
            last()
            stt(sp, z, 0.0, sp, ALU.max, ALU.add)
            last()
            if u >= 2:
                v.wait_ge(*V.at("turned", "sb", u - 2))
            v.tensor_tensor_scan(pr[:, ::-1], one512[:, 0:n], sp[:, ::-1], 0.0, ALU.mult, ALU.add).then_inc(*V.up())
            last()
            tt(pr, z, pr, ALU.subtract, "score_used", "sb", u)
        attention("mb", 1, 0)
        attention("fx", 1, None)
        n = 0
        for i in range(1, TT):
            w = (i + 1) * P
            acc = sel[:, i - 1, 0:w]
            for hh in range(8):
                r = soft[:, n % 2, 0:w]
                wcol = dsv[:, i, HD + hh:HD + hh + 1]
                v.wait_ge(*V.at("ix_used", n))
                last()
                if hh == 0:
                    ts(acc, r, wcol, None, ALU.mult, None, "ix_added", n)
                else:
                    stt(acc, r, wcol, acc, ALU.mult, ALU.add, "ix_added", n)
                n += 1
            last()
            tt(acc[:, i * P:w], acc[:, i * P:w], C("causal"), ALU.add)
            last()
            for r in range(TOPK // 8):
                v.max(top8, acc).then_inc(*V.up())
                last()
                v.match_replace(acc, top8, acc, GONE).then_inc(*V.up())
                last()
            ts(acc, acc, -2e38, NEG, ALU.is_gt, ALU.mult, "sel", i - 1)
        attention("ds", 1, 4)

        t, acc = soft[:, 1, :], soft[:, 0, :]
        with Fori(V, v, "gates", DC) as it:
            for b in range(4):
                s = evac_start(("gate", b))
                v.wait_ge(*V.at("gate_on", b))
                last()
                if b == 0:
                    tt(acc, gates[:, 0, :], bank[2 * s + 1][:, :], ALU.mult, "evac", "gate", b)
                    continue
                tt(t, gates[:, b % 2, :], bank[2 * s + 1][:, :], ALU.mult, *(("evac", "gate", b) if b < 3 else ()))
                last()
                if b < 3:
                    tt(acc, acc, t, ALU.add)
                else:
                    tt(mixed[:, bass.ds(it, 1), :], acc.rearrange("p (c t) -> p c t", c=1),
                       t.rearrange("p (c t) -> p c t", c=1), ALU.add, "evac", "gate", 3)

        def add_to_h(tag, scale):
            with Fori(V, v, tag, 2) as it:
                for j in range(2):
                    s = evac_start((tag, j))
                    for b in range(2):
                        hc = h[:, bass.ds(it * 4 + (2 * j + b), 1), :]
                        stt(hc, bank[2 * s + b][:, :].rearrange("p (c t) -> p c t", c=1), scale, hc, ALU.mult, ALU.add,
                            *(("evac", tag, j) if b else ()))

        def ffn_loop(tag):
            with Fori(V, v, tag + "u", FC // 2) as it:
                for j in range(2):
                    s = evac_start((tag + "u", j))
                    v.wait_ge(*V.at("silu", tag, j))
                    tt(hidden[:, bass.ds(it * 2 + j, 1), :], silu[:, j:j + 1, :],
                       bank[2 * s + 1][:, :].rearrange("p (c t) -> p c t", c=1), ALU.mult, "evac", tag + "u", j)
            add_to_h(tag + "d", 0.5)

        add_to_h("out", 1.0)
        norm("ffn", hk8, xk, pcol[:, A_ROWS["ffn"]:])
        v.memset(padded[:, :, 0:2], 0.0).then_inc(*V.up("pad_zero"))
        v.wait_ge(*V.at("evac", "gate", 3))
        v.wait_ge(*V.at("decay"))
        v.tensor_copy(nrm[:, 0, :], pos_i[:, :].bitcast(I32)).then_inc(*V.up())
        last()
        c1, c2 = 6.28125, 0.0019350051879882812
        c3 = TWO_PI - c1 - c2
        magic = 12582912.0
        for n, (col, turns) in enumerate(((0, 0.25), (0, 0.0), (2, 0.25), (2, 0.0))):
            a, q, r = nrm[:, 1, :], nrm[:, 2, :], rtmp[:, n, :]
            ts(a, nrm[:, 0, :], C("cols")[:, col:col + 1], None, ALU.mult, None)
            last()
            ts(q, a, 1.0 / TWO_PI, turns, ALU.mult, ALU.add)
            last()
            ts(q, q, magic, None, ALU.add, None)
            last()
            ts(q, q, -magic, None, ALU.add, None)
            last()
            stt(r, q, -c1, a, ALU.mult, ALU.add)
            last()
            stt(r, q, -c2, r, ALU.mult, ALU.add)
            last()
            stt(r, q, -c3, r, ALU.mult, ALU.add)
            last()
            if turns:
                ts(r, r, TWO_PI / 4, None, ALU.add, None)
                last()
            ts(r, r, 3.1415925, -3.1415925, ALU.min, ALU.max, "angle", n)
            last()
        for n, col in ((1, 1), (3, 3)):
            v.wait_ge(*V.at("sin", n))
            ts(rope[:, n, :], rope[:, n, :], C("cols")[:, col:col + 1], None, ALU.mult, None, "rope", n)
        with Fori(V, v, "cu", FC // 2) as it:
            for j in range(2):
                s = evac_start(("cu", j))
                v.wait_ge(*V.at("evac", "cu", j))
                for a in range(2):
                    ch = it * 2 + (j + a * FC)
                    src, dst = padded[:, 2 * j + a, :], conv[:, 2 * j + a, :]
                    last()
                    ts(dst, src[:, 0:S], convw[:, 0, bass.ds(ch, 1)],
                       pcol[:, bass.ds(ch + A_ROWS["conv_b"], 1)], ALU.mult, ALU.add)
                    for n in (1, 2):
                        last()
                        stt(dst, src[:, n:n + S], convw[:, n, bass.ds(ch, 1)], dst, ALU.mult, ALU.add,
                            *(("conv_g", j) if n == 2 and a == 0 else ()))
                v.wait_ge(*V.at("gelu", j))
                last()
                tt(hidden[:, bass.ds(it * 2 + j, 1), :], silu[:, j:j + 1, :], conv[:, 2 * j + 1:2 * j + 2, :], ALU.mult,
                   "hidden", "c", j)
        add_to_h("cd", 1.0)
        norm("fin1", hk8, hk8, pcol[:, A_ROWS["fin1"]:])

        with Fori(V, v, "layer", LAYERS) as l:
            last()
            v.tensor_copy(cur[:, 0:L_NROWS], lcol[:, bass.ds(l * L_NROWS, L_NROWS)]).then_inc(*V.up())
            v.tensor_copy(cur[:, L_NROWS:L_NROWS + 8].rearrange("p (o a h) -> p o a h", o=1, a=2),
                          lbs[:, bass.ds(l, 1), :, :]).then_inc(*V.up())

            def g(name):
                return cur[:, L_ROWS[name]:]

            norm("f1", hk8, xk, g("ffn1"))
            ffn_loop("f")
            norm("lm", hk8, xk, g("mix"))
            norm("q", [cq[:, i, :] for i in range(2)], [cq[:, i, :] for i in range(2)], g("q"))
            norm("kv", [ckv], [ckv], g("kv"))
            for n in range(NH + 1):
                x0 = qh[64:96, n, :] if n < NH else kh[64:96, 0, :]
                t0 = lprob[64:96, n % 2, :]
                v.wait_ge(*V.at("swapped", n))
                last()
                tt(t0, SC[n % 2][64:96, :], rope[64:96, 3, :], ALU.mult, "rot_used", n)
                tt(x0, x0, rope[64:96, 2, :], ALU.mult)
                last()
                tt(x0, x0, t0, ALU.add)
            last()
            for n in range(1, NH):
                v.tensor_copy(kh[64:96, n, :], kh[64:96, 0, :]).then_inc(*V.up(*(("k_rot",) if n == NH - 1 else ())))
            v.wait_ge(*V.at("evac", "zv", 0))
            for i in range(TT):
                zi, st = zv[:, i, :], sgst[:, i, :]
                v.tensor_reduce(st[:, 0:1], zi, AX.X, ALU.add).then_inc(*V.up())
                last()
                ts(st[:, 0:1], st[:, 0:1], -1.0 / 256, None, ALU.mult, None)
                last()
                ts(zi, zi, st[:, 0:1], None, ALU.add, None)
                last()
                v.tensor_tensor_reduce(nrm[:, 2, 0:256], zi, zi, 1.0 / 256, 0.0, ALU.mult, ALU.add, st[:, 1:2])\
                    .then_inc(*V.up())
                last()
            ts(sgst[:, :, 2], sgst[:, :, 1], EPS, None, ALU.add, None, "sgvar")
            v.wait_ge(*V.at("sgroot"))
            newton(sgst[:, :, 2], sgst[:, :, 3], sgst[:, :, 4])
            for i in range(TT):
                ts(zv[:, i, :], zv[:, i, :], sgst[:, i, 3:4], None, ALU.mult, None, *(("zv_normed",) if i == TT - 1 else ()))
            v.wait_ge(*V.at("sgw_turned"))
            tt(sgwT, PT[:, :].rearrange("p (h t) -> p h t", h=NH), C("tril")[:, None, :].to_broadcast([P, NH, P]),
               ALU.mult, "sgwT")
            for c in range(2):
                y = lprobT[:, 1, :]
                v.wait_ge(*V.at("sgbb"))
                v.wait_ge(*V.at("sg_mixed", c))
                last()
                stt(y.rearrange("p (i t) -> p i t", i=TT), (PT if c == 0 else OB)[:, :].rearrange("p (i t) -> p i t", i=TT),
                    g("sg")[:, c:c + 1], sgbb[:, c:c + 1, :].to_broadcast([P, TT, P]), ALU.mult, ALU.add)
                last()
                tt(zu[:, c, :], zu[:, c, :], y, ALU.mult, "sg_out", c)
            attention("ml", 2, None)

            for n in range(4):
                x0 = (rq, rk)[n // 2][:, n % 2, :]
                t0 = lprobT[:, n % 2, :]
                v.wait_ge(*V.at("ret_swap", n))
                last()
                tt(t0, SC[n % 2][:, :], rope[:, 1, :], ALU.mult)
                tt(x0, x0, rope[:, 0, :], ALU.mult)
                last()
                tt(x0, x0, t0, ALU.add, "ret_rot", n)

            def group_out(tag, c, gain, gate, centred):
                if centred:
                    v.wait_ge(*V.at("gmean", tag, c))
                    last()
                    tt(gn[:, 0, :], gn[:, 0, :], PT[:, :], ALU.subtract, "gcentred", tag, c)
                rstd(PT[:, :], ("gms", tag, c), "gx", (tag, c))
                stt(gn[:, 1, :], gn[:, 0, :], gain[:, c:c + 1], nrm[:, 1, :], ALU.mult, ALU.mult)
                last()
                tt(gate[:, c, :], gate[:, c, :], gn[:, 1, :], ALU.mult, "gout", tag, c)

            for u in range(NH * TT):
                hh, j = u // TT, u % TT
                n = S - j * P
                v.wait_ge(*V.at("ret_score", u))
                tt(lprob[:, u % 2, 0:n], SC[u % 2][:, 0:n], decay[:, hh, 0:n], ALU.mult, "ret_w", u)
                if u in (2 * TT, 4 * TT - 1):
                    group_out("r", u // (3 * TT), g("ret"), rgate, True)

            for hh in range(NH):
                f = hS[:, hh, :]
                last()
                ts(f, f, cur[:, L_NROWS + 4 + hh:L_NROWS + 5 + hh], cur[:, L_NROWS + hh:L_NROWS + 1 + hh], ALU.mult, ALU.add)
                last()
                ts(hk[:, hh, :], f, -1.0, 1.0, ALU.mult, ALU.add)
                ts(f, f, 2.0 ** -63, None, ALU.max, None, "forget", hh)
            for hh in range(NH):
                f, t0 = hS[:, hh, :], hQ[:, hh % 2, :]
                v.wait_ge(*V.at("logf", hh))
                last()
                v.tensor_copy(t0, f).then_inc(*V.up())
                last()
                v.tensor_tensor_scan(f, C("resets"), t0, 0.0, ALU.mult, ALU.add).then_inc(*V.up())
            last()
            v.memset(hQ, 0.0).then_inc(*V.up())
            v.memset(hK, 0.0).then_inc(*V.up())
            v.memset(scT, 0.0).then_inc(*V.up())
            n = 0
            for hh in range(NH):
                f = hS[:, hh, :]
                f4 = f.rearrange("p (n m) -> p n m", n=TT)

                def split(a, m):
                    a = a.rearrange("p (n two m) -> p n two m", two=2, m=m)
                    return a[:, :, 0, :], a[:, :, 1, :]

                def distances(lv):
                    m = LEVELS[lv]
                    early, late = split(f, m)
                    e_early, e_late = split(hE[:, lv % 2, :], m)
                    ref = early[:, :, m - 1:m].to_broadcast([P, S // (2 * m), m])
                    last()
                    tt(e_late, late, ref, ALU.subtract)
                    tt(e_early, ref, early, ALU.subtract, "lvl_d", hh, lv)

                def masked(x):
                    lx = x % (len(LEVELS) + 1)
                    v.wait_ge(*V.at("lvl", x))
                    last()
                    v.memset(stat[:, 0, 3:4], 0.0).then_inc(*V.up())
                    m = C("levels")[:, lx * P:lx * P + P][:, None, :].bitcast(I32).to_broadcast([P, TT, P])
                    v.copy_predicated(scT.rearrange("p (i t) -> p i t", i=TT), m,
                                      SC[x % 2][:, :].rearrange("p (i t) -> p i t", i=TT)).then_inc(*V.up("lvl_used", x))

                last()
                tt(hE[:, 0, :].rearrange("p (n m) -> p n m", n=TT), f4[:, :, P - 1:P].to_broadcast([P, TT, P]), f4,
                   ALU.subtract, "tail", hh)
                v.wait_ge(*V.at("head_exp", hh))
                if hh:
                    v.wait_ge(*V.at("off", hh - 1, 1))
                tt(qd, hq[:, hh, :], hE[:, 1, :], ALU.mult)
                tt(kd, hk[:, hh, :], hE[:, 0, :], ALU.mult)
                last()
                kvs = kv3.rearrange("p (c t) -> p c t", c=3)
                ts(kvs[:, 0, :], kd[:, 0:P], dend[:, 1:2], None, ALU.mult, None)
                ts(kvs[:, 1, :], kd[:, P:2 * P], dend[:, 2:3], None, ALU.mult, None)
                last()
                ts(kvs[:, 2, :], kvs[:, 0, :], dend[:, 2:3], None, ALU.mult, None, "kv3", hh)
                distances(0)
                for lv in range(len(LEVELS)):
                    if lv + 1 < len(LEVELS):
                        distances(lv + 1)
                    m = LEVELS[lv]
                    e_early, e_late = split(hE[:, lv % 2, :], m)
                    v.wait_ge(*V.at("lvl_e", hh, lv))
                    if n >= 2:
                        v.wait_ge(*V.at("lvl", n - 2))
                    last()
                    tt(split(hQ[:, lv % 2, :], m)[1], split(hq[:, hh, :], m)[1], e_late, ALU.mult)
                    tt(split(hK[:, lv % 2, :], m)[0], split(hk[:, hh, :], m)[0], e_early, ALU.mult, "lvl_k", hh, lv)
                    if lv:
                        masked(n - 1)
                    n += 1
                n += 1
                masked(n - 2)
                masked(n - 1)
                if hh % 2:
                    group_out("h", hh // 2, g("hg"), hgate, False)
            add_to_h("lout", 1.0)
            norm("f2", hk8, xk, g("ffn2"))
            ffn_loop("g")
            norm("pl", hk8, xk, g("ple"))
            with Fori(V, v, "ple", DC // 2) as it:
                for j in range(2):
                    s = evac_start(("ple", j))
                    v.wait_ge(*V.at("ple_on", j))
                    last()
                    tt(sg8[:, j, :], sg8[:, j, :], bank[2 * s + 1][:, :], ALU.mult)
                    last()
                    hc = h[:, bass.ds(it * 2 + j, 1), :]
                    tt(hc, hc, sg8[:, j:j + 1, :], ALU.add, "evac", "ple", j)
        norm("fin", hk8, xk, pcol[:, A_ROWS["fin2"]:])


_INS = ["x", "norm_mix_g", "norm_ffn_g", "norm_final_g", "w_in", "fox_b_f", "t5_bias", "w_gate", "w_branch", "w_out",
        "w_up", "conv_w", "conv_b", "w_down", "p_2", "positions_2", "ffn1_norm_2", "ffn1_w_gate_2", "ffn1_w_up_2",
        "ffn1_w_down_2", "mix_norm_2", "w_in_2", "mla_q_norm_2", "mla_w_uq_2", "mla_kv_norm_2", "mla_w_ukv_2",
        "sg_ln_2", "sg_w_s_2", "sg_b_s_2", "hg_lb_logits_2", "hg_norm_2", "ret_norm_2", "w_out_2", "ffn2_norm_2",
        "ffn2_w_gate_2", "ffn2_w_up_2", "ffn2_w_down_2", "ple_norm_2", "ple_w_proj_2", "ple_w_gate_2",
        "final_norm_2"]


def build(nc, arrays, known=None):
    k = {n: nc.dram_tensor(f"in_{n}", a.shape, mybir.dt.from_np(a.dtype), kind="ExternalInput").ap()
         for n, a in arrays.items()}
    out = nc.dram_tensor("out_0", (1, S, D), F32, kind="ExternalOutput").ap()
    scratch = nc.dram_tensor("t5_by_distance", (8, 640), F32).ap()
    book = Book(known)
    program(nc, k["x"][0], out[0], k, scratch, book)
    return book


def kernel(**inputs):
    import concourse.bacc as bacc
    from concourse.bass_utils import run_bass_kernel_spmd

    arrays = {n: np.ascontiguousarray(inputs[n]) for n in _INS}
    arrays["const"] = np.concatenate(list(constants().values()), 1)
    arrays["decay"] = decays()
    counted = build(bacc.Bacc("TRN2", target_bir_lowering=False, num_devices=1), arrays)
    nc = bacc.Bacc("TRN2", target_bir_lowering=False, num_devices=1)
    build(nc, arrays, counted)
    r = run_bass_kernel_spmd(nc, [{f"in_{n}": a for n, a in arrays.items()}], core_ids=[0])
    return r.results[0]["out_0"]
```

```python
from contextlib import ExitStack

import numpy as np

import concourse.bass as bass
from concourse import mybir

F32 = mybir.dt.float32
F32R = mybir.dt.float32r
U8 = mybir.dt.uint8
I32 = mybir.dt.int32
ACT = mybir.ActivationFunctionType
ALU = mybir.AluOpType
AX = mybir.AxisListType

P = 128
S = 512
TT = S // P
D = 1024
DC = D // P
FF = 2816
FC = FF // P
HD = 64
NH = 4
LAYERS = 2
EPS = 1e-6
NEG = -1e30
GONE = -3e38
TOPK = 128
PIECE = 1024
ARENA = 26560
MLA_D = 96
TWO_PI = 2.0 * float(np.pi)
LEVELS = [64, 32, 16, 8, 4, 2, 1]

A_COLS = dict(sbq=0, sbk=256, sbv=512, mbq=768, mbk=1024, mbv=1280, fxq=1536, fxk=1792, fxv=2048,
              fxf=2304, dsq=2308, dsk=2564, dsv=2628, ixq=2692, ixk=2948, ixw=2980)
B_COLS = dict(cq=0, ckv=256, zu=416, zv=672, hq=928, hf=1440, hi=1952, hg=2208,
              rq=2464, rk=2720, rv=2976, rg=3232)
A_ROWS = dict(mix=0, ffn=8, fin1=16, fin2=24, conv_b=32)
A_NROWS = 32 + 2 * FC
L_ROWS = dict(ffn1=0, mix=8, q=16, kv=18, sg=19, lb=21, hg=25, ret=27, ffn2=29, ple=37)
L_NROWS = 45


def t5_bucket(n):
    n = np.maximum(n, 0)
    large = 16 + (np.log(np.maximum(n, 1) / 16.0) / np.log(8.0) * 16).astype(np.int64)
    return np.where(n < 16, n, np.minimum(large, 31))


def constants():
    p = np.arange(P)
    c = {}
    c["ident"] = np.eye(P)
    c["causal"] = np.where(p[None, :] > p[:, None], NEG, 0.0)
    c["strict"] = np.where(p[None, :] >= p[:, None], NEG, 0.0)
    swap = np.zeros((P, P))
    swap[p, p // 64 * 64 + (p % 64 + 32) % 64] = 1.0
    c["swap"] = swap
    swap32 = np.zeros((P, P))
    swap32[64 + np.arange(32), 64 + (np.arange(32) + 16) % 32] = 1.0
    c["swap32"] = swap32
    c["group"] = np.where(p[:, None] // 64 == p[None, :] // 64, 1.0 / 64, 0.0)
    c["tril"] = (p[:, None] <= p[None, :]).astype(float)
    f32 = np.float32
    inv64 = (f32(10000.0) ** (-np.arange(0, 64, 2, dtype=f32) / f32(64))).astype(f32)
    inv32 = (f32(10000.0) ** (-np.arange(0, 32, 2, dtype=f32) / f32(32))).astype(f32)
    cols = np.zeros((P, 4))
    cols[:, 0] = inv64[p % 32]
    cols[:, 1] = np.where(p % 64 < 32, -1.0, 1.0)
    cols[:, 2] = inv32[p % 16]
    cols[:, 3] = np.where(p % 32 < 16, -1.0, 1.0)
    c["cols"] = cols
    headsel = np.zeros((P, 2, P))
    for h in range(NH):
        headsel[h, h // 2, (h % 2) * 64:(h % 2) * 64 + 64] = 1.0
    c["headsel"] = headsel.reshape(P, -1)
    return {k: np.asarray(v, np.float32) for k, v in c.items()}


def first_constants():
    p = np.arange(P)
    onehot = np.zeros((P, 640))
    onehot[t5_bucket(511 - np.arange(640)), np.arange(640)] = 1.0
    pick = np.zeros((P, 2, NH, P))
    for h in range(NH):
        pick[h, 0, h, :] = 1.0
        pick[h, 1, h, :] = -1.0
    c = dict(onehot=onehot, flip=np.eye(P)[::-1], pick=pick.reshape(P, -1))
    return {k: np.asarray(v, np.float32) for k, v in c.items()}


def level_masks():
    p = np.arange(P)
    lev = [(p[None, :] // m % 2 == 1) & (p[:, None] // m == p[None, :] // m - 1) for m in LEVELS]
    lev.append(p[:, None] == p[None, :])
    return np.concatenate(lev, 1).astype(np.float32)


def decays():
    p, u = np.arange(P)[:, None], np.arange(S)[None, :]
    f32 = np.float32
    lg = np.log1p(-np.power(f32(2.0), -(f32(5.0) + np.arange(NH, dtype=f32)))).astype(f32)
    d = [np.where(u >= p, np.exp(np.maximum(u - p, 0).astype(f32) * g), 0.0) for g in lg]
    return np.concatenate(d, 1).astype(f32)


CONST_AT = {}
_n = 0
for _name, _a in constants().items():
    CONST_AT[_name] = (_n, _a.shape[1])
    _n += _a.shape[1]
CONST_N = _n


UP = dict(first=(0, 0, 0), odd=(2, 1, 2), even=(2, 2, 0))
DOWN = dict(even=(2, 0, 0), odd=(2, 1, 2), last=(0, FC // 2 - 1, 0))
FFN_LOOPS = (FC // 2 - 1) // 2


class Book:

    def __init__(self, known=None):
        self.marks = {}
        self.body = {}
        self.trips = {}
        self.known = known
        self.pieces = 0


class Count:

    def __init__(self, book, sem, name, unit=1):
        self.book, self.sem, self.name, self.unit = book, sem, name, unit
        self.n = 0
        self.loops = []

    def enter(self, loop):
        self.loops.append((loop, self.n))

    def leave(self, trips):
        loop, start = self.loops.pop()
        self.book.body[loop, self.name] = self.n - start
        self.book.trips[loop] = trips
        self.n = start + (self.n - start) * trips

    def up(self, *what):
        self.n += self.unit
        if what:
            assert what not in self.book.marks, what
            self.book.marks[what] = (self.sem, self.name, self.n, tuple(x for x, _ in self.loops))
        return self.sem, self.unit


class Pieces(Count):

    def value(self, e, mul, add):
        known = self.book.known
        v = self.n * mul + add
        for loop, _ in self.loops:
            stride = known.body[loop, self.name] if known else 0
            assert stride % 2 == 0
            if stride:
                v = e.regs[loop] * (stride * mul) + v
        return v


class Engine(Count):

    def __init__(self, book, sem, name):
        super().__init__(book, sem, name)
        self.regs = {}
        self.others = []

    def begin(self, loop, reg):
        self.regs[loop] = reg
        for c in (self, *self.others):
            c.enter(loop)

    def end(self, loop, trips):
        for c in (self, *self.others):
            c.leave(trips)
        del self.regs[loop]

    def value(self, sem_name, n, loops, prev=None):
        known = self.book.known
        v, terms = n, []
        for loop in loops:
            stride = known.body[loop, sem_name] if known else 0
            if loop in self.regs:
                terms.append((self.regs[loop], stride))
                if loop == prev:
                    v -= stride
            elif known:
                v += stride * (known.trips[loop] - 1)
        for reg, stride in terms:
            if stride:
                v = reg * stride + v
        return v

    def at(self, *what, prev=None):
        known = self.book.known
        if known is None:
            return self.sem, 1
        _, name, n, loops = known.marks[what]
        return self.book.sems[name], self.value(name, n, loops, prev)

    def same(self, *what):
        assert what not in self.book.marks, what
        self.book.marks[what] = (self.sem, self.name, self.n, tuple(x for x, _ in self.loops))

    def last(self):
        return self.sem, self.value(self.name, self.n, [x for x, _ in self.loops])


class Fori:

    def __init__(self, e, eng, loop, trips):
        self.e, self.loop, self.trips = e, loop, trips
        self.inner = eng.Fori(0, trips)

    def __enter__(self):
        reg = self.inner.__enter__()
        self.e.begin(self.loop, reg)
        return reg

    def __exit__(self, *a):
        self.e.end(self.loop, self.trips)
        return self.inner.__exit__(*a)


def program(nc, x, out, k, scratch, book):
    ctx = ExitStack()

    def sb(name, shape, dt=F32):
        return ctx.enter_context(nc.sbuf_tensor(name, shape, dt))

    def sem(name):
        return ctx.enter_context(nc.semaphore(name))

    h = sb("h", [P, DC, S])
    xh, xl = sb("xh", [P, DC, S], F32R), sb("xl", [P, DC, S], F32R)
    op_hi, op_lo = sb("op_hi", [P, 4, S], F32R), sb("op_lo", [P, 4, S], F32R)
    raw = sb("raw", [P, 2, PIECE])
    wh, wl = sb("wh", [P, 2, PIECE], F32R), sb("wl", [P, 2, PIECE], F32R)
    const = sb("const", [P, CONST_N])
    levels = sb("levels", [P, 8 * P], U8)
    pcol = sb("pcol", [P, A_NROWS // 4 * 4])
    convw = sb("convw", [P, 3, 2 * FC])
    lcol = sb("lcol", [P, LAYERS * L_NROWS])
    lbs = sb("lbs", [P, LAYERS, 2, NH])
    cur = sb("cur", [P, L_NROWS + 8])
    ones = sb("ones", [P, 3, P])
    nrm = sb("nrm", [P, 3, S])
    stat = sb("stat", [P, 2, 4])
    zero = sb("zero", [P, 1])
    arena = sb("arena", [P, ARENA])

    def C(name, rows=slice(0, P)):
        a, n = CONST_AT[name]
        return const[rows, a:a + n]

    spot = [0]

    def area(n, at=None):
        if at is not None:
            spot[0] = at
        a = spot[0]
        spot[0] += n
        assert spot[0] <= ARENA, spot[0]
        return arena[:, a:a + n]

    def chunks(a, n=2):
        return a.rearrange("p (c t) -> p c t", c=n)

    normed = chunks(area(4096, 0), DC)
    xraw = area(4096, 8192).rearrange("p (i d) -> p i d", i=TT)
    rows_a = area(P)
    rows_c = area(3 * P).rearrange("p (j q) -> p j q", j=3)
    rows_l = area(P)
    t5_in = area(8)
    t5_rev = area(640)
    t5_rows = area(4096, 14200).rearrange("p (h u) -> p h u", h=8)
    sbo = chunks(area(1024, 0))
    sbq, sbk, mbq = chunks(area(1024)), chunks(area(1024)), chunks(area(1024))
    mixed = chunks(arena[:, spot[0]:spot[0] + 4096], DC)
    mbk, fxq, fxk, dsq = (chunks(area(1024)) for _ in range(4))
    sbv, mbv, fxv = (area(1024).rearrange("p (i d) -> p i d", i=TT) for _ in range(3))
    dsk = area(512)
    ixq = chunks(area(1024))
    ixk = area(512)
    dsv = area(TT * 72).rearrange("p (i d) -> p i d", i=TT)
    cum = area(512)
    prob = chunks(area(1024))
    probT = chunks(area(1024))
    soft = chunks(area(1024))
    sel = chunks(area(1536), 3)
    top8 = area(8)
    zlog = area(512)
    gates_at = spot[0]
    gates = chunks(area(2048), 4)
    bias = area(4096).rearrange("p (h u) -> p h u", h=8)
    levels_in = area(8 * P, gates_at + 2048)
    onehot, flip = area(640, gates_at), area(P)
    pick = area(1024, gates_at + 2048 + 4096)
    branch_out = [sbo, sbq, sbk, mbq]
    padded = chunks(area(4 * 514, 5000), 4)
    conv = chunks(area(4 * S), 4)
    silu = chunks(area(2 * S), 2)
    hid = chunks(area(2 * S), 2)
    top = ARENA - 2 * 4 * S
    decay = area(NH * S, top).rearrange("p (h u) -> p h u", h=NH)
    rope = area(4 * S).rearrange("p (h u) -> p h u", h=4)
    pos_i = area(S, 17000)
    rtmp = chunks(area(4 * S), 4)
    cq = chunks(area(1024, 0))
    ckv = area(512)
    zu, zv = chunks(area(1024)), area(1024).rearrange("p (i d) -> p i d", i=TT)
    hq, hS, hk = chunks(area(2048), 4), chunks(area(2048), 4), chunks(area(2048), 4)
    hi = area(1024).rearrange("p (i d) -> p i d", i=TT)
    hgate = chunks(area(1024))
    rgate = chunks(area(1024))
    ret_at = spot[0]
    rq, rk = chunks(area(1024)), chunks(area(1024))
    rv = area(1024).rearrange("p (i d) -> p i d", i=TT)
    mv = area(1024).rearrange("p (i d) -> p i d", i=TT)
    sgw = area(512).rearrange("p (h s) -> p h s", h=NH)
    sgwT = area(512).rearrange("p (h s) -> p h s", h=NH)
    sgb = area(P)
    sgbb = chunks(area(256))
    sgst = area(TT * 8).rearrange("p (i d) -> p i d", i=TT)
    scratch_at = spot[0]
    lprob, lprobT = chunks(area(1024)), chunks(area(1024))
    qh = chunks(area(2048), 4)
    gn = qh[:, 0:2, :]
    kh = hk
    mla_end = spot[0]
    hE, hQ, hK = chunks(area(1024, ret_at)), chunks(area(1024)), chunks(area(1024))
    scT, qd = area(512), area(512)
    off = area(768, scratch_at)
    kd = area(512)
    kv3 = area(384)
    dend = area(4)
    assert max(mla_end, spot[0]) <= top, (mla_end, spot[0], top)
    pin = area(1024, 12000).rearrange("p (i d) -> p i d", i=TT)
    sg8 = chunks(area(2048), 4)
    outrow = area(4096, 8192).rearrange("p (i d) -> p i d", i=TT)

    bank = [ctx.enter_context(nc.psum_tensor(f"bank{i}", [P, S], F32)) for i in range(8)]
    SC, PT, OB = bank[4:6], bank[6], bank[7]

    names = ["tensor_done", "vector_done", "scalar_done", "landed0", "landed1", "pieces_split", "pieces_used",
             "loads", "spills", "stores", "zero_ready"]
    book.sems = {n: sem(n) for n in names}
    landed = [book.sems["landed0"], book.sems["landed1"]]
    split = book.sems["pieces_split"]
    T = Engine(book, book.sems["tensor_done"], "tensor_done")
    V = Engine(book, book.sems["vector_done"], "vector_done")
    A = Engine(book, book.sems["scalar_done"], "scalar_done")
    Q = Engine(book, book.sems["stores"], "stores")
    used = Count(book, book.sems["pieces_used"], "pieces_used")
    used_at = Pieces(book, None, "piece_of_products")
    load_at = Pieces(book, None, "piece_of_loads")
    loads = Count(book, book.sems["loads"], "loads", 16)
    spills = Count(book, book.sems["spills"], "spills", 16)
    Q.unit = 16
    Q.others = [load_at, loads]
    T.others = [used, used_at]
    A.others = [spills]
    pair_of = {}

    block = ctx.enter_context(nc.Block())

    ident = C("ident")

    @block.sync
    def _(sp):
        def load(dst, src, *what):
            sp.dma_start(dst, src).then_inc(*loads.up(*what))

        def rowload(dst, src, n):
            load(dst[0:n, :], src.rearrange("(c q) -> c q", q=P))

        def piece(*parts):
            s = load_at.n % 2
            for dst, src in parts:
                if load_at.n >= 2:
                    sp.wait_ge(split, load_at.value(Q, 2, -2))
                sp.dma_start(dst(raw[:, s, :]), src).then_inc(landed[s], 16)
            assert len(parts) == 2
            load_at.up()

        def whole(w, c0):
            def half(a):
                def dst(slot):
                    return slot.rearrange("p (k c) -> p k c", k=DC)[:, a:a + DC // 2, :]
                return dst, w.rearrange("(k p) c -> p k c", p=P)[:, a:a + DC // 2, bass.ds(c0, P)]
            piece(half(0), half(DC // 2))

        def two_rows(w, k0, c0, n):
            def row(i):
                def dst(slot):
                    return slot[:, i * n:i * n + n].rearrange("p (k c) -> p k c", k=1)
                return dst, w.rearrange("(k p) c -> p k c", p=P)[:, bass.ds(k0 + i, 1), bass.ds(c0, n)]
            piece(row(0), row(1))

        def slab(w, c0):
            whole(w, c0)
            whole(w, c0 + P)

        def some(w, c0, n, at):
            def dst(slot):
                return slot.rearrange("p (k c) -> p k c", k=DC)[:, :, at:at + n]
            return dst, w.rearrange("(k p) c -> p k c", p=P)[:, :, bass.ds(c0, n)]

        load(xraw, x.rearrange("(i p) d -> p i d", p=P), "x")
        load(const[:, :], k["const"])
        load(levels_in, k["levels"])
        for name, dst in (("onehot", onehot), ("flip", flip), ("pick", pick)):
            load(dst, k[name])
        rowload(rows_a, k["norm_mix_g"][0], 8)
        rowload(rows_a[8:16], k["norm_ffn_g"][0], 8)
        rowload(rows_a[16:24], k["norm_final_g"], 8)
        rowload(rows_a[24:32], k["final_norm_2"], 8)
        rowload(rows_a[32:76], k["conv_b"][0], 2 * FC)
        for j in range(3):
            rowload(rows_c[:, j, :], k["conv_w"][0, j], 2 * FC)
        for l in range(LAYERS):
            for name, at, n in (("ffn1_norm_2", 0, 8), ("mix_norm_2", 8, 8), ("mla_q_norm_2", 16, 2),
                                ("mla_kv_norm_2", 18, 1), ("sg_ln_2", 19, 2), ("hg_lb_logits_2", 21, 4),
                                ("hg_norm_2", 25, 2), ("ret_norm_2", 27, 2), ("ffn2_norm_2", 29, 8),
                                ("ple_norm_2", 37, 8)):
                rowload(rows_l[l * L_NROWS + at:], k[name][l], n)
        load(t5_in[0:32, :], k["t5_bias"])
        load(cur[0:4, 49:50], k["fox_b_f"].rearrange("a h -> h a"), "params")

        w = k["w_in"][0]
        for name in ("sbq", "sbk", "sbv", "mbq", "mbk", "mbv", "fxq", "fxk", "fxv", "dsq", "ixq"):
            slab(w, A_COLS[name])
        whole(w, A_COLS["dsk"])
        piece(some(w, A_COLS["ixk"], 40, 0), some(w, A_COLS["fxf"], NH, HD))

        def gates(branches, it):
            for gw, bw in branches:
                slab(gw, it * 256)
                two_rows(bw, 0, it * 256, 256)

        for half in range(2):
            with Fori(Q, sp, f"gates{half}", DC // 2) as it:
                gates([(k["w_gate"][0][b], k["w_branch"][0][b]) for b in (2 * half, 2 * half + 1)], it)

        def proj(tag, w):
            for j in range(4):
                slab(w, j * 256)

        def ffn(tag, w_gate, w_up, w_down):
            def up(phase, it, j):
                m, n, _ = UP[phase]
                for w in (w_gate, w_up):
                    whole(w, it * (m * 256) + (n * 256 + j * P))

            def down(phase, it, half):
                m, n, _ = DOWN[phase]
                two_rows(w_down, it * (2 * m) + 2 * n, half * (D // 2), D // 2)

            for j in range(2):
                up("first", 0, j)
            with Fori(Q, sp, tag, FFN_LOOPS) as it:
                for phase, behind in (("odd", "even"), ("even", "odd")):
                    for j in range(2):
                        up(phase, it, j)
                        down(behind, it, j)
            for half in range(2):
                down("last", 0, half)

        proj("out", k["w_out"][0])
        up = k["w_up"][0]
        sp.wait_ge(*Q.at("evac", "branch", 3))
        load(pos_i[:, :].bitcast(I32), k["positions_2"].to_broadcast([P, S]), "pos")
        load(decay, k["decay"].rearrange("p (h u) -> p h u", h=NH), "decay")
        ffn("c", up[:, 0:FF], up[:, FF:2 * FF], k["w_down"][0])

        with Fori(Q, sp, "layer", LAYERS) as l:
            def at_layer(name):
                a = k[name + "_2"][bass.ds(l, 1)]
                while len(a.shape) > 2:
                    a = a.rearrange("a b c -> (a b) c") if len(a.shape) == 3 else a.rearrange("a b c d -> (a b) c d")
                return a

            ffn("f", at_layer("ffn1_w_gate"), at_layer("ffn1_w_up"), at_layer("ffn1_w_down"))
            w = at_layer("w_in")
            slab(w, B_COLS["cq"])
            whole(w, B_COLS["ckv"])
            whole(w, B_COLS["ckv"] + HD)
            sp.wait_ge(*Q.at("evac", "f", "dlast", 3))
            load(sgw, at_layer("sg_w_s").rearrange("(h t) s -> t h s", h=NH))
            load(sgb[0:NH, :], at_layer("sg_b_s"), "sg")
            for name, n in (("hf", 2), ("hq", 2), ("hi", 1), ("hg", 1), ("zu", 1), ("zv", 1),
                            ("rq", 1), ("rk", 1), ("rv", 1), ("rg", 1)):
                for j in range(n):
                    slab(w, B_COLS[name] + 256 * j)
            two_rows(at_layer("mla_w_uq"), 0, 0, NH * MLA_D)
            ukv = at_layer("mla_w_ukv").rearrange("p (h c) -> p h c", h=NH)

            def keys_or_values(i):
                return (lambda slot: slot[:, 256 * i:256 * i + 256].rearrange("p (h c) -> p h c", h=NH),
                        ukv[:, :, i * HD:i * HD + HD])
            piece(keys_or_values(0), keys_or_values(1))
            proj("lout", at_layer("w_out"))
            ffn("g", at_layer("ffn2_w_gate"), at_layer("ffn2_w_up"), at_layer("ffn2_w_down"))
            sp.wait_ge(*Q.at("evac", "g", "dlast", 3))
            load(pin, at_layer("p").rearrange("(i q) d -> q i d", q=P), "pin")
            pg, pp = at_layer("ple_w_gate"), at_layer("ple_w_proj")
            with Fori(Q, sp, "ple", DC // 4) as it:
                for j in range(2):
                    slab(pg, it * 512 + j * 256)
                    two_rows(pp, 0, it * 512 + j * 256, 256)
        book.pieces = load_at.n

        sp.wait_ge(*Q.at("out_ready"))
        sp.dma_start(out.rearrange("(i p) d -> p i d", p=P), outrow).then_inc(*Q.up("stored"))
        sp.wait_ge(*Q.last())

    @block.gpsimd
    def _(pool):
        pool.memset(zero[:, :], 0.0).then_inc(book.sems["zero_ready"], 1)
        pool.wait_ge(book.sems["zero_ready"], 1)
        zeros = zero[:, 0:1].to_broadcast([P, PIECE])

        def split_piece(s, load_count, use_count, split_count):
            pool.wait_ge(landed[s], load_count)
            if use_count is not None:
                pool.wait_ge(book.sems["pieces_used"], use_count)
            pool.tensor_tensor(wh[:, s, :], raw[:, s, :], zeros, ALU.add).then_inc(split, 1)
            pool.wait_ge(split, split_count)
            pool.tensor_tensor(wl[:, s, :], raw[:, s, :], wh[:, s, :].bitcast(F32), ALU.subtract).then_inc(split, 1)

        for s in range(2):
            split_piece(s, 32, None, 2 * s + 1)
        with pool.Fori(0, (book.known.pieces if book.known else 4) // 2 - 1) as it:
            for s in range(2):
                split_piece(s, it * 32 + 64, it * 2 + (1 + s), it * 4 + (5 + 2 * s))

    @block.tensor
    def _(pe):
        slabs = [[], [], [], []]
        turn = [0, 0]

        def slab_start(key, ready=False, high=0):
            s = 2 * high + turn[high] % 2
            turn[high] += 1
            if not ready:
                for older, prev in slabs[s]:
                    pe.wait_ge(*T.at("evac", *older, prev=prev))
            slabs[s] = [(key, None)]
            pair_of[key] = s
            return s

        def loop(name, trips, keys, high_keys=()):
            f = Fori(T, pe, name, trips)
            for i, key in enumerate(keys):
                slabs[(turn[0] + i) % 2] = [(key, name)]
            for i, key in enumerate(high_keys):
                slabs[2 + (turn[1] + i) % 2] = [(key, name)]
            return f

        def piece_split(part):
            pe.wait_ge(split, used_at.value(T, 2, part))

        def piece_used(ins, *what):
            ins.then_inc(*used.up(*what))
            used_at.up()

        def hold():
            pe.matmul(PT[:, 0:4], ident, ident[:, 0:4], start=True, stop=True)

        def products(psum, cols, rhs, ready=None, wait=True):
            last = len(rhs) - 1
            if wait:
                piece_split(1)
            for i, (xhi, xlo) in enumerate(rhs):
                if ready:
                    pe.wait_ge(*T.at("xl", ready, i))
                pe.matmul(psum, cols(wh, i), xhi, start=(i == 0), stop=False)
                pe.matmul(psum, cols(wh, i), xlo, start=False, stop=False)
            if wait:
                piece_split(2)
            for i, (xhi, xlo) in enumerate(rhs):
                ins = pe.matmul(psum, cols(wl, i), xhi, start=False, stop=(i == last))
            return ins

        def piece_cols(c0=0, width=P, n=P):
            p = used_at.n % 2
            return lambda w, i: w[:, p, i * width + c0:i * width + c0 + n]

        def gemm_fm(key, rhs, ready=None):
            s = slab_start(key, ready is not None)
            for b in range(2):
                ins = products(bank[2 * s + b][:, :], piece_cols(), rhs, ready if b == 0 else None)
                piece_used(ins, *(("gemm", *key) if b else ()))

        def token_major(s, rhs, cols):
            last = len(rhs) - 1
            for i in range(TT):
                o = bank[2 * s + i // 2][:, i % 2 * 256:i % 2 * 256 + 256]
                t = slice(i * P, i * P + P)
                for j, (xhi, xlo) in enumerate(rhs):
                    pe.matmul(o, xhi[:, t], cols(wh, j), start=(j == 0), stop=False)
                    pe.matmul(o, xlo[:, t], cols(wh, j), start=False, stop=False)
                    ins = pe.matmul(o, xhi[:, t], cols(wl, j), start=False, stop=(j == last))
            return ins

        def gemm_tm(key, rhs, fm_key=None):
            assert used_at.n % 2 == 0
            if fm_key:
                s = slab_start(fm_key)
                for p in range(2):
                    pe.wait_ge(split, used_at.value(T, 2, 4))
                    ins = products(bank[2 * s + p][:, :], lambda w, i: w[:, p, i * P:i * P + P], rhs, wait=False)
                ins.then_inc(*T.up("gemm", *fm_key))
            s = slab_start(key)
            pe.wait_ge(split, used_at.value(T, 2, 4))
            ins = token_major(s, rhs, lambda w, j: w[:, :, j * P:j * P + P])
            used.up()
            used.up("gemm", *key)
            ins.then_inc(used.sem, 2)
            used_at.up()
            used_at.up()

        def parts(a, b, n):
            return [(a[:, i, :], b[:, i, :]) for i in range(n)]

        xk = parts(xh, xl, DC)

        def norm_part(tag, src, one, i):
            pe.wait_ge(*T.at("sq", tag, i))
            ins = pe.matmul(SC[0][:, :], ones[:, one, :], src[i], start=(i == 0), stop=(i == len(src) - 1))
            if i == len(src) - 1:
                ins.then_inc(*T.up("ms", tag))

        def norm(tag, src, one):
            for i in range(len(src)):
                norm_part(tag, src, one, i)

        def norm_behind(tag, m):
            for c in ((), (0, 1), (2, 3), (4, 5, 6, 7))[m]:
                norm_part(tag, sq8, 0, c)

        def group_norm(tag, c, centred):
            if centred:
                pe.wait_ge(*T.at("gin", tag, c))
                pe.matmul(PT[:, :], C("group"), gn[:, 0, :], start=True, stop=True).then_inc(*T.up("gmean", tag, c))
            pe.wait_ge(*T.at("gsq", tag, c))
            pe.matmul(PT[:, :], C("group"), gn[:, 1, :], start=True, stop=True).then_inc(*T.up("gms", tag, c))

        def attention(tag, score, value, mode):
            def scores(u):
                hh, i = u // TT, u % TT
                if u >= 2:
                    pe.wait_ge(*T.at("score_used", tag, u - 2))
                score(SC[u % 2], hh, i).then_inc(*T.up("score", tag, u))

            scores(0)
            scores(1)
            for u in range(NH * TT):
                hh, i = u // TT, u % TT
                pe.wait_ge(*T.at("prob", tag, u))
                if u >= 1:
                    pe.wait_ge(*T.at("probT", tag, u - 1))
                p = (prob if mode == 1 else lprob)[:, u % 2, :]
                pt = (probT if mode == 1 else lprobT)[:, u % 2, :]
                for j in range(i + 1):
                    ins = pe.transpose(PT[:, j * P:j * P + P], p[:, j * P:j * P + P], ident)
                ins.then_inc(*T.up("turned", tag, u))
                if u + 2 < NH * TT:
                    scores(u + 2)
                pe.wait_ge(*T.at("probT", tag, u))
                r = hh % 2 * HD
                for j in range(i + 1):
                    ins = pe.matmul(OB[r:r + HD, i * P:i * P + P], value(hh, j), pt[:, j * P:j * P + P],
                                    start=(j == 0), stop=(j == i))
                ins.then_inc(*T.up("pv", tag, u))

        pe.wait_ge(*T.at("params"))
        for c in range(DC):
            if c >= 2:
                pe.wait_ge(*T.at("x_in", c - 2))
            for i in range(TT):
                ins = pe.transpose(SC[c % 2][:, i * P:i * P + P], xraw[:, i, c * P:c * P + P], ident)
            ins.then_inc(*T.up("x_turned", c))
        pe.transpose(PT[:, 0:A_NROWS], rows_a[0:A_NROWS, :], ident[0:A_NROWS, 0:A_NROWS])
        for j in range(3):
            pe.transpose(PT[:, 128 + 44 * j:172 + 44 * j], rows_c[0:44, j, :], ident[0:44, 0:44])
        n = LAYERS * L_NROWS
        pe.transpose(PT[:, 264:264 + n], rows_l[0:n, :], ident[0:n, 0:n]).then_inc(*T.up("cols_turned"))
        pe.matmul(OB[0:8, :], t5_in[0:32, :], onehot[0:32, 0:512], start=True, stop=True)\
            .then_inc(*T.up("t5a"))
        pe.wait_ge(*T.at("cols_in"))
        pe.matmul(PT[0:8, 0:128], t5_in[0:32, :], onehot[0:32, 512:640], start=True, stop=True)\
            .then_inc(*T.up("t5b"))
        pe.wait_ge(*T.at("x_in", DC - 1))
        sq8 = [normed[:, i, :] for i in range(DC)]
        norm("mix", sq8, 0)
        for name in ("sbq", "sbk", "sbv", "mbq", "mbk", "mbv", "fxq", "fxk", "fxv", "dsq"):
            if name[2] == "v":
                gemm_tm((name,), xk)
            else:
                gemm_fm((name,), xk, "mix" if name == "sbq" else None)
        gemm_fm(("ix",), xk)
        gemm_tm(("dst",), xk, ("dsf",))
        pe.wait_ge(*T.at("t5_rows"))
        pe.wait_ge(*T.at("rstd", "mix"))
        for i in range(8):
            if i >= 2:
                pe.wait_ge(*T.at("bias", i - 2))
            pe.matmul(SC[i % 2][:, :], flip, t5_rows[:, i, :], start=True, stop=True).then_inc(*T.up("flip", i))

        def heads(a, hh):
            return a[hh % 2 * HD:hh % 2 * HD + HD, hh // 2, :]

        def diagonal(o, i, mask):
            return pe.matmul(o[:, i * P:i * P + P], ident, C(mask), start=False, stop=True)

        def qk(o, q, kk, i):
            pe.matmul(o[:, 0:(i + 1) * P], q[:, i * P:i * P + P], kk[:, 0:(i + 1) * P], start=True, stop=False)

        def score_sb(o, hh, i):
            qk(o, heads(sbq, hh), heads(sbk, hh), i)
            return diagonal(o, i, "strict")

        def score_mb(o, hh, i):
            qk(o, heads(mbq, hh), heads(mbk, hh), i)
            return diagonal(o, i, "causal")

        def score_fx(o, hh, i):
            qk(o, heads(fxq, hh), heads(fxk, hh), i)
            one = pick[0:NH, :].rearrange("p (g h q) -> p g h q", g=2, h=NH)
            for j in range(i + 1):
                pe.matmul(o[:, j * P:j * P + P], cum[0:NH, i * P:i * P + P], one[:, 0, hh, :], start=False, stop=False)
            pe.matmul(o[:, 0:(i + 1) * P], one[:, 1, hh, :], cum[0:NH, 0:(i + 1) * P], start=False, stop=False)
            return diagonal(o, i, "causal")

        def score_ds(o, hh, i):
            r = slice(hh % 2 * HD, hh % 2 * HD + HD)
            pe.matmul(o[:, 0:(i + 1) * P], dsq[r, hh // 2, i * P:i * P + P], dsk[r, 0:(i + 1) * P], start=True, stop=False)
            if i == 0:
                return diagonal(o, i, "causal")
            return pe.matmul(o[:, 0:(i + 1) * P], ident, sel[:, i - 1, 0:(i + 1) * P], start=False, stop=True)

        pe.wait_ge(*T.at("bias", 7))
        pe.wait_ge(*T.at("evac", "dst"))
        pe.wait_ge(*T.at("t5_kept"))
        attention("sb", score_sb, lambda hh, j: sbv[:, j, hh * HD:hh * HD + HD], 1)
        pe.wait_ge(*T.at("o", "sb", 1))
        attention("mb", score_mb, lambda hh, j: mbv[:, j, hh * HD:hh * HD + HD], 1)
        pe.wait_ge(*T.at("o", "mb", 1))
        pe.wait_ge(*T.at("cum"))
        attention("fx", score_fx, lambda hh, j: fxv[:, j, hh * HD:hh * HD + HD], 1)
        pe.wait_ge(*T.at("o", "fx", 1))
        n = 0
        for i in range(1, TT):
            for hh in range(8):
                if n >= 2:
                    pe.wait_ge(*T.at("ix_used", n - 2))
                r = slice(hh % 4 * 32, hh % 4 * 32 + 32)
                pe.matmul(SC[n % 2][:, 0:(i + 1) * P], ixq[r, hh // 4, i * P:i * P + P], ixk[r, 0:(i + 1) * P],
                          start=True, stop=True).then_inc(*T.up("ix_score", n))
                n += 1
        pe.wait_ge(*T.at("sel", TT - 2))
        attention("ds", score_ds, lambda hh, j: dsv[:, j, 0:HD], 1)
        pe.wait_ge(*T.at("o", "ds", 1))

        def gate_unit(key, rhs2):
            gemm_fm(("gate", *key), xk)
            s = slab_start(("branch", *key))
            for c in range(2):
                ins = products(bank[2 * s + c][:, :], piece_cols(c * P, 256), rhs2)
            piece_used(ins, "gemm", "branch", *key)

        for half in range(2):
            pe.wait_ge(*T.at("branch_split", half))
            hold()
            with loop(f"gates{half}", DC // 2, [("gate", 2 * half + 1), ("branch", 2 * half + 1)]):
                for b in (2 * half, 2 * half + 1):
                    gate_unit((b,), parts(op_hi[:, b % 2 * 2:, :], op_lo[:, b % 2 * 2:, :], 2))

        def proj(tag, then):
            for j in range(4):
                gemm_fm((tag, j), xk, tag if j == 0 else None)
                norm_behind(then, j)

        def ffn(tag, after, then):
            def up(phase, j):
                gemm_fm((tag, phase, j), xk, after if (phase, j) == ("first", 0) else None)

            def down(phase, half):
                at = DOWN[phase][2]
                rhs = parts(op_hi[:, at:, :], op_lo[:, at:, :], 2)
                for m in (2 * half, 2 * half + 1):
                    s = slab_start((tag, "d" + phase, m), (phase, m) == ("last", 0), phase != "last")
                    for b in range(2):
                        ins = products(bank[2 * s + b][:, :], piece_cols((m % 2 * 2 + b) * P, 512), rhs)
                    if m % 2:
                        piece_used(ins, "gemm", tag, "d" + phase, m)
                    else:
                        ins.then_inc(*T.up("gemm", tag, "d" + phase, m))
                    if phase == "last":
                        norm_behind(then, m)

            for j in range(2):
                up("first", j)
            pe.wait_ge(*T.at("evac", tag, "first", 1))
            hold()
            with loop(tag, FFN_LOOPS, [(tag, "even", 0), (tag, "even", 1)], [(tag, "dodd", 2), (tag, "dodd", 3)]):
                for phase, behind in (("odd", "even"), ("even", "odd")):
                    for j in range(2):
                        up(phase, j)
                        down(behind, j)
            pe.wait_ge(*T.at("hidden", tag, "even", 1))
            for half in range(2):
                down("last", half)

        proj("out", "ffn")
        ffn("c", "ffn", "fin1")

        with Fori(T, pe, "layer", LAYERS):
            norm("f1", sq8, 0)
            ffn("f", "f1", "lm")
            gemm_fm(("cq",), xk, "lm")
            gemm_fm(("ckv",), xk)
            for name, n in (("hf", 2), ("hq", 2), ("hi", 1), ("hg", 1), ("zu", 1), ("zv", 1),
                            ("rq", 1), ("rk", 1), ("rv", 1), ("rg", 1)):
                for j in range(n):
                    if name in ("hi", "zv", "rv"):
                        gemm_tm((name, j), xk)
                    else:
                        gemm_fm((name, j), xk)
            norm("q", [lprob[:, i, :] for i in range(2)], 1)
            pe.wait_ge(*T.at("rstd", "q"))
            norm("kv", [lprobT[:, 0, :]], 2)
            pe.wait_ge(*T.at("xl", "q", 1))
            hold()
            for j in range(2):
                s = slab_start(("uq", j))
                for b in range(2):
                    ins = products(bank[2 * s + b][0:MLA_D, :], piece_cols((2 * j + b) * MLA_D, NH * MLA_D, MLA_D),
                                   parts(op_hi, op_lo, 2))
                if j:
                    piece_used(ins, "gemm", "uq", j)
                else:
                    ins.then_inc(*T.up("gemm", "uq", j))
            pe.wait_ge(*T.at("xl", "kv", 0))
            hold()
            kv_in = parts(op_hi[:, 2:, :], op_lo[:, 2:, :], 1)
            s = slab_start(("uk",))
            for b in range(2):
                ins = products(bank[2 * s + b][:, :], piece_cols(b * P, 512), kv_in)
            ins.then_inc(*T.up("gemm", "uk"))
            s = slab_start(("uv",))
            ins = token_major(s, kv_in, piece_cols(256, 512, 256))
            piece_used(ins, "gemm", "uv")
            swap32 = C("swap32", slice(64, 96))
            for n in range(NH + 1):
                src = qh[64:96, n, :] if n < NH else kh[64:96, 0, :]
                if n == 0:
                    pe.wait_ge(*T.at("rstd", "kv"))
                    pe.wait_ge(*T.at("evac", "uq", 1))
                if n >= 2:
                    pe.wait_ge(*T.at("rot_used", n - 2))
                pe.matmul(SC[n % 2][:, :], swap32, src, start=True, stop=True).then_inc(*T.up("swapped", n))
            pe.wait_ge(*T.at("sg"))
            for i in range(NH):
                ins = pe.transpose(PT[:, i * P:i * P + P], sgw[:, i, :], ident)
            ins.then_inc(*T.up("sgw_turned"))
            hs = C("headsel", slice(0, NH)).rearrange("p (c q) -> p c q", c=2)
            for c in range(2):
                ins = pe.matmul(OB[:, c * P:c * P + P], hs[:, c, :], sgb[0:NH, :], start=True, stop=True)
            ins.then_inc(*T.up("sgb_spread"))
            pe.wait_ge(*T.at("sgwT"))
            pe.wait_ge(*T.at("sgbb"))
            for c in range(2):
                dst = PT if c == 0 else OB
                for hh in (2 * c, 2 * c + 1):
                    r = hh % 2 * HD
                    for i in range(TT):
                        ins = pe.matmul(dst[r:r + HD, i * P:i * P + P], zv[:, i, hh * HD:hh * HD + HD],
                                        sgwT[:, hh, :], start=True, stop=True)
                ins.then_inc(*T.up("sg_mixed", c))
            pe.wait_ge(*T.at("sg_out", 1))

            def score_mla(o, hh, i):
                qk(o, qh[0:MLA_D, hh, :], kh[0:MLA_D, hh, :], i)
                return diagonal(o, i, "causal")

            pe.wait_ge(*T.at("evac", "uv"))
            attention("ml", score_mla, lambda hh, j: mv[:, j, hh * HD:hh * HD + HD], 2)
            pe.wait_ge(*T.at("o", "ml", 1))
            for n in range(4):
                src = (rq, rk)[n // 2][:, n % 2, :]
                if n >= 2:
                    pe.wait_ge(*T.at("ret_rot", n - 2))
                pe.matmul(SC[n % 2][:, :], C("swap"), src, start=True, stop=True).then_inc(*T.up("ret_swap", n))
            pe.wait_ge(*T.at("ret_rot", 3))

            def ret_scores(u):
                hh, j = u // TT, u % TT
                if u >= 2:
                    pe.wait_ge(*T.at("ret_w", u - 2))
                pe.matmul(SC[u % 2][:, 0:S - j * P], heads(rk, hh)[:, j * P:j * P + P], heads(rq, hh)[:, j * P:S],
                          start=True, stop=True).then_inc(*T.up("ret_score", u))

            ret_scores(0)
            for u in range(NH * TT):
                hh, j = u // TT, u % TT
                if u + 1 < NH * TT:
                    ret_scores(u + 1)
                pe.wait_ge(*T.at("ret_w", u))
                if u == 2 * TT:
                    pe.wait_ge(*T.at("gin", "r", 0))
                r = hh % 2 * HD
                pe.matmul(OB[r:r + HD, j * P:S], rv[:, j, hh * HD:hh * HD + HD], lprob[:, u % 2, 0:S - j * P],
                          start=(j == 0), stop=(j == TT - 1)).then_inc(*T.up("ret_pv", u))
                if u in (2 * TT - 1, 4 * TT - 1):
                    c = u // (2 * TT)
                    group_norm("r", c, True)
            n = 0
            for hh in range(NH):
                r = hh % 2 * HD
                for lv in range(len(LEVELS) + 1):
                    if lv < len(LEVELS):
                        pe.wait_ge(*T.at("lvl_k", hh, lv))
                        kk, qq = hK[:, lv % 2, :], hQ[:, lv % 2, :]
                    else:
                        pe.wait_ge(*T.at("lvl_used", n - 2))
                        kk, qq = hk[:, hh, :], hq[:, hh, :]
                    for i in range(TT):
                        ins = pe.matmul(SC[n % 2][:, i * P:i * P + P], kk[:, i * P:i * P + P], qq[:, i * P:i * P + P],
                                        start=True, stop=True)
                    ins.then_inc(*T.up("lvl", n))
                    n += 1
                pe.wait_ge(*T.at("kv3", hh))
                kvs = kv3.rearrange("p (c t) -> p c t", c=3)
                blocks = [(1, kd[:, 0:P]), (2, kd[:, P:2 * P]), (3, kd[:, 2 * P:3 * P]), (2, kvs[:, 0, :]),
                          (3, kvs[:, 1, :]), (3, kvs[:, 2, :])]
                for b, (i, kk) in enumerate(blocks):
                    if b == 4:
                        pe.wait_ge(*T.at("offs", hh, 0))
                    ins = pe.matmul(PT[:, b % 4 * P:b % 4 * P + P], kk, qd[:, i * P:i * P + P], start=True, stop=True)
                    if b in (3, 5):
                        ins.then_inc(*T.up("off", hh, b // 4))
                where = {(1, 0): 0, (2, 1): 1, (3, 2): 2, (2, 0): 3, (3, 1): 4, (3, 0): 5}
                pe.wait_ge(*T.at("offs", hh, 1))
                pe.wait_ge(*T.at("lvl_used", n - 1))
                for i in range(TT):
                    for j in range(i + 1):
                        w = scT[:, i * P:i * P + P] if i == j else off[:, where[i, j] * P:where[i, j] * P + P]
                        ins = pe.matmul(OB[r:r + HD, i * P:i * P + P], hi[:, j, hh * HD:hh * HD + HD], w,
                                        start=(j == 0), stop=(j == i))
                ins.then_inc(*T.up("hg_pv", hh))
                if hh % 2 == 1:
                    group_norm("h", hh // 2, False)
            proj("lout", "f2")
            ffn("g", "f2", "pl")
            pe.wait_ge(*T.at("rstd", "pl"))
            pe.wait_ge(*T.at("pin"))
            for c in range(2):
                for i in range(TT):
                    ins = pe.transpose(SC[c][:, i * P:i * P + P], pin[:, i, c * P:c * P + P], ident)
                ins.then_inc(*T.up("p_turned", c))
            pe.wait_ge(*T.at("p_split"))
            hold()
            with loop("ple", DC // 4, [("gate", "p", 1), ("branch", "p", 1)]):
                for j in range(2):
                    gate_unit(("p", j), parts(op_hi, op_lo, 2))

        norm("fin", sq8, 0)
        pe.wait_ge(*T.at("rstd", "fin"))
        for c in range(DC):
            pe.wait_ge(*T.at("xn", "fin", c))
            if c >= 2:
                pe.wait_ge(*T.at("out_row", c - 2))
            for i in range(TT):
                ins = pe.transpose(SC[c % 2][:, i * P:i * P + P], normed[:, c, i * P:i * P + P], ident)
            ins.then_inc(*T.up("out_turned", c))

    @block.scalar
    def _(act):
        def copy_pair(key, dst, scale=1.0, f=ACT.Copy):
            s = evac_start(key)
            for b in range(2):
                ins = act.activation(dst[b], bank[2 * s + b][:, :], f, scale=scale)
                ins.then_inc(*A.up(*(("evac", *key) if b == 1 else ())))

        def evac_start(key):
            act.wait_ge(*A.at("gemm", *key))
            return pair_of[key]

        def copy_tm(key, dst, f=ACT.Copy):
            copy_pair(key, [dst[:, 2 * b:2 * b + 2, :].rearrange("p i d -> p (i d)") for b in range(2)], f=f)

        def first_parts(tag, src, dst, ready="xn"):
            for i, a in enumerate(src):
                if ready:
                    act.wait_ge(*A.at(ready, tag, i))
                act.activation(dst[:, i, :], a, ACT.Copy).then_inc(*A.up("xh", tag, i))

        def norm(tag, src, tmp, dst=None, ready=None):
            for i, a in enumerate(src):
                if ready:
                    act.wait_ge(*A.at(*ready, i))
                act.activation(tmp[i], a, ACT.Square).then_inc(*A.up("sq", tag, i))
            root("msx", tag)
            if dst is not None:
                first_parts(tag, tmp, dst)

        def root(*what):
            act.wait_ge(*A.at(*what))
            act.activation(nrm[:, 1, :], nrm[:, 0, :], ACT.Sqrt).then_inc(*A.up("rt", *what[1:]))

        hk8 = [h[:, i, :] for i in range(DC)]
        n8 = [normed[:, i, :] for i in range(DC)]

        def two(a):
            return [a[:, 0, :], a[:, 1, :]]

        def attention(tag, odst, mode, biased):
            pr, pt = (prob, probT) if mode == 1 else (lprob, lprobT)

            def expo(u):
                n = (u % TT + 1) * P
                act.wait_ge(*A.at("negmax", tag, u))
                src = pr[:, u % 2, 0:n] if biased else SC[u % 2][:, 0:n]
                if not biased and u >= 2:
                    act.wait_ge(*A.at("turned", tag, u - 2))
                act.activation(pr[:, u % 2, 0:n], src, ACT.Exp, bias=stat[:, u % 2, 1:2],
                               accum_out=stat[:, u % 2, 2:3])\
                    .then_inc(*A.up(*(("expo", tag, u) if biased else ("score_used", tag, u))))

            def copy_turned(u):
                n = (u % TT + 1) * P
                act.wait_ge(*A.at("turned", tag, u))
                act.activation(pt[:, u % 2, 0:n], PT[:, 0:n], ACT.Copy).then_inc(*A.up("probT", tag, u))

            expo(0)
            for u in range(NH * TT):
                if u + 1 < NH * TT:
                    expo(u + 1)
                copy_turned(u)
                if u % (2 * TT) == 2 * TT - 1:
                    c = u // (2 * TT)
                    act.wait_ge(*A.at("pv", tag, u))
                    act.activation(odst[:, c, :], OB[:, :], ACT.Copy).then_inc(*A.up("o", tag, c))

        def stick_breaking():
            def soft3(u):
                n = (u % TT + 1) * P
                a = soft[:, u % 2, 0:n]
                act.wait_ge(*A.at("score", "sb", u))
                if u >= 2:
                    act.wait_ge(*A.at("score_used", "sb", u - 2))
                act.activation(a, SC[u % 2][:, 0:n], ACT.Abs).then_inc(*A.up())
                act.wait_ge(*A.last())
                act.activation(a, a, ACT.Exp, scale=-1.0).then_inc(*A.up())
                act.wait_ge(*A.last())
                act.activation(a, a, ACT.Ln, bias=1.0).then_inc(*A.up("soft", u))

            soft3(0)
            for u in range(NH * TT):
                n = (u % TT + 1) * P
                if u + 1 < NH * TT:
                    soft3(u + 1)
                act.wait_ge(*A.at("score_used", "sb", u))
                act.activation(prob[:, u % 2, 0:n], prob[:, u % 2, 0:n], ACT.Exp).then_inc(*A.up("prob", "sb", u))
                act.wait_ge(*A.at("turned", "sb", u))
                act.activation(probT[:, u % 2, 0:n], PT[:, 0:n], ACT.Copy).then_inc(*A.up("probT", "sb", u))
                if u % (2 * TT) == 2 * TT - 1:
                    c = u // (2 * TT)
                    act.wait_ge(*A.at("pv", "sb", u))
                    act.activation(sbo[:, c, :], OB[:, :], ACT.Copy).then_inc(*A.up("o", "sb", c))

        for c in range(DC):
            act.wait_ge(*A.at("x_turned", c))
            act.activation(h[:, c, :], SC[c % 2][:, :], ACT.Copy).then_inc(*A.up("x_in", c))
        act.wait_ge(*A.at("cols_turned"))
        n = LAYERS * L_NROWS
        act.activation(pcol[:, 0:A_NROWS], PT[:, 0:A_NROWS], ACT.Copy).then_inc(*A.up())
        act.activation(convw.rearrange("p j c -> p (j c)"), PT[:, 128:128 + 6 * FC], ACT.Copy).then_inc(*A.up())
        act.activation(lcol[:, :], PT[:, 264:264 + n], ACT.Copy).then_inc(*A.up("cols_in"))
        act.wait_ge(*A.at("lb_in"))
        act.activation(nrm[:, 2, 0:8], nrm[:, 2, 0:8], ACT.Exp).then_inc(*A.up("lb_exp"))
        for i, a in enumerate(hk8):
            act.activation(n8[i], a, ACT.Square).then_inc(*A.up("sq", "mix", i))
        act.wait_ge(*A.at("t5a"))
        act.activation(t5_rev[0:8, 0:512], OB[0:8, :], ACT.Copy).then_inc(*A.up())
        act.wait_ge(*A.at("t5b"))
        act.activation(t5_rev[0:8, 512:640], PT[0:8, 0:128], ACT.Copy).then_inc(*A.up("t5_kept"))
        act.wait_ge(*A.last())
        act.dma_start(scratch, t5_rev[0:8, :]).then_inc(*spills.up("t5_out"))
        root("msx", "mix")
        first_parts("mix", n8, xh)
        act.wait_ge(*A.at("t5_out"))
        toeplitz = bass.AP(tensor=scratch.tensor, offset=0, ap=[[1, P], [640, 8], [1, 512]])
        act.dma_start(t5_rows, toeplitz).then_inc(*spills.up("t5_rows"))
        q8 = HD ** -0.5
        for name, dst, kind in (("sbq", sbq, "q"), ("sbk", sbk, "k"), ("sbv", sbv, "v"), ("mbq", mbq, "q"),
                                ("mbk", mbk, "k"), ("mbv", mbv, "v"), ("fxq", fxq, "q"), ("fxk", fxk, "k"),
                                ("fxv", fxv, "v"), ("dsq", dsq, "q")):
            if kind == "v":
                copy_tm((name,), dst)
            else:
                copy_pair((name,), two(dst), q8 if kind == "q" else 1.0)
        copy_pair(("ix",), two(ixq))
        s = evac_start(("dsf",))
        for a in range(2):
            act.activation(dsk[a * HD:a * HD + HD, :], bank[2 * s][0:HD, :], ACT.Copy).then_inc(*A.up())
        for a in range(4):
            act.activation(ixk[32 * a:32 * a + 32, :], bank[2 * s + 1][0:32, :], ACT.Copy).then_inc(*A.up())
        act.activation(zlog[0:NH, :], bank[2 * s + 1][HD:HD + NH, :], ACT.Copy).then_inc(*A.up("evac", "dsf"))
        s = evac_start(("dst",))
        for b in range(2):
            src = bank[2 * s + b][:, :].rearrange("p (i d) -> p i d", i=2)
            dst = dsv[:, 2 * b:2 * b + 2, :]
            act.activation(dst[:, :, 0:HD], src[:, :, HD:P], ACT.Copy).then_inc(*A.up())
            act.activation(dst[:, :, HD:], src[:, :, P + 32:P + 40], ACT.Copy)\
                .then_inc(*A.up(*(("evac", "dst") if b else ())))
        for i in range(8):
            act.wait_ge(*A.at("flip", i))
            act.activation(bias[:, i, :], SC[i % 2][:, :], ACT.Copy).then_inc(*A.up("bias", i))
        act.wait_ge(*A.at("zlog"))
        a = soft[0:NH, 0, :]
        act.activation(a, zlog[0:NH, :], ACT.Abs).then_inc(*A.up())
        act.wait_ge(*A.last())
        act.activation(a, a, ACT.Exp, scale=-1.0).then_inc(*A.up())
        act.wait_ge(*A.last())
        act.activation(a, a, ACT.Ln, bias=1.0).then_inc(*A.up("zsoft"))
        act.wait_ge(*A.at("cum"))
        stick_breaking()
        attention("mb", sbq, 1, True)
        attention("fx", sbk, 1, False)
        n = 0
        for i in range(1, TT):
            for hh in range(8):
                act.wait_ge(*A.at("ix_score", n))
                if n >= 2:
                    act.wait_ge(*A.at("ix_added", n - 2))
                act.activation(soft[:, n % 2, 0:(i + 1) * P], SC[n % 2][:, 0:(i + 1) * P], ACT.Relu)\
                    .then_inc(*A.up("ix_used", n))
                n += 1
        attention("ds", mbq, 1, True)

        for half in range(2):
            for i in range(4):
                if half:
                    act.wait_ge(*A.at("evac", "branch", 1))
                act.activation(op_hi[:, i, :], branch_out[2 * half + i // 2][:, i % 2, :], ACT.Copy)\
                    .then_inc(*A.up("branch_first", half, i))
            with Fori(A, act, f"gates{half}", DC // 2):
                for b in (2 * half, 2 * half + 1):
                    s = evac_start(("gate", b))
                    act.wait_ge(*A.at("branch_split", half))
                    act.wait_ge(*A.at("evac", "branch", b, prev=f"gates{half}"))
                    for c in range(2):
                        act.activation(gates[:, b % 2 * 2 + c, :], bank[2 * s + c][:, :], ACT.Sigmoid)\
                            .then_inc(*A.up(*(("evac", "gate", b) if c else ())))

        def ffn(tag):
            def up(phase):
                at = UP[phase][2]
                for j in range(2):
                    s = evac_start((tag, phase, j))
                    act.activation(silu[:, j, :], bank[2 * s][:, :], ACT.Silu).then_inc(*A.up("silu", tag, phase, j))
                    act.wait_ge(*A.at("evac", tag, phase, j))
                    act.activation(op_hi[:, at + j, :], hid[:, j, :], ACT.Copy).then_inc(*A.up("hh", tag, phase, j))

            up("first")
            with Fori(A, act, tag, FFN_LOOPS):
                up("odd")
                up("even")

        def conv_ffn():
            def up(phase):
                at = UP[phase][2]
                for j in range(2):
                    s = evac_start(("c", phase, j))
                    act.activation(padded[:, 2 * j, 2:514], bank[2 * s][:, :], ACT.Copy).then_inc(*A.up())
                    act.activation(padded[:, 2 * j + 1, 2:514], bank[2 * s + 1][:, :], ACT.Copy)\
                        .then_inc(*A.up("evac", "c", phase, j))
                    act.wait_ge(*A.at("conv_g", phase, j))
                    act.activation(silu[:, j, :], conv[:, 2 * j, :], ACT.Gelu).then_inc(*A.up("gelu", phase, j))
                    act.wait_ge(*A.at("hid", phase, j))
                    act.activation(op_hi[:, at + j, :], hid[:, j, :], ACT.Copy).then_inc(*A.up("hh", "c", phase, j))

            up("first")
            with Fori(A, act, "c", FFN_LOOPS):
                up("odd")
                up("even")

        def sincos():
            for n in range(4):
                act.wait_ge(*A.at("angle", n))
                act.activation(rope[:, n, :], rtmp[:, n, :], ACT.Sin).then_inc(*A.up("sin", n))

        act.wait_ge(*A.at("mixed_all"))
        first_parts("out", [mixed[:, i, :] for i in range(DC)], xh, None)
        norm("ffn", hk8, n8, xh, ("added", "out"))
        sincos()
        act.wait_ge(*A.at("pad_zero"))
        conv_ffn()
        norm("fin1", hk8, n8, None, ("added", "c"))

        with Fori(A, act, "layer", LAYERS):
            act.wait_ge(*A.at("xn", "fin1", DC - 1))
            act.wait_ge(*A.at("evac", "branch", "p", 1, prev="layer"))
            norm("f1", hk8, n8, xh)
            ffn("f")
            norm("lm", hk8, n8, xh, ("added", "f"))
            copy_pair(("cq",), two(cq))
            s = evac_start(("ckv",))
            act.activation(ckv, bank[2 * s][:, :], ACT.Copy).then_inc(*A.up())
            act.activation(kh[64:96, 0, :], bank[2 * s + 1][64:96, :], ACT.Copy).then_inc(*A.up("evac", "ckv"))
            for j in range(2):
                copy_pair(("hf", j), [hS[:, 2 * j, :], hS[:, 2 * j + 1, :]], f=ACT.Sigmoid)
            for j in range(2):
                copy_pair(("hq", j), [hq[:, 2 * j, :], hq[:, 2 * j + 1, :]])
            copy_tm(("hi", 0), hi)
            copy_pair(("hg", 0), two(hgate), f=ACT.Silu)
            copy_pair(("zu", 0), two(zu), f=ACT.Gelu)
            copy_tm(("zv", 0), zv, f=ACT.Gelu)
            copy_pair(("rq", 0), two(rq))
            copy_pair(("rk", 0), two(rk), q8)
            copy_tm(("rv", 0), rv)
            copy_pair(("rg", 0), two(rgate), f=ACT.Silu)
            norm("q", two(cq), two(lprob))
            first_parts("q", two(cq), op_hi)
            norm("kv", [ckv], [lprobT[:, 0, :]])
            first_parts("kv", [ckv], op_hi[:, 2:, :])
            for j in range(2):
                s = evac_start(("uq", j))
                for b in range(2):
                    ins = act.activation(qh[0:MLA_D, 2 * j + b, :], bank[2 * s + b][0:MLA_D, :], ACT.Copy,
                                         scale=MLA_D ** -0.5)
                    ins.then_inc(*A.up(*(("evac", "uq", j) if b else ())))
            s = evac_start(("uk",))
            for hh in range(NH):
                ins = act.activation(kh[0:HD, hh, :], bank[2 * s + hh // 2][hh % 2 * HD:hh % 2 * HD + HD, :], ACT.Copy)
                ins.then_inc(*A.up(*(("evac", "uk") if hh == 3 else ())))
            copy_tm(("uv",), mv)
            act.wait_ge(*A.at("sgvar"))
            act.activation(sgst[:, :, 3], sgst[:, :, 2], ACT.Sqrt).then_inc(*A.up("sgroot"))
            act.wait_ge(*A.at("sgb_spread"))
            act.activation(sgbb.rearrange("p c t -> p (c t)"), OB[:, 0:2 * P], ACT.Copy).then_inc(*A.up("sgbb"))
            attention("ml", cq, 2, False)

            def group_in(tag, c, last_pv, centred):
                act.wait_ge(*A.at(*last_pv))
                act.activation(gn[:, 0, :], OB[:, :], ACT.Copy).then_inc(*A.up("gin", tag, c))
                act.wait_ge(*(A.at("gcentred", tag, c) if centred else A.last()))
                act.activation(gn[:, 1, :], gn[:, 0, :], ACT.Square).then_inc(*A.up("gsq", tag, c))
                root("gx", tag, c)

            for c in range(2):
                if c:
                    act.wait_ge(*A.at("gout", "r", c - 1))
                group_in("r", c, ("ret_pv", 2 * TT * (c + 1) - 1), True)
            act.wait_ge(*A.at("gout", "r", 1))
            first_parts("lout", [a[:, c, :] for a in (cq, zu) for c in range(2)], xh, None)
            for c in range(2):
                act.activation(xh[:, 6 + c, :], rgate[:, c, :], ACT.Copy).then_inc(*A.up("xh", "lout", 6 + c))
            for hh in range(NH):
                act.wait_ge(*A.at("forget", hh))
                act.activation(hS[:, hh, :], hS[:, hh, :], ACT.Ln).then_inc(*A.up("logf", hh))
            for hh in range(NH):
                act.wait_ge(*A.at("tail", hh))
                act.activation(hE[:, 0, :], hE[:, 0, :], ACT.Exp).then_inc(*A.up())
                act.activation(hE[:, 1, :], hS[:, hh, :], ACT.Exp).then_inc(*A.up())
                ends = hS[:, hh, :].rearrange("p (n m) -> p n m", n=TT)[:, :, P - 1]
                act.activation(dend, ends, ACT.Exp).then_inc(*A.up("head_exp", hh))
                for lv in range(len(LEVELS)):
                    act.wait_ge(*A.at("lvl_d", hh, lv))
                    act.activation(hE[:, lv % 2, :], hE[:, lv % 2, :], ACT.Exp).then_inc(*A.up("lvl_e", hh, lv))
                act.wait_ge(*A.at("off", hh, 0))
                act.activation(off[:, 0:512], PT[:, :], ACT.Copy).then_inc(*A.up("offs", hh, 0))
                act.wait_ge(*A.at("off", hh, 1))
                act.activation(off[:, 512:768], PT[:, 0:256], ACT.Copy).then_inc(*A.up("offs", hh, 1))
                if hh % 2:
                    if hh == 3:
                        act.wait_ge(*A.at("gout", "h", 0))
                    group_in("h", hh // 2, ("hg_pv", hh), False)
            for c in range(2):
                act.wait_ge(*A.at("gout", "h", c))
                act.activation(xh[:, 4 + c, :], hgate[:, c, :], ACT.Copy).then_inc(*A.up("xh", "lout", 4 + c))
            norm("f2", hk8, n8, xh, ("added", "lout"))
            ffn("g")
            norm("pl", hk8, n8, xh, ("added", "g"))
            for c in range(2):
                act.wait_ge(*A.at("p_turned", c))
                act.activation(op_hi[:, c, :], SC[c][:, :], ACT.Copy).then_inc(*A.up("p_first", c))
            with Fori(A, act, "ple", DC // 4):
                for j in range(2):
                    s = evac_start(("gate", "p", j))
                    act.wait_ge(*A.at("evac", "branch", "p", j, prev="ple"))
                    for c in range(2):
                        act.activation(sg8[:, 2 * j + c, :], bank[2 * s + c][:, :], ACT.Sigmoid)\
                            .then_inc(*A.up(*(("evac", "gate", "p", j) if c else ())))

        act.wait_ge(*A.at("evac", "branch", "p", 1))
        norm("fin", hk8, n8)
        for c in range(DC):
            act.wait_ge(*A.at("out_turned", c))
            dst = outrow[:, :, c * P:c * P + P]
            act.activation(dst, SC[c % 2][:, :].rearrange("p (i d) -> p i d", i=TT), ACT.Copy)\
                .then_inc(*A.up("out_row", c))
        act.wait_ge(*A.last())
        act.activation(stat[:, 0, 3:4], outrow[:, 0, 0:1], ACT.Copy).then_inc(*A.up("out_ready"))

    @block.vector
    def _(v):
        def evac_start(key):
            v.wait_ge(*V.at("gemm", *key))
            return pair_of[key]

        def last():
            v.wait_ge(*V.last())

        def tt(out, a, b, op, *what):
            v.tensor_tensor(out, a, b, op).then_inc(*V.up(*what))

        def ts(out, a, s1, s2, op0, op1, *what):
            if op1 is None:
                v.tensor_scalar(out, a, s1, None, op0).then_inc(*V.up(*what))
            else:
                v.tensor_scalar(out, a, s1, s2, op0, op1).then_inc(*V.up(*what))

        def stt(out, a, s, b, op0, op1, *what):
            v.scalar_tensor_tensor(out=out, in0=a, scalar=s, in1=b, op0=op0, op1=op1).then_inc(*V.up(*what))

        def newton(x, y, t, *what):
            v.reciprocal(y, y).then_inc(*V.up())
            last()
            tt(t, x, y, ALU.mult)
            last()
            tt(t, t, y, ALU.mult)
            last()
            ts(t, t, -0.5, 1.5, ALU.mult, ALU.add)
            last()
            tt(y, y, t, ALU.mult, *what)
            last()

        def rstd(psum, ms, x, tag):
            v.wait_ge(*V.at(*ms))
            last()
            ts(nrm[:, 0, :], psum, EPS, None, ALU.add, None, x, *tag)
            v.wait_ge(*V.at("rt", *tag))
            newton(nrm[:, 0, :], nrm[:, 1, :], nrm[:, 2, :], "rstd", *tag)

        def rest(tag, i, src, first, dst):
            v.wait_ge(*V.at("xh", tag, i))
            tt(dst, src, first.bitcast(F32), ALU.subtract, "xl", tag, i)

        def norm(tag, src, dst, g, first=None, second=None):
            rstd(SC[0][:, :], ("ms", tag), "msx", (tag,))
            for i in range(len(src) + 1):
                if i < len(src):
                    stt(dst[i], src[i], g[:, i:i + 1], nrm[:, 1, :], ALU.mult, ALU.mult, "xn", tag, i)
                if i and first is not None:
                    rest(tag, i - 1, dst[i - 1], first[:, i - 1, :], second[:, i - 1, :])

        hk8 = [h[:, i, :] for i in range(DC)]
        n8 = [normed[:, i, :] for i in range(DC)]

        def attention(tag, mode, table):
            pr = prob if mode == 1 else lprob

            def peak(u):
                hh, i = u // TT, u % TT
                n = (i + 1) * P
                v.wait_ge(*V.at("score", tag, u))
                last()
                if table is not None:
                    if u >= 2:
                        v.wait_ge(*V.at("turned", tag, u - 2))
                    v.tensor_tensor_reduce(pr[:, u % 2, 0:n], SC[u % 2][:, 0:n], bias[:, table + hh, S - n:S], 1.0, GONE,
                                           ALU.add, ALU.max, stat[:, u % 2, 0:1])\
                        .then_inc(*V.up("score_used", tag, u))
                else:
                    v.tensor_reduce(stat[:, u % 2, 0:1], SC[u % 2][:, 0:n], AX.X, ALU.max).then_inc(*V.up())
                last()
                ts(stat[:, u % 2, 1:2], stat[:, u % 2, 0:1], -1.0, None, ALU.mult, None, "negmax", tag, u)

            peak(0)
            for u in range(NH * TT):
                n = (u % TT + 1) * P
                if u + 1 < NH * TT:
                    peak(u + 1)
                v.wait_ge(*V.at(*(("expo", tag, u) if table is not None else ("score_used", tag, u))))
                v.reciprocal(stat[:, u % 2, 3:4], stat[:, u % 2, 2:3]).then_inc(*V.up())
                last()
                ts(pr[:, u % 2, 0:n], pr[:, u % 2, 0:n], stat[:, u % 2, 3:4], None, ALU.mult, None, "prob", tag, u)

        v.memset(ones[:, 0, :], 1.0 / D).then_inc(*V.up())
        v.memset(ones[:, 1, :], 1.0 / 256).then_inc(*V.up())
        v.memset(ones[:, 2, :], 1.0 / 128).then_inc(*V.up())
        v.wait_ge(*V.at("params"))
        v.tensor_copy(levels[:, :], levels_in).then_inc(*V.up())
        v.wait_ge(*V.at("cols_in"))
        a0, a1 = (lcol[:, l * L_NROWS + 21:l * L_NROWS + 25] for l in range(LAYERS))
        e0, e1, m, r = (nrm[:, 2, 4 * i:4 * i + 4] for i in range(4))
        tt(m, a0, a1, ALU.max)
        last()
        tt(e0, a0, m, ALU.subtract)
        tt(e1, a1, m, ALU.subtract, "lb_in")
        v.wait_ge(*V.at("lb_exp"))
        tt(m, e0, e1, ALU.add)
        last()
        v.reciprocal(r, m).then_inc(*V.up())
        last()
        tt(e0, e0, r, ALU.mult)
        tt(e1, e1, r, ALU.mult)
        last()
        tt(m, e0, e1, ALU.add)
        v.memset(lbs[:, 0, 0, :], 0.0).then_inc(*V.up())
        v.memset(lbs[:, 0, 1, :], 1.0).then_inc(*V.up())
        last()
        tt(lbs[:, 1, 0, :], m, e0, ALU.subtract)
        last()
        ts(lbs[:, 1, 1, :], lbs[:, 1, 0, :], -1.0, 1.0, ALU.mult, ALU.add)

        norm("mix", hk8, n8, pcol[:, A_ROWS["mix"]:], xh, xl)
        v.wait_ge(*V.at("bias", 7))
        z = zlog[0:NH, :]
        ts(z, z, cur[0:NH, 49:50], None, ALU.add, None, "zlog")
        v.wait_ge(*V.at("zsoft"))
        last()
        stt(z, z, 0.0, soft[0:NH, 0, :], ALU.min, ALU.subtract)
        last()
        v.tensor_tensor_scan(cum[0:NH, :], z, z, 0.0, ALU.add, ALU.bypass).then_inc(*V.up("cum"))
        for u in range(NH * TT):
            n = (u % TT + 1) * P
            sp, pr, z = soft[:, u % 2, 0:n], prob[:, u % 2, 0:n], SC[u % 2][:, 0:n]
            v.wait_ge(*V.at("soft", u))
            last()
            stt(sp, z, 0.0, sp, ALU.max, ALU.add)
            last()
            if u >= 2:
                v.wait_ge(*V.at("turned", "sb", u - 2))
            v.tensor_tensor_scan(pr[:, ::-1], sp[:, ::-1], sp[:, ::-1], 0.0, ALU.add, ALU.bypass).then_inc(*V.up())
            last()
            tt(pr, z, pr, ALU.subtract, "score_used", "sb", u)
        attention("mb", 1, 0)
        attention("fx", 1, None)
        n = 0
        for i in range(1, TT):
            w = (i + 1) * P
            acc = sel[:, i - 1, 0:w]
            for hh in range(8):
                r = soft[:, n % 2, 0:w]
                wcol = dsv[:, i, HD + hh:HD + hh + 1]
                v.wait_ge(*V.at("ix_used", n))
                last()
                if hh == 0:
                    ts(acc, r, wcol, None, ALU.mult, None, "ix_added", n)
                else:
                    stt(acc, r, wcol, acc, ALU.mult, ALU.add, "ix_added", n)
                n += 1
            last()
            tt(acc[:, i * P:w], acc[:, i * P:w], C("causal"), ALU.add)
            last()
            for r in range(TOPK // 8):
                v.max(top8, acc).then_inc(*V.up())
                last()
                v.match_replace(acc, top8, acc, GONE).then_inc(*V.up())
                last()
            ts(acc, acc, -2e38, NEG, ALU.is_gt, ALU.mult, "sel", i - 1)
        attention("ds", 1, 4)

        for half in range(2):
            for i in range(4):
                v.wait_ge(*V.at("branch_first", half, i))
                tt(op_lo[:, i, :], branch_out[2 * half + i // 2][:, i % 2, :], op_hi[:, i, :].bitcast(F32), ALU.subtract,
                   *(("branch_split", half) if i == 3 else ()))
            with Fori(V, v, f"gates{half}", DC // 2) as it:
                for b in (2 * half, 2 * half + 1):
                    s = evac_start(("branch", b))
                    v.wait_ge(*V.at("evac", "gate", b))
                    for c in range(2):
                        m = mixed[:, bass.ds(it * 2 + c, 1), :]
                        g, o = gates[:, b % 2 * 2 + c:b % 2 * 2 + c + 1, :], bank[2 * s + c][:, :].rearrange("p (c t) -> p c t", c=1)
                        done = ("evac", "branch", b) if c else ()
                        if b == 0:
                            tt(m, g, o, ALU.mult, *done)
                        else:
                            t = soft[:, c:c + 1, :]
                            last()
                            tt(t, g, o, ALU.mult, *done)
                            last()
                            tt(m, m, t, ALU.add)
        last()
        v.memset(stat[:, 0, 3:4], 0.0).then_inc(*V.up("mixed_all"))
        for i in range(DC):
            rest("out", i, mixed[:, i, :], xh[:, i, :], xl[:, i, :])

        def add_slab(tag, key, m, scale, final):
            s = evac_start((*key, m))
            for b in range(2):
                c = 2 * m + b
                last()
                names = [("evac", *key, m)] if b else []
                if final:
                    names.append(("added", tag, c))
                stt(h[:, c, :], bank[2 * s + b][:, :], scale, h[:, c, :], ALU.mult, ALU.add, *(names[0] if names else ()))
                if len(names) > 1:
                    V.same(*names[1])

        def proj(tag):
            for j in range(4):
                add_slab(tag, (tag,), j, 1.0, True)

        def ffn(tag, scale, up):
            def down(phase, half):
                for m in (2 * half, 2 * half + 1):
                    add_slab(tag, (tag, "d" + phase), m, scale, phase == "last")

            for j in range(2):
                up(tag, "first", 0, j)
            for _ in range(2):
                last()
                v.memset(stat[:, 0, 3:4], 0.0).then_inc(*V.up())
            with Fori(V, v, tag, FFN_LOOPS) as it:
                for phase, behind in (("odd", "even"), ("even", "odd")):
                    for j in range(2):
                        up(tag, phase, it, j)
                        down(behind, j)
            for half in range(2):
                down("last", half)

        def hidden_rest(tag, phase, j):
            at = UP[phase][2] + j
            v.wait_ge(*V.at("hh", tag, phase, j))
            tt(op_lo[:, at, :], hid[:, j, :], op_hi[:, at, :].bitcast(F32), ALU.subtract, "hidden", tag, phase, j)

        def gated_up(tag, phase, it, j):
            s = evac_start((tag, phase, j))
            v.wait_ge(*V.at("silu", tag, phase, j))
            tt(hid[:, j, :], silu[:, j, :], bank[2 * s + 1][:, :], ALU.mult, "evac", tag, phase, j)
            hidden_rest(tag, phase, j)

        def conv_up(tag, phase, it, j):
            m, n, _ = UP[phase]
            v.wait_ge(*V.at("evac", "c", phase, j))
            for a in range(2):
                ch = it * (2 * m) + (2 * n + j + a * FC)

                def col(t, c0=0):
                    return t[:, c0 + ch:c0 + ch + 1] if isinstance(ch, int) else t[:, bass.ds(ch + c0, 1)]
                src, dst = padded[:, 2 * j + a, :], conv[:, 2 * j + a, :]
                last()
                ts(dst, src[:, 0:S], col(convw[:, 0, :]), col(pcol, A_ROWS["conv_b"]), ALU.mult, ALU.add)
                for n3 in (1, 2):
                    last()
                    stt(dst, src[:, n3:n3 + S], col(convw[:, n3, :]), dst, ALU.mult, ALU.add,
                        *(("conv_g", phase, j) if n3 == 2 and a == 0 else ()))
            v.wait_ge(*V.at("gelu", phase, j))
            last()
            tt(hid[:, j, :], silu[:, j, :], conv[:, 2 * j + 1, :], ALU.mult, "hid", phase, j)
            hidden_rest("c", phase, j)

        proj("out")
        norm("ffn", hk8, n8, pcol[:, A_ROWS["ffn"]:], xh, xl)
        v.memset(padded[:, :, 0:2], 0.0).then_inc(*V.up("pad_zero"))
        v.wait_ge(*V.at("decay"))
        v.tensor_copy(nrm[:, 0, :], pos_i[:, :].bitcast(I32)).then_inc(*V.up())
        last()
        c1, c2 = 6.28125, 0.0019350051879882812
        c3 = TWO_PI - c1 - c2
        magic = 12582912.0
        for n, (col, turns) in enumerate(((0, 0.25), (0, 0.0), (2, 0.25), (2, 0.0))):
            a, q, r = nrm[:, 1, :], nrm[:, 2, :], rtmp[:, n, :]
            ts(a, nrm[:, 0, :], C("cols")[:, col:col + 1], None, ALU.mult, None)
            last()
            ts(q, a, 1.0 / TWO_PI, turns, ALU.mult, ALU.add)
            last()
            ts(q, q, magic, None, ALU.add, None)
            last()
            ts(q, q, -magic, None, ALU.add, None)
            last()
            stt(r, q, -c1, a, ALU.mult, ALU.add)
            last()
            stt(r, q, -c2, r, ALU.mult, ALU.add)
            last()
            stt(r, q, -c3, r, ALU.mult, ALU.add)
            last()
            if turns:
                ts(r, r, TWO_PI / 4, None, ALU.add, None)
                last()
            ts(r, r, 3.1415925, -3.1415925, ALU.min, ALU.max, "angle", n)
            last()
        for n, col in ((1, 1), (3, 3)):
            v.wait_ge(*V.at("sin", n))
            ts(rope[:, n, :], rope[:, n, :], C("cols")[:, col:col + 1], None, ALU.mult, None, "rope", n)
        ffn("c", 1.0, conv_up)
        norm("fin1", hk8, hk8, pcol[:, A_ROWS["fin1"]:])

        with Fori(V, v, "layer", LAYERS) as l:
            last()
            v.tensor_copy(cur[:, 0:L_NROWS], lcol[:, bass.ds(l * L_NROWS, L_NROWS)]).then_inc(*V.up())
            v.tensor_copy(cur[:, L_NROWS:L_NROWS + 8].rearrange("p (o a h) -> p o a h", o=1, a=2),
                          lbs[:, bass.ds(l, 1), :, :]).then_inc(*V.up())

            def g(name):
                return cur[:, L_ROWS[name]:]

            norm("f1", hk8, n8, g("ffn1"), xh, xl)
            ffn("f", 0.5, gated_up)
            norm("lm", hk8, n8, g("mix"), xh, xl)
            norm("q", [cq[:, i, :] for i in range(2)], [cq[:, i, :] for i in range(2)], g("q"), op_hi, op_lo)
            norm("kv", [ckv], [ckv], g("kv"), op_hi[:, 2:, :], op_lo[:, 2:, :])
            for n in range(NH + 1):
                x0 = qh[64:96, n, :] if n < NH else kh[64:96, 0, :]
                t0 = lprob[64:96, n % 2, :]
                v.wait_ge(*V.at("swapped", n))
                last()
                tt(t0, SC[n % 2][64:96, :], rope[64:96, 3, :], ALU.mult, "rot_used", n)
                tt(x0, x0, rope[64:96, 2, :], ALU.mult)
                last()
                tt(x0, x0, t0, ALU.add)
            last()
            for n in range(1, NH):
                v.tensor_copy(kh[64:96, n, :], kh[64:96, 0, :]).then_inc(*V.up(*(("k_rot",) if n == NH - 1 else ())))
            v.wait_ge(*V.at("evac", "zv", 0))
            for i in range(TT):
                zi, st = zv[:, i, :], sgst[:, i, :]
                v.tensor_reduce(st[:, 0:1], zi, AX.X, ALU.add).then_inc(*V.up())
                last()
                ts(st[:, 0:1], st[:, 0:1], -1.0 / 256, None, ALU.mult, None)
                last()
                ts(zi, zi, st[:, 0:1], None, ALU.add, None)
                last()
                v.tensor_tensor_reduce(nrm[:, 2, 0:256], zi, zi, 1.0 / 256, 0.0, ALU.mult, ALU.add, st[:, 1:2])\
                    .then_inc(*V.up())
                last()
            ts(sgst[:, :, 2], sgst[:, :, 1], EPS, None, ALU.add, None, "sgvar")
            v.wait_ge(*V.at("sgroot"))
            newton(sgst[:, :, 2], sgst[:, :, 3], sgst[:, :, 4])
            for i in range(TT):
                ts(zv[:, i, :], zv[:, i, :], sgst[:, i, 3:4], None, ALU.mult, None, *(("zv_normed",) if i == TT - 1 else ()))
            v.wait_ge(*V.at("sgw_turned"))
            tt(sgwT, PT[:, :].rearrange("p (h t) -> p h t", h=NH), C("tril")[:, None, :].to_broadcast([P, NH, P]),
               ALU.mult, "sgwT")
            for c in range(2):
                y = lprobT[:, 1, :]
                v.wait_ge(*V.at("sgbb"))
                v.wait_ge(*V.at("sg_mixed", c))
                last()
                stt(y.rearrange("p (i t) -> p i t", i=TT), (PT if c == 0 else OB)[:, :].rearrange("p (i t) -> p i t", i=TT),
                    g("sg")[:, c:c + 1], sgbb[:, c:c + 1, :].to_broadcast([P, TT, P]), ALU.mult, ALU.add)
                last()
                tt(zu[:, c, :], zu[:, c, :], y, ALU.mult, "sg_out", c)
            attention("ml", 2, None)

            for n in range(4):
                x0 = (rq, rk)[n // 2][:, n % 2, :]
                t0 = lprobT[:, n % 2, :]
                v.wait_ge(*V.at("ret_swap", n))
                last()
                tt(t0, SC[n % 2][:, :], rope[:, 1, :], ALU.mult)
                tt(x0, x0, rope[:, 0, :], ALU.mult)
                last()
                tt(x0, x0, t0, ALU.add, "ret_rot", n)

            def group_out(tag, c, gain, gate, centred):
                if centred:
                    v.wait_ge(*V.at("gmean", tag, c))
                    last()
                    tt(gn[:, 0, :], gn[:, 0, :], PT[:, :], ALU.subtract, "gcentred", tag, c)
                rstd(PT[:, :], ("gms", tag, c), "gx", (tag, c))
                stt(gn[:, 1, :], gn[:, 0, :], gain[:, c:c + 1], nrm[:, 1, :], ALU.mult, ALU.mult)
                last()
                tt(gate[:, c, :], gate[:, c, :], gn[:, 1, :], ALU.mult, "gout", tag, c)

            for u in range(NH * TT):
                hh, j = u // TT, u % TT
                n = S - j * P
                v.wait_ge(*V.at("ret_score", u))
                tt(lprob[:, u % 2, 0:n], SC[u % 2][:, 0:n], decay[:, hh, 0:n], ALU.mult, "ret_w", u)
                if u in (2 * TT, 4 * TT - 1):
                    group_out("r", u // (3 * TT), g("ret"), rgate, True)

            parts = (cq, zu, hgate, rgate)
            for i in (0, 1, 2, 3, 6, 7):
                rest("lout", i, parts[i // 2][:, i % 2, :], xh[:, i, :], xl[:, i, :])
            for hh in range(NH):
                f = hS[:, hh, :]
                last()
                ts(f, f, cur[:, L_NROWS + 4 + hh:L_NROWS + 5 + hh], cur[:, L_NROWS + hh:L_NROWS + 1 + hh], ALU.mult, ALU.add)
                last()
                ts(hk[:, hh, :], f, -1.0, 1.0, ALU.mult, ALU.add)
                ts(f, f, 2.0 ** -63, None, ALU.max, None, "forget", hh)
            for hh in range(NH):
                f, t0 = hS[:, hh, :], hQ[:, hh % 2, :]
                v.wait_ge(*V.at("logf", hh))
                last()
                v.tensor_copy(t0, f).then_inc(*V.up())
                last()
                for i in range(TT):
                    t = slice(i * P, i * P + P)
                    v.tensor_tensor_scan(f[:, t], t0[:, t], t0[:, t], 0.0, ALU.add, ALU.bypass).then_inc(*V.up())
            last()
            v.memset(hQ, 0.0).then_inc(*V.up())
            v.memset(hK, 0.0).then_inc(*V.up())
            v.memset(scT, 0.0).then_inc(*V.up())
            n = 0
            for hh in range(NH):
                f = hS[:, hh, :]
                f4 = f.rearrange("p (n m) -> p n m", n=TT)

                def split(a, m):
                    a = a.rearrange("p (n two m) -> p n two m", two=2, m=m)
                    return a[:, :, 0, :], a[:, :, 1, :]

                def distances(lv):
                    m = LEVELS[lv]
                    early, late = split(f, m)
                    e_early, e_late = split(hE[:, lv % 2, :], m)
                    ref = early[:, :, m - 1:m].to_broadcast([P, S // (2 * m), m])
                    last()
                    tt(e_late, late, ref, ALU.subtract)
                    tt(e_early, ref, early, ALU.subtract, "lvl_d", hh, lv)

                def masked(x):
                    lx = x % (len(LEVELS) + 1)
                    v.wait_ge(*V.at("lvl", x))
                    last()
                    v.memset(stat[:, 0, 3:4], 0.0).then_inc(*V.up())
                    m = levels[:, lx * P:lx * P + P][:, None, :].to_broadcast([P, TT, P])
                    v.copy_predicated(scT.rearrange("p (i t) -> p i t", i=TT), m,
                                      SC[x % 2][:, :].rearrange("p (i t) -> p i t", i=TT)).then_inc(*V.up("lvl_used", x))

                last()
                tt(hE[:, 0, :].rearrange("p (n m) -> p n m", n=TT), f4[:, :, P - 1:P].to_broadcast([P, TT, P]), f4,
                   ALU.subtract, "tail", hh)
                v.wait_ge(*V.at("head_exp", hh))
                if hh:
                    v.wait_ge(*V.at("off", hh - 1, 1))
                tt(qd, hq[:, hh, :], hE[:, 1, :], ALU.mult)
                tt(kd, hk[:, hh, :], hE[:, 0, :], ALU.mult)
                last()
                kvs = kv3.rearrange("p (c t) -> p c t", c=3)
                ts(kvs[:, 0, :], kd[:, 0:P], dend[:, 1:2], None, ALU.mult, None)
                ts(kvs[:, 1, :], kd[:, P:2 * P], dend[:, 2:3], None, ALU.mult, None)
                last()
                ts(kvs[:, 2, :], kvs[:, 0, :], dend[:, 2:3], None, ALU.mult, None, "kv3", hh)
                distances(0)
                for lv in range(len(LEVELS)):
                    if lv + 1 < len(LEVELS):
                        distances(lv + 1)
                    m = LEVELS[lv]
                    e_early, e_late = split(hE[:, lv % 2, :], m)
                    v.wait_ge(*V.at("lvl_e", hh, lv))
                    if n >= 2:
                        v.wait_ge(*V.at("lvl", n - 2))
                    last()
                    tt(split(hQ[:, lv % 2, :], m)[1], split(hq[:, hh, :], m)[1], e_late, ALU.mult)
                    tt(split(hK[:, lv % 2, :], m)[0], split(hk[:, hh, :], m)[0], e_early, ALU.mult, "lvl_k", hh, lv)
                    if lv:
                        masked(n - 1)
                    n += 1
                n += 1
                masked(n - 2)
                masked(n - 1)
                if hh % 2:
                    group_out("h", hh // 2, g("hg"), hgate, False)
            for i in (4, 5):
                rest("lout", i, hgate[:, i % 2, :], xh[:, i, :], xl[:, i, :])
            v.memset(stat[:, 0, 3:4], 0.0).then_inc(*V.up())
            proj("lout")
            norm("f2", hk8, n8, g("ffn2"), xh, xl)
            ffn("g", 0.5, gated_up)
            norm("pl", hk8, n8, g("ple"), xh, xl)
            for c in range(2):
                v.wait_ge(*V.at("p_first", c))
                tt(op_lo[:, c, :], SC[c][:, :], op_hi[:, c, :].bitcast(F32), ALU.subtract, *(("p_split",) if c else ()))
            with Fori(V, v, "ple", DC // 4) as it:
                for j in range(2):
                    s = evac_start(("branch", "p", j))
                    v.wait_ge(*V.at("evac", "gate", "p", j))
                    for c in range(2):
                        a = sg8[:, 2 * j + c:2 * j + c + 1, :]
                        last()
                        tt(a, a, bank[2 * s + c][:, :].rearrange("p (c t) -> p c t", c=1), ALU.mult)
                        last()
                        hc = h[:, bass.ds(it * 4 + (2 * j + c), 1), :]
                        tt(hc, hc, a, ALU.add, *(("evac", "branch", "p", j) if c else ()))
        norm("fin", hk8, n8, pcol[:, A_ROWS["fin2"]:])


_INS = ["x", "norm_mix_g", "norm_ffn_g", "norm_final_g", "w_in", "fox_b_f", "t5_bias", "w_gate", "w_branch", "w_out",
        "w_up", "conv_w", "conv_b", "w_down", "p_2", "positions_2", "ffn1_norm_2", "ffn1_w_gate_2", "ffn1_w_up_2",
        "ffn1_w_down_2", "mix_norm_2", "w_in_2", "mla_q_norm_2", "mla_w_uq_2", "mla_kv_norm_2", "mla_w_ukv_2",
        "sg_ln_2", "sg_w_s_2", "sg_b_s_2", "hg_lb_logits_2", "hg_norm_2", "ret_norm_2", "w_out_2", "ffn2_norm_2",
        "ffn2_w_gate_2", "ffn2_w_up_2", "ffn2_w_down_2", "ple_norm_2", "ple_w_proj_2", "ple_w_gate_2",
        "final_norm_2"]


def build(nc, arrays, known=None):
    k = {n: nc.dram_tensor(f"in_{n}", a.shape, mybir.dt.from_np(a.dtype), kind="ExternalInput").ap()
         for n, a in arrays.items()}
    out = nc.dram_tensor("out_0", (1, S, D), F32, kind="ExternalOutput").ap()
    scratch = nc.dram_tensor("t5_by_distance", (8, 640), F32).ap()
    book = Book(known)
    program(nc, k["x"][0], out[0], k, scratch, book)
    return book


def kernel(**inputs):
    import concourse.bacc as bacc
    from concourse.bass_utils import run_bass_kernel_spmd

    arrays = {n: np.ascontiguousarray(inputs[n]) for n in _INS}
    arrays["const"] = np.concatenate(list(constants().values()), 1)
    arrays.update(first_constants())
    arrays["levels"] = level_masks()
    arrays["decay"] = decays()
    counted = build(bacc.Bacc("TRN2", target_bir_lowering=False, num_devices=1), arrays)
    nc = bacc.Bacc("TRN2", target_bir_lowering=False, num_devices=1)
    build(nc, arrays, counted)
    r = run_bass_kernel_spmd(nc, [{f"in_{n}": a for n, a in arrays.items()}], core_ids=[0])
    return r.results[0]["out_0"]
```

```python
from contextlib import ExitStack

import numpy as np

import concourse.bass as bass
from concourse import mybir

F32 = mybir.dt.float32
F32R = mybir.dt.float32r
U8 = mybir.dt.uint8
I32 = mybir.dt.int32
ACT = mybir.ActivationFunctionType
ALU = mybir.AluOpType
AX = mybir.AxisListType

P = 128
S = 512
TT = S // P
D = 1024
DC = D // P
FF = 2816
FC = FF // P
HD = 64
NH = 4
LAYERS = 2
EPS = 1e-6
NEG = -1e30
GONE = -3e38
TOPK = 128
PIECE = 1024
ARENA = 26920
MLA_D = 96
TWO_PI = 2.0 * float(np.pi)
LEVELS = [64, 32, 16, 8, 4, 2, 1]

A_COLS = dict(sbq=0, sbk=256, sbv=512, mbq=768, mbk=1024, mbv=1280, fxq=1536, fxk=1792, fxv=2048,
              fxf=2304, dsq=2308, dsk=2564, dsv=2628, ixq=2692, ixk=2948, ixw=2980)
B_COLS = dict(cq=0, ckv=256, zu=416, zv=672, hq=928, hf=1440, hi=1952, hg=2208,
              rq=2464, rk=2720, rv=2976, rg=3232)
SB_BEHIND = ("mbq", "mbk", "mbv", "fxq", "fxk", "fxv", "dsq", "ix")
MLA_BEHIND = ("zu", "zv", "rq", "rk", "rv")
A_ROWS = dict(mix=0, ffn=8, fin1=16, fin2=24, conv_b=32)
A_NROWS = 32 + 2 * FC
L_ROWS = dict(ffn1=0, mix=8, q=16, kv=18, sg=19, lb=21, hg=25, ret=27, ffn2=29, ple=37)
L_NROWS = 45


def unit_of(piece):
    return next(u for u in range(16) if piece < (u + 1) * 20 // 16)


def t5_bucket(n):
    n = np.maximum(n, 0)
    large = 16 + (np.log(np.maximum(n, 1) / 16.0) / np.log(8.0) * 16).astype(np.int64)
    return np.where(n < 16, n, np.minimum(large, 31))


def constants():
    p = np.arange(P)
    c = {}
    c["ident"] = np.eye(P)
    c["causal"] = np.where(p[None, :] > p[:, None], NEG, 0.0)
    c["strict"] = np.where(p[None, :] >= p[:, None], NEG, 0.0)
    swap = np.zeros((P, P))
    swap[p, p // 64 * 64 + (p % 64 + 32) % 64] = 1.0
    c["swap"] = swap
    swap32 = np.zeros((P, P))
    swap32[64 + np.arange(32), 64 + (np.arange(32) + 16) % 32] = 1.0
    c["swap32"] = swap32
    c["group"] = np.where(p[:, None] // 64 == p[None, :] // 64, 1.0 / 64, 0.0)
    c["tril"] = (p[:, None] <= p[None, :]).astype(float)
    f32 = np.float32
    inv64 = (f32(10000.0) ** (-np.arange(0, 64, 2, dtype=f32) / f32(64))).astype(f32)
    inv32 = (f32(10000.0) ** (-np.arange(0, 32, 2, dtype=f32) / f32(32))).astype(f32)
    cols = np.zeros((P, 4))
    cols[:, 0] = inv64[p % 32]
    cols[:, 1] = np.where(p % 64 < 32, -1.0, 1.0)
    cols[:, 2] = inv32[p % 16]
    cols[:, 3] = np.where(p % 32 < 16, -1.0, 1.0)
    c["cols"] = cols
    headsel = np.zeros((P, 2, P))
    for h in range(NH):
        headsel[h, h // 2, (h % 2) * 64:(h % 2) * 64 + 64] = 1.0
    c["headsel"] = headsel.reshape(P, -1)
    return {k: np.asarray(v, np.float32) for k, v in c.items()}


def first_constants():
    p = np.arange(P)
    onehot = np.zeros((P, 640))
    onehot[t5_bucket(511 - np.arange(640)), np.arange(640)] = 1.0
    pick = np.zeros((P, 2, NH, P))
    for h in range(NH):
        pick[h, 0, h, :] = 1.0
        pick[h, 1, h, :] = -1.0
    c = dict(onehot=onehot, flip=np.eye(P)[::-1], pick=pick.reshape(P, -1))
    return {k: np.asarray(v, np.float32) for k, v in c.items()}


def level_masks():
    p = np.arange(P)
    lev = [(p[None, :] // m % 2 == 1) & (p[:, None] // m == p[None, :] // m - 1) for m in LEVELS]
    lev.append(p[:, None] == p[None, :])
    return np.concatenate(lev, 1).astype(np.float32)


def decays():
    p, u = np.arange(P)[:, None], np.arange(S)[None, :]
    f32 = np.float32
    lg = np.log1p(-np.power(f32(2.0), -(f32(5.0) + np.arange(NH, dtype=f32)))).astype(f32)
    d = [np.where(u >= p, np.exp(np.maximum(u - p, 0).astype(f32) * g), 0.0) for g in lg]
    return np.concatenate(d, 1).astype(f32)


CONST_AT = {}
_n = 0
for _name, _a in constants().items():
    CONST_AT[_name] = (_n, _a.shape[1])
    _n += _a.shape[1]
CONST_N = _n


UP = dict(first=(0, 0, 0), odd=(2, 1, 2), even=(2, 2, 0))
DOWN = dict(even=(2, 0, 0), odd=(2, 1, 2), last=(0, FC // 2 - 1, 0))
FFN_LOOPS = (FC // 2 - 1) // 2


class Book:

    def __init__(self, known=None):
        self.marks = {}
        self.body = {}
        self.trips = {}
        self.known = known
        self.pieces = 0


class Count:

    def __init__(self, book, sem, name, unit=1):
        self.book, self.sem, self.name, self.unit = book, sem, name, unit
        self.n = 0
        self.loops = []

    def enter(self, loop):
        self.loops.append((loop, self.n))

    def leave(self, trips):
        loop, start = self.loops.pop()
        self.book.body[loop, self.name] = self.n - start
        self.book.trips[loop] = trips
        self.n = start + (self.n - start) * trips

    def up(self, *what):
        self.n += self.unit
        if what:
            assert what not in self.book.marks, what
            self.book.marks[what] = (self.sem, self.name, self.n, tuple(x for x, _ in self.loops))
        return self.sem, self.unit


class Pieces(Count):

    def value(self, e, mul, add):
        known = self.book.known
        v = self.n * mul + add
        for loop, _ in self.loops:
            stride = known.body[loop, self.name] if known else 0
            assert stride % 2 == 0
            if stride:
                v = e.regs[loop] * (stride * mul) + v
        return v


class Engine(Count):

    def __init__(self, book, sem, name):
        super().__init__(book, sem, name)
        self.regs = {}
        self.others = []

    def begin(self, loop, reg):
        self.regs[loop] = reg
        for c in (self, *self.others):
            c.enter(loop)

    def end(self, loop, trips):
        for c in (self, *self.others):
            c.leave(trips)
        del self.regs[loop]

    def value(self, sem_name, n, loops, prev=None):
        known = self.book.known
        v, terms = n, []
        for loop in loops:
            stride = known.body[loop, sem_name] if known else 0
            if loop in self.regs:
                terms.append((self.regs[loop], stride))
                if loop == prev:
                    v -= stride
            elif known:
                v += stride * (known.trips[loop] - 1)
        for reg, stride in terms:
            if stride:
                v = reg * stride + v
        return v

    def at(self, *what, prev=None):
        known = self.book.known
        if known is None:
            return self.sem, 1
        _, name, n, loops = known.marks[what]
        return self.book.sems[name], self.value(name, n, loops, prev)

    def same(self, *what):
        assert what not in self.book.marks, what
        self.book.marks[what] = (self.sem, self.name, self.n, tuple(x for x, _ in self.loops))

    def last(self):
        return self.sem, self.value(self.name, self.n, [x for x, _ in self.loops])


class Fori:

    def __init__(self, e, eng, loop, trips):
        self.e, self.loop, self.trips = e, loop, trips
        self.inner = eng.Fori(0, trips)

    def __enter__(self):
        reg = self.inner.__enter__()
        self.e.begin(self.loop, reg)
        return reg

    def __exit__(self, *a):
        self.e.end(self.loop, self.trips)
        return self.inner.__exit__(*a)


def program(nc, x, out, k, scratch, book):
    ctx = ExitStack()

    def sb(name, shape, dt=F32):
        return ctx.enter_context(nc.sbuf_tensor(name, shape, dt))

    def sem(name):
        return ctx.enter_context(nc.semaphore(name))

    h = sb("h", [P, DC, S])
    xh, xl = sb("xh", [P, DC, S], F32R), sb("xl", [P, DC, S], F32R)
    op_hi, op_lo = sb("op_hi", [P, 4, S], F32R), sb("op_lo", [P, 4, S], F32R)
    raw = sb("raw", [P, 2, PIECE])
    wh, wl = sb("wh", [P, 2, PIECE], F32R), sb("wl", [P, 2, PIECE], F32R)
    const = sb("const", [P, CONST_N])
    levels = sb("levels", [P, 8 * P], U8)
    pcol = sb("pcol", [P, A_NROWS // 4 * 4])
    convw = sb("convw", [P, 3, 2 * FC])
    lcol = sb("lcol", [P, LAYERS * L_NROWS])
    lbs = sb("lbs", [P, LAYERS, 2, NH])
    cur = sb("cur", [P, L_NROWS + 8])
    ones = sb("ones", [P, 3, P])
    nrm = sb("nrm", [P, 3, S])
    stat = sb("stat", [P, 2, 4])
    zero = sb("zero", [P, 1])
    eps = sb("eps", [P, 1])
    arena = sb("arena", [P, ARENA])

    def C(name, rows=slice(0, P)):
        a, n = CONST_AT[name]
        return const[rows, a:a + n]

    spot = [0]

    def area(n, at=None):
        if at is not None:
            spot[0] = at
        a = spot[0]
        spot[0] += n
        assert spot[0] <= ARENA, spot[0]
        return arena[:, a:a + n]

    def chunks(a, n=2):
        return a.rearrange("p (c t) -> p c t", c=n)

    normed = chunks(area(4096, 0), DC)
    xraw = area(4096, 8192).rearrange("p (i d) -> p i d", i=TT)
    rows_a = area(P)
    rows_c = area(3 * P).rearrange("p (j q) -> p j q", j=3)
    rows_l = area(P)
    t5_in = area(8)
    t5_rev = area(640)
    t5_rows = area(4096, 14200).rearrange("p (h u) -> p h u", h=8)
    attn = chunks(area(1024, 0))
    sbq, sbk = chunks(area(1024)), chunks(area(1024))
    sbv = area(1024).rearrange("p (i d) -> p i d", i=TT)
    zlog = area(1024)
    mbq, mbk, fxq, fxk, dsq = (chunks(area(1024)) for _ in range(5))
    mbv, fxv = (area(1024).rearrange("p (i d) -> p i d", i=TT) for _ in range(2))
    mixed = chunks(arena[:, 1024:5120], DC)
    late_gates = chunks(arena[:, 5120:9216], DC)
    dsk = area(512)
    ixq = chunks(area(1024))
    ixk = area(512)
    dsv = area(TT * 72).rearrange("p (i d) -> p i d", i=TT)
    cum = area(512)
    prob = chunks(area(1024))
    probT = chunks(area(1024))
    soft = chunks(area(1024))
    sel = chunks(area(1536), 3)
    top8 = area(8)
    gates_at = spot[0]
    gates = chunks(area(2048), 4)
    bias = area(4096).rearrange("p (h u) -> p h u", h=8)
    levels_in = area(8 * P, gates_at + 2048)
    onehot, flip = area(640, gates_at), area(P)
    pick = area(1024, gates_at + 2048 + 4096)
    padded = chunks(area(4 * 514, 5000), 4)
    conv = chunks(area(4 * S), 4)
    silu = chunks(area(2 * S), 2)
    hid = chunks(area(2 * S), 2)
    top = ARENA - 2 * 4 * S
    decay = area(NH * S, top).rearrange("p (h u) -> p h u", h=NH)
    rope = area(4 * S).rearrange("p (h u) -> p h u", h=4)
    pos_i = area(S, 17000)
    rtmp = chunks(area(4 * S), 4)
    cq = chunks(area(1024, 0))
    ckv = area(512)
    zu, zv = chunks(area(1024)), area(1024).rearrange("p (i d) -> p i d", i=TT)
    hq, hS, hk = chunks(area(2048), 4), chunks(area(2048), 4), chunks(area(2048), 4)
    hi = area(1024).rearrange("p (i d) -> p i d", i=TT)
    hgate = chunks(area(1024))
    rgate = chunks(area(1024))
    ret_at = spot[0]
    rq, rk = chunks(area(1024)), chunks(area(1024))
    rv = area(1024).rearrange("p (i d) -> p i d", i=TT)
    mv = area(1024).rearrange("p (i d) -> p i d", i=TT)
    sgw = area(512).rearrange("p (h s) -> p h s", h=NH)
    sgwT = area(512).rearrange("p (h s) -> p h s", h=NH)
    sgb = area(P)
    sgbb = chunks(area(256))
    sgst = area(TT * 8).rearrange("p (i d) -> p i d", i=TT)
    scratch_at = spot[0]
    lprob, lprobT = chunks(area(1024)), chunks(area(1024))
    qh = chunks(area(2048), 4)
    gn = qh[:, 0:2, :]
    kh = hk
    mla_end = spot[0]
    hE, hQ, hK = chunks(area(1024, ret_at)), chunks(area(1024)), chunks(area(1024))
    scT, qd = area(512), area(512)
    off = area(768, scratch_at)
    kd = area(512)
    kv3 = area(384)
    dend = area(4)
    assert max(mla_end, spot[0]) <= top, (mla_end, spot[0], top)
    pin = area(1024, 12000).rearrange("p (i d) -> p i d", i=TT)
    sg8 = chunks(area(2048), 4)
    outrow = area(4096, 8192).rearrange("p (i d) -> p i d", i=TT)

    bank = [ctx.enter_context(nc.psum_tensor(f"bank{i}", [P, S], F32)) for i in range(8)]
    SC, PT, OB = bank[4:6], bank[6], bank[7]

    names = ["tensor_done", "vector_done", "scalar_done", "landed0", "landed1", "pieces_split", "pieces_used",
             "loads", "first_loads", "spills", "stores", "zero_ready"]
    book.sems = {n: sem(n) for n in names}
    landed = [book.sems["landed0"], book.sems["landed1"]]
    split = book.sems["pieces_split"]
    T = Engine(book, book.sems["tensor_done"], "tensor_done")
    V = Engine(book, book.sems["vector_done"], "vector_done")
    A = Engine(book, book.sems["scalar_done"], "scalar_done")
    Q = Engine(book, book.sems["stores"], "stores")
    used = Count(book, book.sems["pieces_used"], "pieces_used")
    used_at = Pieces(book, None, "piece_of_products")
    load_at = Pieces(book, None, "piece_of_loads")
    loads = Count(book, book.sems["loads"], "loads", 16)
    first_loads = Count(book, book.sems["first_loads"], "first_loads", 16)
    spills = Count(book, book.sems["spills"], "spills", 16)
    Q.unit = 16
    Q.others = [load_at, loads]
    T.others = [used, used_at]
    A.others = [spills]
    pair_of = {}

    block = ctx.enter_context(nc.Block())

    ident = C("ident")

    @block.sync
    def _(sp):
        def load(dst, src, *what):
            sp.dma_start(dst, src).then_inc(*loads.up(*what))

        def rowload(dst, src, n):
            load(dst[0:n, :], src.rearrange("(c q) -> c q", q=P))

        def piece(*parts):
            s = load_at.n % 2
            for dst, src in parts:
                if load_at.n >= 2:
                    sp.wait_ge(split, load_at.value(Q, 2, -2))
                sp.dma_start(dst(raw[:, s, :]), src).then_inc(landed[s], 16)
            assert len(parts) == 2
            load_at.up()

        def whole(w, c0):
            def half(a):
                def dst(slot):
                    return slot.rearrange("p (k c) -> p k c", k=DC)[:, a:a + DC // 2, :]
                return dst, w.rearrange("(k p) c -> p k c", p=P)[:, a:a + DC // 2, bass.ds(c0, P)]
            piece(half(0), half(DC // 2))

        def two_rows(w, k0, c0, n):
            def row(i):
                def dst(slot):
                    return slot[:, i * n:i * n + n].rearrange("p (k c) -> p k c", k=1)
                return dst, w.rearrange("(k p) c -> p k c", p=P)[:, bass.ds(k0 + i, 1), bass.ds(c0, n)]
            piece(row(0), row(1))

        def slab(w, c0):
            whole(w, c0)
            whole(w, c0 + P)

        def some(w, c0, n, at):
            def dst(slot):
                return slot.rearrange("p (k c) -> p k c", k=DC)[:, :, at:at + n]
            return dst, w.rearrange("(k p) c -> p k c", p=P)[:, :, bass.ds(c0, n)]

        sp.dma_start(xraw, x.rearrange("(i p) d -> p i d", p=P)).then_inc(*first_loads.up())
        sp.dma_start(const[:, :], k["const"]).then_inc(*first_loads.up("x"))
        load(levels_in, k["levels"])
        for name, dst in (("onehot", onehot), ("flip", flip), ("pick", pick)):
            load(dst, k[name])
        rowload(rows_a, k["norm_mix_g"][0], 8)
        rowload(rows_a[8:16], k["norm_ffn_g"][0], 8)
        rowload(rows_a[16:24], k["norm_final_g"], 8)
        rowload(rows_a[24:32], k["final_norm_2"], 8)
        rowload(rows_a[32:76], k["conv_b"][0], 2 * FC)
        for j in range(3):
            rowload(rows_c[:, j, :], k["conv_w"][0, j], 2 * FC)
        for l in range(LAYERS):
            for name, at, n in (("ffn1_norm_2", 0, 8), ("mix_norm_2", 8, 8), ("mla_q_norm_2", 16, 2),
                                ("mla_kv_norm_2", 18, 1), ("sg_ln_2", 19, 2), ("hg_lb_logits_2", 21, 4),
                                ("hg_norm_2", 25, 2), ("ret_norm_2", 27, 2), ("ffn2_norm_2", 29, 8),
                                ("ple_norm_2", 37, 8)):
                rowload(rows_l[l * L_NROWS + at:], k[name][l], n)
        load(t5_in[0:32, :], k["t5_bias"])
        load(cur[0:4, 49:50], k["fox_b_f"].rearrange("a h -> h a"), "params")

        w = k["w_in"][0]
        for name in ("sbq", "sbk", "sbv", "mbq", "mbk", "mbv", "fxq", "fxk", "fxv", "dsq", "ixq"):
            slab(w, A_COLS[name])
        whole(w, A_COLS["dsk"])
        piece(some(w, A_COLS["ixk"], 40, 0), some(w, A_COLS["fxf"], NH, HD))

        gate_w, branch_w = k["w_gate"][0], k["w_branch"][0]
        for b in range(3):
            for c in range(DC // 2):
                slab(gate_w[b], c * 256)
                two_rows(branch_w[b], 0, c * 256, 256)
        for c in range(DC // 2):
            slab(gate_w[3], c * 256)
        for c in range(DC // 2):
            two_rows(branch_w[3], 0, c * 256, 256)

        def proj(tag, w):
            for j in range(4):
                slab(w, j * 256)

        def ffn(tag, w_gate, w_up, w_down):
            def up(phase, it, j):
                m, n, _ = UP[phase]
                for w in (w_gate, w_up):
                    whole(w, it * (m * 256) + (n * 256 + j * P))

            def down(phase, it, half):
                m, n, _ = DOWN[phase]
                two_rows(w_down, it * (2 * m) + 2 * n, half * (D // 2), D // 2)

            for j in range(2):
                up("first", 0, j)
            with Fori(Q, sp, tag, FFN_LOOPS) as it:
                for phase, behind in (("odd", "even"), ("even", "odd")):
                    for j in range(2):
                        up(phase, it, j)
                        down(behind, it, j)
            for half in range(2):
                down("last", 0, half)

        proj("out", k["w_out"][0])
        up = k["w_up"][0]
        sp.wait_ge(*Q.at("mixed_all"))
        load(pos_i[:, :].bitcast(I32), k["positions_2"].to_broadcast([P, S]), "pos")
        load(decay, k["decay"].rearrange("p (h u) -> p h u", h=NH), "decay")
        ffn("c", up[:, 0:FF], up[:, FF:2 * FF], k["w_down"][0])

        with Fori(Q, sp, "layer", LAYERS) as l:
            def at_layer(name):
                a = k[name + "_2"][bass.ds(l, 1)]
                while len(a.shape) > 2:
                    a = a.rearrange("a b c -> (a b) c") if len(a.shape) == 3 else a.rearrange("a b c d -> (a b) c d")
                return a

            ffn("f", at_layer("ffn1_w_gate"), at_layer("ffn1_w_up"), at_layer("ffn1_w_down"))
            w = at_layer("w_in")
            slab(w, B_COLS["cq"])
            whole(w, B_COLS["ckv"])
            whole(w, B_COLS["ckv"] + HD)
            sp.wait_ge(*Q.at("evac", "f", "dlast", 3))
            load(sgw, at_layer("sg_w_s").rearrange("(h t) s -> t h s", h=NH))
            load(sgb[0:NH, :], at_layer("sg_b_s"), "sg")
            for j in range(2):
                slab(w, B_COLS["hf"] + 256 * j)
            slab(w, B_COLS["hq"])
            two_rows(at_layer("mla_w_uq"), 0, 0, NH * MLA_D)
            ukv = at_layer("mla_w_ukv").rearrange("p (h c) -> p h c", h=NH)

            def keys_or_values(i):
                return (lambda slot: slot[:, 256 * i:256 * i + 256].rearrange("p (h c) -> p h c", h=NH),
                        ukv[:, :, i * HD:i * HD + HD])
            piece(keys_or_values(0), keys_or_values(1))
            slab(w, B_COLS["hq"] + 256)
            for name in (*MLA_BEHIND, "hi", "rg", "hg"):
                slab(w, B_COLS[name])
            proj("lout", at_layer("w_out"))
            ffn("g", at_layer("ffn2_w_gate"), at_layer("ffn2_w_up"), at_layer("ffn2_w_down"))
            sp.wait_ge(*Q.at("evac", "g", "dlast", 3))
            load(pin, at_layer("p").rearrange("(i q) d -> q i d", q=P), "pin")
            pg, pp = at_layer("ple_w_gate"), at_layer("ple_w_proj")
            with Fori(Q, sp, "ple", DC // 4) as it:
                for j in range(2):
                    slab(pg, it * 512 + j * 256)
                    two_rows(pp, 0, it * 512 + j * 256, 256)
        book.pieces = load_at.n

        sp.wait_ge(*Q.at("out_ready"))
        sp.dma_start(out.rearrange("(i p) d -> p i d", p=P), outrow).then_inc(*Q.up("stored"))
        sp.wait_ge(*Q.last())

    @block.gpsimd
    def _(pool):
        pool.memset(zero[:, :], 0.0).then_inc(book.sems["zero_ready"], 1)
        pool.wait_ge(book.sems["zero_ready"], 1)
        zeros = zero[:, 0:1].to_broadcast([P, PIECE])

        def split_piece(s, load_count, use_count, split_count):
            pool.wait_ge(landed[s], load_count)
            if use_count is not None:
                pool.wait_ge(book.sems["pieces_used"], use_count)
            pool.tensor_tensor(wh[:, s, :], raw[:, s, :], zeros, ALU.add).then_inc(split, 1)
            pool.wait_ge(split, split_count)
            pool.tensor_tensor(wl[:, s, :], raw[:, s, :], wh[:, s, :].bitcast(F32), ALU.subtract).then_inc(split, 1)

        for s in range(2):
            split_piece(s, 32, None, 2 * s + 1)
        with pool.Fori(0, (book.known.pieces if book.known else 4) // 2 - 1) as it:
            for s in range(2):
                split_piece(s, it * 32 + 64, it * 2 + (1 + s), it * 4 + (5 + 2 * s))

    @block.tensor
    def _(pe):
        slabs = [[], [], [], []]
        turn = [0, 0]

        def slab_start(key, ready=False, high=0):
            s = 2 * high + turn[high] % 2
            turn[high] += 1
            if not ready:
                for older, prev in slabs[s]:
                    pe.wait_ge(*T.at("evac", *older, prev=prev))
            slabs[s] = [(key, None)]
            pair_of[key] = s
            return s

        def loop(name, trips, keys, high_keys=()):
            f = Fori(T, pe, name, trips)
            for i, key in enumerate(keys):
                slabs[(turn[0] + i) % 2] = [(key, name)]
            for i, key in enumerate(high_keys):
                slabs[2 + (turn[1] + i) % 2] = [(key, name)]
            return f

        def piece_split(part):
            pe.wait_ge(split, used_at.value(T, 2, part))

        def piece_used(ins, *what):
            ins.then_inc(*used.up(*what))
            used_at.up()

        def hold():
            pe.matmul(PT[:, 0:4], ident, ident[:, 0:4], start=True, stop=True)

        def products(psum, cols, rhs, wait=True):
            last = len(rhs) - 1
            if wait:
                piece_split(1)
            for i, (xhi, xlo) in enumerate(rhs):
                pe.matmul(psum, cols(wh, i), xhi, start=(i == 0), stop=False)
                pe.matmul(psum, cols(wh, i), xlo, start=False, stop=False)
            if wait:
                piece_split(2)
            for i, (xhi, xlo) in enumerate(rhs):
                ins = pe.matmul(psum, cols(wl, i), xhi, start=False, stop=(i == last))
            return ins

        def piece_cols(c0=0, width=P, n=P):
            p = used_at.n % 2
            return lambda w, i: w[:, p, i * width + c0:i * width + c0 + n]

        def gemm_fm(key, rhs, ready=None):
            if ready is None:
                for b in range(2):
                    gemm_half(key, rhs, b)
                return
            s = slab_start(key, True)
            p = used_at.n % 2
            pe.wait_ge(split, used_at.value(T, 2, 4))
            for i, (xhi, xlo) in enumerate(rhs):
                pe.wait_ge(*T.at("xl", ready, i))
                for b in range(2):
                    c = slice(i * P, i * P + P)
                    w_hi, w_lo = wh[:, (p + b) % 2, c], wl[:, (p + b) % 2, c]
                    o = bank[2 * s + b][:, :]
                    pe.matmul(o, w_hi, xhi, start=(i == 0), stop=False)
                    pe.matmul(o, w_hi, xlo, start=False, stop=False)
                    ins = pe.matmul(o, w_lo, xhi, start=False, stop=(i == DC - 1))
                    if i == DC - 1:
                        piece_used(ins, *(("gemm", *key) if b else ()))


        def gemm_half(key, rhs, b):
            s = slab_start(key) if b == 0 else pair_of[key]
            ins = products(bank[2 * s + b][:, :], piece_cols(), rhs)
            piece_used(ins, *(("gemm", *key) if b else ()))

        def token_major(s, rhs, cols, both_parts=None):
            last = len(rhs) - 1
            for tiles in ((0, 2), (1, 3)):
                out = {i: bank[2 * s + i // 2][:, i % 2 * 256:i % 2 * 256 + 256] for i in tiles}
                for i in tiles:
                    t = slice(i * P, i * P + P)
                    for j, (xhi, xlo) in enumerate(rhs):
                        pe.matmul(out[i], xhi[:, t], cols(wh, j), start=(j == 0), stop=False)
                        pe.matmul(out[i], xlo[:, t], cols(wh, j), start=False, stop=False)
                if both_parts:
                    pe.wait_ge(*both_parts)
                    both_parts = None
                for i in tiles:
                    for j, (xhi, _) in enumerate(rhs):
                        ins = pe.matmul(out[i], xhi[:, i * P:i * P + P], cols(wl, j), start=False, stop=(j == last))
            return ins

        def gemm_tm(key, rhs, fm_key=None):
            assert used_at.n % 2 == 0
            if fm_key:
                s = slab_start(fm_key)
                for p in range(2):
                    pe.wait_ge(split, used_at.value(T, 2, 2 * p + 2))
                    ins = products(bank[2 * s + p][:, :], lambda w, i: w[:, p, i * P:i * P + P], rhs, wait=False)
                ins.then_inc(*T.up("gemm", *fm_key))
            s = slab_start(key)
            pe.wait_ge(split, used_at.value(T, 2, 3))
            ins = token_major(s, rhs, lambda w, j: w[:, :, j * P:j * P + P], (split, used_at.value(T, 2, 4)))
            used.up()
            used.up("gemm", *key)
            ins.then_inc(used.sem, 2)
            used_at.up()
            used_at.up()

        def parts(a, b, n):
            return [(a[:, i, :], b[:, i, :]) for i in range(n)]

        xk = parts(xh, xl, DC)

        def norm_part(tag, src, one, i):
            pe.wait_ge(*T.at("sq", tag, i))
            ins = pe.matmul(SC[int(tag == "kv")][:, :], ones[:, one, :], src[i], start=(i == 0),
                            stop=(i == len(src) - 1))
            if i == len(src) - 1:
                ins.then_inc(*T.up("ms", tag))

        def norm(tag, src, one):
            for i in range(len(src)):
                norm_part(tag, src, one, i)

        def norm_behind(tag, m):
            for c in ((), (0, 1), (2, 3), (4, 5, 6, 7))[m]:
                norm_part(tag, sq8, 0, c)

        def group_norm(tag, c, centred, between=lambda: None):
            if centred:
                pe.wait_ge(*T.at("gin", tag, c))
                pe.matmul(PT[:, :], C("group"), gn[:, 0, :], start=True, stop=True).then_inc(*T.up("gmean", tag, c))
                between()
            pe.wait_ge(*T.at("gsq", tag, c))
            pe.matmul(PT[:, :], C("group"), gn[:, 1, :], start=True, stop=True).then_inc(*T.up("gms", tag, c))

        def attention(tag, score, value, mode, between=None):
            def scores(u):
                hh, i = u // TT, u % TT
                if u >= 2:
                    pe.wait_ge(*T.at("score_used", tag, u - 2))
                score(SC[u % 2], hh, i).then_inc(*T.up("score", tag, u))

            scores(0)
            scores(1)
            for u in range(NH * TT):
                hh, i = u // TT, u % TT
                pe.wait_ge(*T.at("prob", tag, u))
                if u >= 1:
                    pe.wait_ge(*T.at("probT", tag, u - 1))
                p = (prob if mode == 1 else lprob)[:, u % 2, :]
                pt = (probT if mode == 1 else lprobT)[:, u % 2, :]
                for j in range(i + 1):
                    ins = pe.transpose(PT[:, j * P:j * P + P], p[:, j * P:j * P + P], ident)
                ins.then_inc(*T.up("turned", tag, u))
                if u + 2 < NH * TT:
                    scores(u + 2)
                if between:
                    between(u)
                pe.wait_ge(*T.at("probT", tag, u))
                r = hh % 2 * HD
                for j in range(i + 1):
                    ins = pe.matmul(OB[r:r + HD, i * P:i * P + P], value(hh, j), pt[:, j * P:j * P + P],
                                    start=(j == 0), stop=(j == i))
                ins.then_inc(*T.up("pv", tag, u))

        pe.wait_ge(*T.at("x"))
        for c in range(DC):
            if c >= 2:
                pe.wait_ge(*T.at("x_in", c - 2))
            for i in range(TT):
                ins = pe.transpose(SC[c % 2][:, i * P:i * P + P], xraw[:, i, c * P:c * P + P], ident)
            ins.then_inc(*T.up("x_turned", c))
        pe.wait_ge(*T.at("params"))
        pe.transpose(PT[:, 0:A_NROWS], rows_a[0:A_NROWS, :], ident[0:A_NROWS, 0:A_NROWS])
        for j in range(3):
            pe.transpose(PT[:, 128 + 44 * j:172 + 44 * j], rows_c[0:44, j, :], ident[0:44, 0:44])
        n = LAYERS * L_NROWS
        pe.transpose(PT[:, 264:264 + n], rows_l[0:n, :], ident[0:n, 0:n]).then_inc(*T.up("cols_turned"))
        pe.matmul(OB[0:8, :], t5_in[0:32, :], onehot[0:32, 0:512], start=True, stop=True)\
            .then_inc(*T.up("t5a"))
        pe.wait_ge(*T.at("cols_in"))
        pe.matmul(PT[0:8, 0:128], t5_in[0:32, :], onehot[0:32, 512:640], start=True, stop=True)\
            .then_inc(*T.up("t5b"))
        pe.wait_ge(*T.at("x_in", DC - 1))
        sq8 = [normed[:, i, :] for i in range(DC)]
        norm("mix", sq8, 0)
        gemm_fm(("sbq",), xk, "mix")
        gemm_fm(("sbk",), xk)
        gemm_tm(("sbv",), xk)

        def behind(names, key, u):
            name = names[u // 2]
            if name in ("mbv", "fxv", "hi", "zv", "rv"):
                if u % 2:
                    gemm_tm((name, *key), xk)
            else:
                gemm_half((name, *key), xk, u % 2)

        pe.wait_ge(*T.at("t5_rows"))
        pe.wait_ge(*T.at("rstd", "mix"))
        for i in range(8):
            if i >= 2:
                pe.wait_ge(*T.at("bias", i - 2))
            pe.matmul(SC[i % 2][:, :], flip, t5_rows[:, i, :], start=True, stop=True).then_inc(*T.up("flip", i))

        def heads(a, hh):
            return a[hh % 2 * HD:hh % 2 * HD + HD, hh // 2, :]

        def diagonal(o, i, mask):
            return pe.matmul(o[:, i * P:i * P + P], ident, C(mask), start=False, stop=True)

        def qk(o, q, kk, i):
            pe.matmul(o[:, 0:(i + 1) * P], q[:, i * P:i * P + P], kk[:, 0:(i + 1) * P], start=True, stop=False)

        def score_sb(o, hh, i):
            qk(o, heads(sbq, hh), heads(sbk, hh), i)
            return diagonal(o, i, "strict")

        def score_mb(o, hh, i):
            qk(o, heads(mbq, hh), heads(mbk, hh), i)
            return diagonal(o, i, "causal")

        def score_fx(o, hh, i):
            qk(o, heads(fxq, hh), heads(fxk, hh), i)
            one = pick[0:NH, :].rearrange("p (g h q) -> p g h q", g=2, h=NH)
            for j in range(i + 1):
                pe.matmul(o[:, j * P:j * P + P], cum[0:NH, i * P:i * P + P], one[:, 0, hh, :], start=False, stop=False)
            pe.matmul(o[:, 0:(i + 1) * P], one[:, 1, hh, :], cum[0:NH, 0:(i + 1) * P], start=False, stop=False)
            return diagonal(o, i, "causal")

        def score_ds(o, hh, i):
            r = slice(hh % 2 * HD, hh % 2 * HD + HD)
            pe.matmul(o[:, 0:(i + 1) * P], dsq[r, hh // 2, i * P:i * P + P], dsk[r, 0:(i + 1) * P],
                      start=True, stop=False)
            if i == 0:
                return diagonal(o, i, "causal")
            return pe.matmul(o[:, 0:(i + 1) * P], ident, sel[:, i - 1, 0:(i + 1) * P], start=False, stop=True)

        pe.wait_ge(*T.at("bias", 7))
        pe.wait_ge(*T.at("evac", "sbv"))
        pe.wait_ge(*T.at("t5_kept"))
        attention("sb", score_sb, lambda hh, j: sbv[:, j, hh * HD:hh * HD + HD], 1,
                  lambda u: behind(SB_BEHIND, (), u))
        gemm_tm(("dst",), xk, ("dsf",))

        def gate_piece(b, g, n):
            if n < 2:
                gemm_half(("gate", b, g), xk, n)
                return
            if g == 0:
                pe.wait_ge(*T.at("branch_split", b))
            at = b % 2 * 2
            branch(("branch", b, g), parts(op_hi[:, at:, :], op_lo[:, at:, :], 2))

        def branch(key, rhs2):
            s = slab_start(key)
            for c in range(2):
                ins = products(bank[2 * s + c][:, :], piece_cols(c * P, 256), rhs2)
            piece_used(ins, "gemm", *key)

        def gates_behind(b):
            return lambda u: gate_piece(b, u // 4, u % 4) if u % 4 < 3 else None

        pe.wait_ge(*T.at("o", "sb", 1))
        pe.wait_ge(*T.at("evac", "dst"))
        pe.wait_ge(*T.at("evac", "ix"))
        attention("mb", score_mb, lambda hh, j: mbv[:, j, hh * HD:hh * HD + HD], 1, gates_behind(0))
        pe.wait_ge(*T.at("o", "mb", 1))
        n = 0
        for i in range(1, TT):
            for hh in range(8):
                if n >= 2:
                    pe.wait_ge(*T.at("ix_used", n - 2))
                r = slice(hh % 4 * 32, hh % 4 * 32 + 32)
                pe.matmul(SC[n % 2][:, 0:(i + 1) * P], ixq[r, hh // 4, i * P:i * P + P], ixk[r, 0:(i + 1) * P],
                          start=True, stop=True).then_inc(*T.up("ix_score", n))
                n += 1
        pe.wait_ge(*T.at("cum"))
        for u in (n - 2, n - 1):
            pe.wait_ge(*T.at("ix_used", u))
        attention("fx", score_fx, lambda hh, j: fxv[:, j, hh * HD:hh * HD + HD], 1, gates_behind(1))
        pe.wait_ge(*T.at("o", "fx", 1))
        def late_behind(u):
            for n in range(20):
                if unit_of(n) == u:
                    gate_piece(*((2, n // 3, n % 3) if n < 12 else (3, (n - 12) // 2, n % 2)))

        pe.wait_ge(*T.at("sel", TT - 2))
        attention("ds", score_ds, lambda hh, j: dsv[:, j, 0:HD], 1,
                  late_behind)
        pe.wait_ge(*T.at("o", "ds", 1))

        for g in range(DC // 2):
            gate_piece(3, g, 2)

        def proj(tag, then):
            for j in range(4):
                gemm_fm((tag, j), xk, tag if j == 0 else None)
                norm_behind(then, j)

        def ffn(tag, after, then):
            def up(phase, j):
                gemm_fm((tag, phase, j), xk, after if (phase, j) == ("first", 0) else None)

            def down(phase, half):
                at = DOWN[phase][2]
                rhs = parts(op_hi[:, at:, :], op_lo[:, at:, :], 2)
                for m in (2 * half, 2 * half + 1):
                    s = slab_start((tag, "d" + phase, m), (phase, m) == ("last", 0), phase != "last")
                    for b in range(2):
                        ins = products(bank[2 * s + b][:, :], piece_cols((m % 2 * 2 + b) * P, 512), rhs)
                    if m % 2:
                        piece_used(ins, "gemm", tag, "d" + phase, m)
                    else:
                        ins.then_inc(*T.up("gemm", tag, "d" + phase, m))
                    if phase == "last":
                        norm_behind(then, m)

            for j in range(2):
                up("first", j)
            pe.wait_ge(*T.at("evac", tag, "first", 1))
            hold()
            with loop(tag, FFN_LOOPS, [(tag, "even", 0), (tag, "even", 1)], [(tag, "dodd", 2), (tag, "dodd", 3)]):
                for phase, behind in (("odd", "even"), ("even", "odd")):
                    for j in range(2):
                        up(phase, j)
                        down(behind, j)
            pe.wait_ge(*T.at("hidden", tag, "even", 1))
            for half in range(2):
                down("last", half)

        proj("out", "ffn")
        ffn("c", "ffn", "fin1")

        with Fori(T, pe, "layer", LAYERS):
            norm("f1", sq8, 0)
            ffn("f", "f1", "lm")
            gemm_fm(("cq",), xk, "lm")
            gemm_fm(("ckv",), xk)
            gemm_fm(("hf", 0), xk)
            norm("q", [lprob[:, i, :] for i in range(2)], 1)
            norm("kv", [lprobT[:, 0, :]], 2)
            gemm_fm(("hf", 1), xk)
            gemm_fm(("hq", 0), xk)
            pe.wait_ge(*T.at("xl", "q", 1))
            hold()
            for j in range(2):
                s = slab_start(("uq", j))
                for b in range(2):
                    ins = products(bank[2 * s + b][0:MLA_D, :], piece_cols((2 * j + b) * MLA_D, NH * MLA_D, MLA_D),
                                   parts(op_hi, op_lo, 2))
                if j:
                    piece_used(ins, "gemm", "uq", j)
                else:
                    ins.then_inc(*T.up("gemm", "uq", j))
            pe.wait_ge(*T.at("xl", "kv", 0))
            hold()
            kv_in = parts(op_hi[:, 2:, :], op_lo[:, 2:, :], 1)
            s = slab_start(("uk",))
            for b in range(2):
                ins = products(bank[2 * s + b][:, :], piece_cols(b * P, 512), kv_in)
            ins.then_inc(*T.up("gemm", "uk"))
            s = slab_start(("uv",))
            ins = token_major(s, kv_in, piece_cols(256, 512, 256))
            piece_used(ins, "gemm", "uv")
            swap32 = C("swap32", slice(64, 96))
            for n in range(NH + 1):
                src = qh[64:96, n, :] if n < NH else kh[64:96, 0, :]
                if n == 0:
                    pe.wait_ge(*T.at("rstd", "kv"))
                    pe.wait_ge(*T.at("evac", "uq", 1))
                if n >= 2:
                    pe.wait_ge(*T.at("rot_used", n - 2))
                pe.matmul(SC[n % 2][:, :], swap32, src, start=True, stop=True).then_inc(*T.up("swapped", n))
                if n == 1:
                    gemm_fm(("hq", 1), xk)
            def score_mla(o, hh, i):
                qk(o, qh[0:MLA_D, hh, :], kh[0:MLA_D, hh, :], i)
                return diagonal(o, i, "causal")

            pe.wait_ge(*T.at("evac", "uv"))
            pe.wait_ge(*T.at("k_rot"))
            attention("ml", score_mla, lambda hh, j: mv[:, j, hh * HD:hh * HD + HD], 2,
                      lambda u: behind(MLA_BEHIND, (0,), u) if u < 2 * len(MLA_BEHIND) else None)
            pe.wait_ge(*T.at("o", "ml", 1))
            pe.wait_ge(*T.at("sg"))
            for i in range(NH):
                ins = pe.transpose(PT[:, i * P:i * P + P], sgw[:, i, :], ident)
            ins.then_inc(*T.up("sgw_turned"))
            hs = C("headsel", slice(0, NH)).rearrange("p (c q) -> p c q", c=2)
            for c in range(2):
                ins = pe.matmul(OB[:, c * P:c * P + P], hs[:, c, :], sgb[0:NH, :], start=True, stop=True)
            ins.then_inc(*T.up("sgb_spread"))
            gemm_tm(("hi", 0), xk)
            pe.wait_ge(*T.at("sgwT"))
            pe.wait_ge(*T.at("sgbb"))
            for c in range(2):
                dst = PT if c == 0 else OB
                for hh in (2 * c, 2 * c + 1):
                    r = hh % 2 * HD
                    for i in range(TT):
                        ins = pe.matmul(dst[r:r + HD, i * P:i * P + P], zv[:, i, hh * HD:hh * HD + HD],
                                        sgwT[:, hh, :], start=True, stop=True)
                ins.then_inc(*T.up("sg_mixed", c))
            pe.wait_ge(*T.at("sg_out", 1))
            for n in range(4):
                src = (rq, rk)[n // 2][:, n % 2, :]
                if n >= 2:
                    pe.wait_ge(*T.at("ret_rot", n - 2))
                pe.matmul(SC[n % 2][:, :], C("swap"), src, start=True, stop=True).then_inc(*T.up("ret_swap", n))
                if n % 2:
                    gemm_half(("rg", 0), xk, n // 2)
            pe.wait_ge(*T.at("ret_rot", 3))

            def ret_scores(u):
                hh, j = u // TT, u % TT
                if u >= 2:
                    pe.wait_ge(*T.at("ret_w", u - 2))
                pe.matmul(SC[u % 2][:, 0:S - j * P], heads(rk, hh)[:, j * P:j * P + P], heads(rq, hh)[:, j * P:S],
                          start=True, stop=True).then_inc(*T.up("ret_score", u))

            ret_scores(0)
            for u in range(NH * TT):
                hh, j = u // TT, u % TT
                if u + 1 < NH * TT:
                    ret_scores(u + 1)
                pe.wait_ge(*T.at("ret_w", u))
                if u == 2 * TT:
                    pe.wait_ge(*T.at("gin", "r", 0))
                r = hh % 2 * HD
                pe.matmul(OB[r:r + HD, j * P:S], rv[:, j, hh * HD:hh * HD + HD], lprob[:, u % 2, 0:S - j * P],
                          start=(j == 0), stop=(j == TT - 1)).then_inc(*T.up("ret_pv", u))
                if u in (2 * TT - 1, 4 * TT - 1):
                    c = u // (2 * TT)
                    group_norm("r", c, True, lambda: gemm_half(("hg", 0), xk, c))
            n = 0
            for hh in range(NH):
                r = hh % 2 * HD
                for lv in range(len(LEVELS) + 1):
                    if lv < len(LEVELS):
                        pe.wait_ge(*T.at("lvl_k", hh, lv))
                        kk, qq = hK[:, lv % 2, :], hQ[:, lv % 2, :]
                    else:
                        pe.wait_ge(*T.at("lvl_used", n - 2))
                        kk, qq = hk[:, hh, :], hq[:, hh, :]
                    for i in range(TT):
                        ins = pe.matmul(SC[n % 2][:, i * P:i * P + P], kk[:, i * P:i * P + P], qq[:, i * P:i * P + P],
                                        start=True, stop=True)
                    ins.then_inc(*T.up("lvl", n))
                    n += 1
                pe.wait_ge(*T.at(*(("gout", "h", 0) if hh == 2 else ("kv3", hh))))
                kvs = kv3.rearrange("p (c t) -> p c t", c=3)
                blocks = [(1, kd[:, 0:P]), (2, kd[:, P:2 * P]), (3, kd[:, 2 * P:3 * P]), (2, kvs[:, 0, :]),
                          (3, kvs[:, 1, :]), (3, kvs[:, 2, :])]
                for b, (i, kk) in enumerate(blocks):
                    if b == 4:
                        pe.wait_ge(*T.at("offs", hh, 0))
                    ins = pe.matmul(PT[:, b % 4 * P:b % 4 * P + P], kk, qd[:, i * P:i * P + P], start=True, stop=True)
                    if b in (3, 5):
                        ins.then_inc(*T.up("off", hh, b // 4))
                where = {(1, 0): 0, (2, 1): 1, (3, 2): 2, (2, 0): 3, (3, 1): 4, (3, 0): 5}
                pe.wait_ge(*T.at("offs", hh, 1))
                pe.wait_ge(*T.at("lvl_used", n - 1))
                for i in range(TT):
                    for j in range(i + 1):
                        w = scT[:, i * P:i * P + P] if i == j else off[:, where[i, j] * P:where[i, j] * P + P]
                        ins = pe.matmul(OB[r:r + HD, i * P:i * P + P], hi[:, j, hh * HD:hh * HD + HD], w,
                                        start=(j == 0), stop=(j == i))
                ins.then_inc(*T.up("hg_pv", hh))
                if hh % 2 == 1:
                    group_norm("h", hh // 2, False)
            proj("lout", "f2")
            ffn("g", "f2", "pl")
            pe.wait_ge(*T.at("rstd", "pl"))
            pe.wait_ge(*T.at("pin"))
            for c in range(2):
                for i in range(TT):
                    ins = pe.transpose(SC[c][:, i * P:i * P + P], pin[:, i, c * P:c * P + P], ident)
                ins.then_inc(*T.up("p_turned", c))
            pe.wait_ge(*T.at("p_split"))
            hold()
            with loop("ple", DC // 4, [("gate", "p", 1), ("branch", "p", 1)]):
                for j in range(2):
                    gemm_fm(("gate", "p", j), xk)
                    branch(("branch", "p", j), parts(op_hi, op_lo, 2))

        norm("fin", sq8, 0)
        pe.wait_ge(*T.at("rstd", "fin"))
        for c in range(DC):
            pe.wait_ge(*T.at("xn", "fin", c))
            if c >= 2:
                pe.wait_ge(*T.at("out_row", c - 2))
            for i in range(TT):
                ins = pe.transpose(SC[c % 2][:, i * P:i * P + P], normed[:, c, i * P:i * P + P], ident)
            ins.then_inc(*T.up("out_turned", c))

    @block.scalar
    def _(act):
        def copy_pair(key, dst, scale=1.0, f=ACT.Copy):
            s = evac_start(key)
            for b in range(2):
                ins = act.activation(dst[b], bank[2 * s + b][:, :], f, scale=scale)
                ins.then_inc(*A.up(*(("evac", *key) if b == 1 else ())))

        def evac_start(key):
            act.wait_ge(*A.at("gemm", *key))
            return pair_of[key]

        def copy_tm(key, dst, f=ACT.Copy):
            copy_pair(key, [dst[:, 2 * b:2 * b + 2, :].rearrange("p i d -> p (i d)") for b in range(2)], f=f)

        def first_parts(tag, src, dst, ready="xn"):
            for i, a in enumerate(src):
                if ready:
                    act.wait_ge(*A.at(*((ready, i) if ready == "mixed" else (ready, tag, i))))
                act.activation(dst[:, i, :], a, ACT.Copy).then_inc(*A.up("xh", tag, i))

        def norm(tag, src, tmp, dst=None, ready=None):
            for i, a in enumerate(src):
                if ready:
                    act.wait_ge(*A.at(*ready, i))
                act.activation(tmp[i], a, ACT.Square).then_inc(*A.up("sq", tag, i))
            root(SC[0][:, :], "ms", tag)
            if dst is not None:
                first_parts(tag, tmp, dst)

        def root(psum, *what):
            act.wait_ge(*A.at(*what))
            act.activation(nrm[:, 0, :], psum, ACT.Ln, bias=eps[:, 0:1]).then_inc(*A.up())
            act.wait_ge(*A.last())
            act.activation(nrm[:, 1, :], nrm[:, 0, :], ACT.Exp, scale=-0.5).then_inc(*A.up("rt", *what[1:]))

        hk8 = [h[:, i, :] for i in range(DC)]
        n8 = [normed[:, i, :] for i in range(DC)]

        def two(a):
            return [a[:, 0, :], a[:, 1, :]]

        def attention(tag, mode, biased, between=None, b=None):
            pr, pt = (prob, probT) if mode == 1 else (lprob, lprobT)

            def expo(u):
                n = (u % TT + 1) * P
                act.wait_ge(*A.at("negmax", tag, u))
                src = pr[:, u % 2, 0:n] if biased else SC[u % 2][:, 0:n]
                if not biased and u >= 2:
                    act.wait_ge(*A.at("turned", tag, u - 2))
                act.activation(pr[:, u % 2, 0:n], src, ACT.Exp, bias=stat[:, u % 2, 1:2],
                               accum_out=stat[:, u % 2, 2:3])\
                    .then_inc(*A.up(*(("expo", tag, u) if biased else ("score_used", tag, u))))

            def copy_turned(u):
                n = (u % TT + 1) * P
                act.wait_ge(*A.at("turned", tag, u))
                act.activation(pt[:, u % 2, 0:n], PT[:, 0:n], ACT.Copy).then_inc(*A.up("probT", tag, u))

            expo(0)
            for u in range(NH * TT):
                if u + 1 < NH * TT:
                    expo(u + 1)
                copy_turned(u)
                if between:
                    between(u)
                if u % (2 * TT) == 2 * TT - 1:
                    out_half(tag, u, b)

        def out_half(tag, u, b):
            c = u // (2 * TT)
            act.wait_ge(*A.at("pv", tag, u))
            if b is None:
                act.activation(cq[:, c, :], OB[:, :], ACT.Copy).then_inc(*A.up("o", tag, c))
                return
            if b and c == 0:
                act.wait_ge(*A.at("branch_split", b - 1))
                if b >= 2:
                    act.wait_ge(*A.at("evac", "branch", b - 2, DC // 2 - 1))
            act.activation(attn[:, c, :], OB[:, :], ACT.Copy).then_inc(*A.up("o", tag, c))
            act.wait_ge(*A.last())
            act.activation(op_hi[:, b % 2 * 2 + c, :], attn[:, c, :], ACT.Copy).then_inc(*A.up("branch_first", b, c))

        def gate_on(b, g, dst):
            s = evac_start(("gate", b, g))
            if b < 3 and 4 * b + g >= 2:
                act.wait_ge(*A.at("evac", "branch", *divmod(4 * b + g - 2, DC // 2)))
            for c in range(2):
                act.activation(dst[:, c, :], bank[2 * s + c][:, :], ACT.Sigmoid)\
                    .then_inc(*A.up(*(("evac", "gate", b, g) if c else ())))

        def gates_behind(b):
            def between(u):
                if u % 4 == 2:
                    gate_on(b, u // 4, gates[:, u // 4 % 2 * 2:, :])
            return between

        def stick_breaking():
            def soft3(u):
                n = (u % TT + 1) * P
                a = soft[:, u % 2, 0:n]
                act.wait_ge(*A.at("score", "sb", u))
                if u >= 2:
                    act.wait_ge(*A.at("score_used", "sb", u - 2))
                act.activation(a, SC[u % 2][:, 0:n], ACT.Abs).then_inc(*A.up())
                act.wait_ge(*A.last())
                act.activation(a, a, ACT.Exp, scale=-1.0).then_inc(*A.up())
                act.wait_ge(*A.last())
                act.activation(a, a, ACT.Ln, bias=1.0).then_inc(*A.up("soft", u))

            soft3(0)
            for u in range(NH * TT):
                n = (u % TT + 1) * P
                if u + 1 < NH * TT:
                    soft3(u + 1)
                act.wait_ge(*A.at("score_used", "sb", u))
                act.activation(prob[:, u % 2, 0:n], prob[:, u % 2, 0:n], ACT.Exp).then_inc(*A.up("prob", "sb", u))
                act.wait_ge(*A.at("turned", "sb", u))
                act.activation(probT[:, u % 2, 0:n], PT[:, 0:n], ACT.Copy).then_inc(*A.up("probT", "sb", u))
                if u % (2 * TT) == 2 * TT - 1:
                    out_half("sb", u, 0)

        for c in range(DC):
            act.wait_ge(*A.at("x_turned", c))
            act.activation(h[:, c, :], SC[c % 2][:, :], ACT.Copy).then_inc(*A.up("x_in", c))
        act.wait_ge(*A.at("cols_turned"))
        n = LAYERS * L_NROWS
        act.activation(pcol[:, 0:A_NROWS], PT[:, 0:A_NROWS], ACT.Copy).then_inc(*A.up())
        act.activation(convw.rearrange("p j c -> p (j c)"), PT[:, 128:128 + 6 * FC], ACT.Copy).then_inc(*A.up())
        act.activation(lcol[:, :], PT[:, 264:264 + n], ACT.Copy).then_inc(*A.up("cols_in"))
        act.wait_ge(*A.at("lb_in"))
        act.activation(nrm[:, 2, 0:8], nrm[:, 2, 0:8], ACT.Exp).then_inc(*A.up("lb_exp"))
        for i, a in enumerate(hk8):
            act.activation(n8[i], a, ACT.Square).then_inc(*A.up("sq", "mix", i))
        act.wait_ge(*A.at("t5a"))
        act.activation(t5_rev[0:8, 0:512], OB[0:8, :], ACT.Copy).then_inc(*A.up())
        act.wait_ge(*A.at("t5b"))
        act.activation(t5_rev[0:8, 512:640], PT[0:8, 0:128], ACT.Copy).then_inc(*A.up("t5_kept"))
        act.wait_ge(*A.last())
        act.dma_start(scratch, t5_rev[0:8, :]).then_inc(*spills.up("t5_out"))
        root(SC[0][:, :], "ms", "mix")
        first_parts("mix", n8, xh)
        act.wait_ge(*A.at("t5_out"))
        toeplitz = bass.AP(tensor=scratch.tensor, offset=0, ap=[[1, P], [640, 8], [1, 512]])
        act.dma_start(t5_rows, toeplitz).then_inc(*spills.up("t5_rows"))
        q8 = HD ** -0.5
        copy_pair(("sbq",), two(sbq), q8)
        copy_pair(("sbk",), two(sbk))
        copy_tm(("sbv",), sbv)
        for i in range(8):
            act.wait_ge(*A.at("flip", i))
            act.activation(bias[:, i, :], SC[i % 2][:, :], ACT.Copy).then_inc(*A.up("bias", i))
        stick_breaking()
        s = evac_start(("dsf",))
        for a in range(2):
            act.activation(dsk[a * HD:a * HD + HD, :], bank[2 * s][0:HD, :], ACT.Copy).then_inc(*A.up())
        for a in range(4):
            act.activation(ixk[32 * a:32 * a + 32, :], bank[2 * s + 1][0:32, :], ACT.Copy).then_inc(*A.up())
        act.activation(zlog[0:NH, 0:S], bank[2 * s + 1][HD:HD + NH, :], ACT.Copy).then_inc(*A.up("evac", "dsf"))
        s = evac_start(("dst",))
        for b in range(2):
            src = bank[2 * s + b][:, :].rearrange("p (i d) -> p i d", i=2)
            dst = dsv[:, 2 * b:2 * b + 2, :]
            act.activation(dst[:, :, 0:HD], src[:, :, HD:P], ACT.Copy).then_inc(*A.up())
            act.activation(dst[:, :, HD:], src[:, :, P + 32:P + 40], ACT.Copy)\
                .then_inc(*A.up(*(("evac", "dst") if b else ())))
        act.wait_ge(*A.at("zlog"))
        a = soft[0:NH, 0, :]
        act.activation(a, zlog[0:NH, 0:S], ACT.Abs).then_inc(*A.up())
        act.wait_ge(*A.last())
        act.activation(a, a, ACT.Exp, scale=-1.0).then_inc(*A.up())
        act.wait_ge(*A.last())
        act.activation(a, a, ACT.Ln, bias=1.0).then_inc(*A.up("zsoft"))
        act.wait_ge(*A.at("cum"))
        attention("mb", 1, True, gates_behind(0), 1)
        n = 0
        for i in range(1, TT):
            for hh in range(8):
                act.wait_ge(*A.at("ix_score", n))
                if n >= 2:
                    act.wait_ge(*A.at("ix_added", n - 2))
                act.activation(soft[:, n % 2, 0:(i + 1) * P], SC[n % 2][:, 0:(i + 1) * P], ACT.Relu)\
                    .then_inc(*A.up("ix_used", n))
                n += 1
        attention("fx", 1, False, gates_behind(1), 2)

        def late_behind(u):
            for g in range(DC // 2):
                if unit_of(3 * g + 1) + 1 == u:
                    gate_on(2, g, gates[:, g % 2 * 2:, :])
                if unit_of(13 + 2 * g) + 1 == u:
                    gate_on(3, g, late_gates[:, 2 * g:, :])

        attention("ds", 1, True, late_behind, 3)
        late_behind(NH * TT)

        def ffn(tag):
            def up(phase):
                at = UP[phase][2]
                for j in range(2):
                    s = evac_start((tag, phase, j))
                    act.activation(silu[:, j, :], bank[2 * s][:, :], ACT.Silu).then_inc(*A.up("silu", tag, phase, j))
                    act.wait_ge(*A.at("evac", tag, phase, j))
                    act.activation(op_hi[:, at + j, :], hid[:, j, :], ACT.Copy).then_inc(*A.up("hh", tag, phase, j))

            up("first")
            with Fori(A, act, tag, FFN_LOOPS):
                up("odd")
                up("even")

        def conv_ffn():
            def up(phase):
                at = UP[phase][2]
                for j in range(2):
                    s = evac_start(("c", phase, j))
                    act.activation(padded[:, 2 * j, 2:514], bank[2 * s][:, :], ACT.Copy).then_inc(*A.up())
                    act.activation(padded[:, 2 * j + 1, 2:514], bank[2 * s + 1][:, :], ACT.Copy)\
                        .then_inc(*A.up("evac", "c", phase, j))
                    act.wait_ge(*A.at("conv_g", phase, j))
                    act.activation(silu[:, j, :], conv[:, 2 * j, :], ACT.Gelu).then_inc(*A.up("gelu", phase, j))
                    act.wait_ge(*A.at("hid", phase, j))
                    act.activation(op_hi[:, at + j, :], hid[:, j, :], ACT.Copy).then_inc(*A.up("hh", "c", phase, j))

            up("first")
            with Fori(A, act, "c", FFN_LOOPS):
                up("odd")
                up("even")

        def sincos():
            for n in range(4):
                act.wait_ge(*A.at("angle", n))
                act.activation(rope[:, n, :], rtmp[:, n, :], ACT.Sin).then_inc(*A.up("sin", n))

        first_parts("out", [mixed[:, i, :] for i in range(DC)], xh, "mixed")
        norm("ffn", hk8, n8, xh, ("added", "out"))
        sincos()
        act.wait_ge(*A.at("pad_zero"))
        conv_ffn()
        norm("fin1", hk8, n8, None, ("added", "c"))

        with Fori(A, act, "layer", LAYERS):
            act.wait_ge(*A.at("xn", "fin1", DC - 1))
            act.wait_ge(*A.at("evac", "branch", "p", 1, prev="layer"))
            norm("f1", hk8, n8, xh)
            ffn("f")
            norm("lm", hk8, n8, xh, ("added", "f"))
            copy_pair(("cq",), two(cq))
            s = evac_start(("ckv",))
            act.activation(ckv, bank[2 * s][:, :], ACT.Copy).then_inc(*A.up())
            act.activation(kh[64:96, 0, :], bank[2 * s + 1][64:96, :], ACT.Copy).then_inc(*A.up("evac", "ckv"))
            def squares(tag, src, tmp):
                for i, a in enumerate(src):
                    act.activation(tmp[i], a, ACT.Square).then_inc(*A.up("sq", tag, i))

            act.wait_ge(*A.last())
            squares("q", two(cq), two(lprob))
            squares("kv", [ckv], [lprobT[:, 0, :]])
            copy_pair(("hf", 0), [hS[:, i, :] for i in (0, 1)], f=ACT.Sigmoid)
            root(SC[0][:, :], "ms", "q")
            first_parts("q", two(cq), op_hi)
            root(SC[1][:, :], "ms", "kv")
            first_parts("kv", [ckv], op_hi[:, 2:, :])
            copy_pair(("hf", 1), [hS[:, i, :] for i in (2, 3)], f=ACT.Sigmoid)
            copy_pair(("hq", 0), [hq[:, i, :] for i in (0, 1)])
            for j in range(2):
                s = evac_start(("uq", j))
                for b in range(2):
                    ins = act.activation(qh[0:MLA_D, 2 * j + b, :], bank[2 * s + b][0:MLA_D, :], ACT.Copy,
                                         scale=MLA_D ** -0.5)
                    ins.then_inc(*A.up(*(("evac", "uq", j) if b else ())))
            s = evac_start(("uk",))
            for hh in range(NH):
                ins = act.activation(kh[0:HD, hh, :], bank[2 * s + hh // 2][hh % 2 * HD:hh % 2 * HD + HD, :], ACT.Copy)
                ins.then_inc(*A.up(*(("evac", "uk") if hh == 3 else ())))
            copy_tm(("uv",), mv)
            copy_pair(("hq", 1), [hq[:, i, :] for i in (2, 3)])

            def layer_out(name):
                if name in ("hi", "zv", "rv"):
                    copy_tm((name, 0), dict(hi=hi, zv=zv, rv=rv)[name], ACT.Gelu if name == "zv" else ACT.Copy)
                else:
                    dst, f, scale = dict(hg=(hgate, ACT.Silu, 1.0), zu=(zu, ACT.Gelu, 1.0), rq=(rq, ACT.Copy, 1.0),
                                         rk=(rk, ACT.Copy, q8), rg=(rgate, ACT.Silu, 1.0))[name]
                    copy_pair((name, 0), two(dst), scale, f)

            attention("ml", 2, False,
                      lambda u: layer_out(MLA_BEHIND[u // 2 - 1]) if u in range(2, 12, 2) else None)
            act.wait_ge(*A.at("sgvar"))
            act.activation(sgst[:, :, 3], sgst[:, :, 2], ACT.Sqrt).then_inc(*A.up("sgroot"))
            act.wait_ge(*A.at("sgb_spread"))
            act.activation(sgbb.rearrange("p c t -> p (c t)"), OB[:, 0:2 * P], ACT.Copy).then_inc(*A.up("sgbb"))
            layer_out("hi")
            layer_out("rg")
            for hh in range(NH):
                act.wait_ge(*A.at("forget", hh))
                act.activation(hS[:, hh, :], hS[:, hh, :], ACT.Ln).then_inc(*A.up("logf", hh))

            def group_in(tag, c, last_pv, centred, later=False):
                act.wait_ge(*A.at(*last_pv))
                act.activation(gn[:, 0, :], OB[:, :], ACT.Copy).then_inc(*A.up("gin", tag, c))
                act.wait_ge(*(A.at("gcentred", tag, c) if centred else A.last()))
                act.activation(gn[:, 1, :], gn[:, 0, :], ACT.Square).then_inc(*A.up("gsq", tag, c))
                if not later:
                    root(PT[:, :], "gms", tag, c)

            for c in range(2):
                if c:
                    act.wait_ge(*A.at("gout", "r", c - 1))
                group_in("r", c, ("ret_pv", 2 * TT * (c + 1) - 1), True)
            layer_out("hg")
            for hh in range(NH):
                act.wait_ge(*A.at("tail", hh))
                act.activation(hE[:, 0, :], hE[:, 0, :], ACT.Exp).then_inc(*A.up())
                act.activation(hE[:, 1, :], hS[:, hh, :], ACT.Exp).then_inc(*A.up())
                ends = hS[:, hh, :].rearrange("p (n m) -> p n m", n=TT)[:, :, P - 1]
                act.activation(dend, ends, ACT.Exp).then_inc(*A.up("head_exp", hh))
                for lv in range(len(LEVELS)):
                    act.wait_ge(*A.at("lvl_d", hh, lv))
                    act.activation(hE[:, lv % 2, :], hE[:, lv % 2, :], ACT.Exp).then_inc(*A.up("lvl_e", hh, lv))
                    if (hh, lv) == (2, 2):
                        root(PT[:, :], "gms", "h", 0)
                act.wait_ge(*A.at("off", hh, 0))
                act.activation(off[:, 0:512], PT[:, :], ACT.Copy).then_inc(*A.up("offs", hh, 0))
                act.wait_ge(*A.at("off", hh, 1))
                act.activation(off[:, 512:768], PT[:, 0:256], ACT.Copy).then_inc(*A.up("offs", hh, 1))
                if hh % 2:
                    if hh == 3:
                        act.wait_ge(*A.at("gout", "r", 1))
                        first_parts("lout", [a[:, c, :] for a in (cq, zu) for c in range(2)], xh, None)
                        for c in range(2):
                            act.activation(xh[:, 6 + c, :], rgate[:, c, :], ACT.Copy)\
                                .then_inc(*A.up("xh", "lout", 6 + c))
                        act.wait_ge(*A.at("gout", "h", 0))
                    group_in("h", hh // 2, ("hg_pv", hh), False, hh == 1)
            for c in range(2):
                act.wait_ge(*A.at("gout", "h", c))
                act.activation(xh[:, 4 + c, :], hgate[:, c, :], ACT.Copy).then_inc(*A.up("xh", "lout", 4 + c))
            norm("f2", hk8, n8, xh, ("added", "lout"))
            ffn("g")
            norm("pl", hk8, n8, xh, ("added", "g"))
            for c in range(2):
                act.wait_ge(*A.at("p_turned", c))
                act.activation(op_hi[:, c, :], SC[c][:, :], ACT.Copy).then_inc(*A.up("p_first", c))
            with Fori(A, act, "ple", DC // 4):
                for j in range(2):
                    s = evac_start(("gate", "p", j))
                    act.wait_ge(*A.at("evac", "branch", "p", j, prev="ple"))
                    for c in range(2):
                        act.activation(sg8[:, 2 * j + c, :], bank[2 * s + c][:, :], ACT.Sigmoid)\
                            .then_inc(*A.up(*(("evac", "gate", "p", j) if c else ())))

        act.wait_ge(*A.at("evac", "branch", "p", 1))
        norm("fin", hk8, n8)
        for c in range(DC):
            act.wait_ge(*A.at("out_turned", c))
            dst = outrow[:, :, c * P:c * P + P]
            act.activation(dst, SC[c % 2][:, :].rearrange("p (i d) -> p i d", i=TT), ACT.Copy)\
                .then_inc(*A.up("out_row", c))
        act.wait_ge(*A.last())
        act.activation(stat[:, 0, 3:4], outrow[:, 0, 0:1], ACT.Copy).then_inc(*A.up("out_ready"))

    @block.vector
    def _(v):
        def evac_start(key):
            v.wait_ge(*V.at("gemm", *key))
            return pair_of[key]

        def last():
            v.wait_ge(*V.last())

        def tt(out, a, b, op, *what):
            v.tensor_tensor(out, a, b, op).then_inc(*V.up(*what))

        def ts(out, a, s1, s2, op0, op1, *what):
            if op1 is None:
                v.tensor_scalar(out, a, s1, None, op0).then_inc(*V.up(*what))
            else:
                v.tensor_scalar(out, a, s1, s2, op0, op1).then_inc(*V.up(*what))

        def stt(out, a, s, b, op0, op1, *what):
            v.scalar_tensor_tensor(out=out, in0=a, scalar=s, in1=b, op0=op0, op1=op1).then_inc(*V.up(*what))

        def newton(x, y, t, *what):
            v.reciprocal(y, y).then_inc(*V.up())
            last()
            tt(t, x, y, ALU.mult)
            last()
            tt(t, t, y, ALU.mult)
            last()
            ts(t, t, -0.5, 1.5, ALU.mult, ALU.add)
            last()
            tt(y, y, t, ALU.mult, *what)
            last()

        def rstd(psum, ms, tag):
            x, y, t = psum, nrm[:, 1, :], nrm[:, 2, :]
            v.wait_ge(*V.at("rt", *tag))
            last()
            stt(t, x, EPS, y, ALU.add, ALU.mult)
            last()
            tt(t, t, y, ALU.mult)
            last()
            stt(t, t, -0.5, y, ALU.mult, ALU.mult)
            last()
            stt(y, y, 1.5, t, ALU.mult, ALU.add, "rstd", *tag)
            last()

        def rest(tag, i, src, first, dst):
            v.wait_ge(*V.at("xh", tag, i))
            tt(dst, src, first.bitcast(F32), ALU.subtract, "xl", tag, i)

        def norm(tag, src, dst, g, first=None, second=None):
            rstd(SC[int(tag == "kv")][:, :], ("ms", tag), (tag,))
            for i in range(len(src) + 1):
                if i < len(src):
                    stt(dst[i], src[i], g[:, i:i + 1], nrm[:, 1, :], ALU.mult, ALU.mult, "xn", tag, i)
                if i and first is not None:
                    rest(tag, i - 1, dst[i - 1], first[:, i - 1, :], second[:, i - 1, :])

        hk8 = [h[:, i, :] for i in range(DC)]
        n8 = [normed[:, i, :] for i in range(DC)]

        def attention(tag, mode, table, between=None):
            pr = prob if mode == 1 else lprob

            def peak(u):
                hh, i = u // TT, u % TT
                n = (i + 1) * P
                v.wait_ge(*V.at("score", tag, u))
                last()
                if table is not None:
                    if u >= 2:
                        v.wait_ge(*V.at("turned", tag, u - 2))
                    v.tensor_tensor_reduce(pr[:, u % 2, 0:n], SC[u % 2][:, 0:n], bias[:, table + hh, S - n:S], 1.0, GONE,
                                           ALU.add, ALU.max, stat[:, u % 2, 0:1])\
                        .then_inc(*V.up("score_used", tag, u))
                else:
                    v.tensor_reduce(stat[:, u % 2, 0:1], SC[u % 2][:, 0:n], AX.X, ALU.max).then_inc(*V.up())
                last()
                ts(stat[:, u % 2, 1:2], stat[:, u % 2, 0:1], -1.0, None, ALU.mult, None, "negmax", tag, u)

            peak(0)
            for u in range(NH * TT):
                n = (u % TT + 1) * P
                if u + 1 < NH * TT:
                    peak(u + 1)
                v.wait_ge(*V.at(*(("expo", tag, u) if table is not None else ("score_used", tag, u))))
                v.reciprocal(stat[:, u % 2, 3:4], stat[:, u % 2, 2:3]).then_inc(*V.up())
                last()
                ts(pr[:, u % 2, 0:n], pr[:, u % 2, 0:n], stat[:, u % 2, 3:4], None, ALU.mult, None, "prob", tag, u)
                if between:
                    between(u)

        def branch_rest(b):
            for c in range(2):
                at = b % 2 * 2 + c
                v.wait_ge(*V.at("branch_first", b, c))
                tt(op_lo[:, at, :], attn[:, c, :], op_hi[:, at, :].bitcast(F32), ALU.subtract,
                   *(("branch_split", b) if c else ()))

        def gate_branch(b, g, gate, tmp):
            s = evac_start(("branch", b, g))
            v.wait_ge(*V.at("evac", "gate", b, g))
            for c in range(2):
                m = mixed[:, 2 * g + c, :]
                done = ("evac", "branch", b, g) if c else ()
                if b == 0:
                    tt(m, gate[:, c, :], bank[2 * s + c][:, :], ALU.mult, *done)
                else:
                    last()
                    tt(tmp[:, c, :], gate[:, c, :], bank[2 * s + c][:, :], ALU.mult, *done)
                    last()
                    tt(m, m, tmp[:, c, :], ALU.add, *(("mixed", 2 * g + c) if b == 3 else ()))

        def gates_behind(b):
            return lambda u: gate_branch(b, u // 4, gates[:, u // 4 % 2 * 2:, :], soft) if u % 4 == 3 else None

        v.memset(eps[:, :], EPS).then_inc(*V.up("eps"))
        v.memset(ones[:, 0, :], 1.0 / D).then_inc(*V.up())
        v.memset(ones[:, 1, :], 1.0 / 256).then_inc(*V.up())
        v.memset(ones[:, 2, :], 1.0 / 128).then_inc(*V.up())
        v.wait_ge(*V.at("params"))
        v.tensor_copy(levels[:, :], levels_in).then_inc(*V.up())
        v.wait_ge(*V.at("cols_in"))
        a0, a1 = (lcol[:, l * L_NROWS + 21:l * L_NROWS + 25] for l in range(LAYERS))
        e0, e1, m, r = (nrm[:, 2, 4 * i:4 * i + 4] for i in range(4))
        tt(m, a0, a1, ALU.max)
        last()
        tt(e0, a0, m, ALU.subtract)
        tt(e1, a1, m, ALU.subtract, "lb_in")
        v.wait_ge(*V.at("lb_exp"))
        tt(m, e0, e1, ALU.add)
        last()
        v.reciprocal(r, m).then_inc(*V.up())
        last()
        tt(e0, e0, r, ALU.mult)
        tt(e1, e1, r, ALU.mult)
        last()
        tt(m, e0, e1, ALU.add)
        v.memset(lbs[:, 0, 0, :], 0.0).then_inc(*V.up())
        v.memset(lbs[:, 0, 1, :], 1.0).then_inc(*V.up())
        last()
        tt(lbs[:, 1, 0, :], m, e0, ALU.subtract)
        last()
        ts(lbs[:, 1, 1, :], lbs[:, 1, 0, :], -1.0, 1.0, ALU.mult, ALU.add)

        norm("mix", hk8, n8, pcol[:, A_ROWS["mix"]:], xh, xl)
        def w_in_out(name):
            dst = dict(mbq=mbq, mbk=mbk, mbv=mbv, fxq=fxq, fxk=fxk, fxv=fxv, dsq=dsq, ix=ixq)[name]
            s = evac_start((name,))
            for b in range(2):
                d = dst[:, 2 * b:2 * b + 2, :].rearrange("p i d -> p (i d)") if name[2:] == "v" else dst[:, b, :]
                ts(d, bank[2 * s + b][:, :], HD ** -0.5 if name[2:] == "q" else 1.0, None, ALU.mult, None,
                   *(("evac", name) if b else ()))

        for u in range(NH * TT):
            n = (u % TT + 1) * P
            sp, pr, z = soft[:, u % 2, 0:n], prob[:, u % 2, 0:n], SC[u % 2][:, 0:n]
            v.wait_ge(*V.at("soft", u))
            last()
            stt(sp, z, 0.0, sp, ALU.max, ALU.add)
            last()
            if u >= 2:
                v.wait_ge(*V.at("turned", "sb", u - 2))
            v.tensor_tensor_scan(pr[:, ::-1], sp[:, ::-1], sp[:, ::-1], 0.0, ALU.add, ALU.bypass).then_inc(*V.up())
            last()
            tt(pr, z, pr, ALU.subtract, "score_used", "sb", u)
            if u and u % 2 == 0:
                w_in_out(SB_BEHIND[u // 2 - 1])
        w_in_out(SB_BEHIND[-1])
        branch_rest(0)
        v.wait_ge(*V.at("evac", "dst"))
        z = zlog[0:NH, 0:S]
        ts(z, z, cur[0:NH, 49:50], None, ALU.add, None, "zlog")
        v.wait_ge(*V.at("zsoft"))
        last()
        stt(z, z, 0.0, soft[0:NH, 0, :], ALU.min, ALU.subtract)
        last()
        v.tensor_tensor_scan(cum[0:NH, :], z, z, 0.0, ALU.add, ALU.bypass).then_inc(*V.up("cum"))
        attention("mb", 1, 0, gates_behind(0))
        branch_rest(1)
        n = 0
        for i in range(1, TT):
            w = (i + 1) * P
            acc = sel[:, i - 1, 0:w]
            for hh in range(8):
                r = soft[:, n % 2, 0:w]
                wcol = dsv[:, i, HD + hh:HD + hh + 1]
                v.wait_ge(*V.at("ix_used", n))
                last()
                if hh == 0:
                    ts(acc, r, wcol, None, ALU.mult, None, "ix_added", n)
                else:
                    stt(acc, r, wcol, acc, ALU.mult, ALU.add, "ix_added", n)
                n += 1
            last()
            tt(acc[:, i * P:w], acc[:, i * P:w], C("causal"), ALU.add)

        def largest_behind(u):
            for n in range(3 * u, 3 * u + 3):
                i, round_no = n // (TOPK // 8) + 1, n % (TOPK // 8)
                acc = sel[:, i - 1, 0:(i + 1) * P]
                last()
                v.max(top8, acc).then_inc(*V.up())
                last()
                v.match_replace(acc, top8, acc, GONE).then_inc(*V.up())
                if round_no == TOPK // 8 - 1:
                    last()
                    ts(acc, acc, -2e38, NEG, ALU.is_gt, ALU.mult, "sel", i - 1)
            gates_behind(1)(u)

        attention("fx", 1, None, largest_behind)
        branch_rest(2)

        def late_behind(u):
            for g in range(DC // 2):
                if unit_of(3 * g + 2) + 1 == u:
                    gate_branch(2, g, gates[:, g % 2 * 2:, :], soft)

        attention("ds", 1, 4, late_behind)
        branch_rest(3)
        for g in range(DC // 2):
            gate_branch(3, g, late_gates[:, 2 * g:, :], soft)
        for i in range(DC):
            rest("out", i, mixed[:, i, :], xh[:, i, :], xl[:, i, :])
        V.same("mixed_all")

        def add_slab(tag, key, m, scale, final):
            s = evac_start((*key, m))
            for b in range(2):
                c = 2 * m + b
                last()
                names = [("evac", *key, m)] if b else []
                if final:
                    names.append(("added", tag, c))
                stt(h[:, c, :], bank[2 * s + b][:, :], scale, h[:, c, :], ALU.mult, ALU.add,
                    *(names[0] if names else ()))
                if len(names) > 1:
                    V.same(*names[1])

        def proj(tag):
            for j in range(4):
                add_slab(tag, (tag,), j, 1.0, True)

        def ffn(tag, scale, up):
            def down(phase, half):
                for m in (2 * half, 2 * half + 1):
                    add_slab(tag, (tag, "d" + phase), m, scale, phase == "last")

            for j in range(2):
                up(tag, "first", 0, j)
            for _ in range(2):
                last()
                v.memset(stat[:, 0, 3:4], 0.0).then_inc(*V.up())
            with Fori(V, v, tag, FFN_LOOPS) as it:
                for phase, behind in (("odd", "even"), ("even", "odd")):
                    for j in range(2):
                        up(tag, phase, it, j)
                        down(behind, j)
            for half in range(2):
                down("last", half)

        def hidden_rest(tag, phase, j):
            at = UP[phase][2] + j
            v.wait_ge(*V.at("hh", tag, phase, j))
            tt(op_lo[:, at, :], hid[:, j, :], op_hi[:, at, :].bitcast(F32), ALU.subtract, "hidden", tag, phase, j)

        def gated_up(tag, phase, it, j):
            s = evac_start((tag, phase, j))
            v.wait_ge(*V.at("silu", tag, phase, j))
            tt(hid[:, j, :], silu[:, j, :], bank[2 * s + 1][:, :], ALU.mult, "evac", tag, phase, j)
            hidden_rest(tag, phase, j)

        def conv_up(tag, phase, it, j):
            m, n, _ = UP[phase]
            v.wait_ge(*V.at("evac", "c", phase, j))
            for a in range(2):
                ch = it * (2 * m) + (2 * n + j + a * FC)

                def col(t, c0=0):
                    return t[:, c0 + ch:c0 + ch + 1] if isinstance(ch, int) else t[:, bass.ds(ch + c0, 1)]
                src, dst = padded[:, 2 * j + a, :], conv[:, 2 * j + a, :]
                last()
                ts(dst, src[:, 0:S], col(convw[:, 0, :]), col(pcol, A_ROWS["conv_b"]), ALU.mult, ALU.add)
                for n3 in (1, 2):
                    last()
                    stt(dst, src[:, n3:n3 + S], col(convw[:, n3, :]), dst, ALU.mult, ALU.add,
                        *(("conv_g", phase, j) if n3 == 2 and a == 0 else ()))
            v.wait_ge(*V.at("gelu", phase, j))
            last()
            tt(hid[:, j, :], silu[:, j, :], conv[:, 2 * j + 1, :], ALU.mult, "hid", phase, j)
            hidden_rest("c", phase, j)

        proj("out")
        norm("ffn", hk8, n8, pcol[:, A_ROWS["ffn"]:], xh, xl)
        v.memset(padded[:, :, 0:2], 0.0).then_inc(*V.up("pad_zero"))
        v.wait_ge(*V.at("decay"))
        v.tensor_copy(nrm[:, 0, :], pos_i[:, :].bitcast(I32)).then_inc(*V.up())
        last()
        c1, c2 = 6.28125, 0.0019350051879882812
        c3 = TWO_PI - c1 - c2
        magic = 12582912.0
        for n, (col, turns) in enumerate(((0, 0.25), (0, 0.0), (2, 0.25), (2, 0.0))):
            a, q, r = nrm[:, 1, :], nrm[:, 2, :], rtmp[:, n, :]
            ts(a, nrm[:, 0, :], C("cols")[:, col:col + 1], None, ALU.mult, None)
            last()
            ts(q, a, 1.0 / TWO_PI, turns, ALU.mult, ALU.add)
            last()
            ts(q, q, magic, None, ALU.add, None)
            last()
            ts(q, q, -magic, None, ALU.add, None)
            last()
            stt(r, q, -c1, a, ALU.mult, ALU.add)
            last()
            stt(r, q, -c2, r, ALU.mult, ALU.add)
            last()
            stt(r, q, -c3, r, ALU.mult, ALU.add)
            last()
            if turns:
                ts(r, r, TWO_PI / 4, None, ALU.add, None)
                last()
            ts(r, r, 3.1415925, -3.1415925, ALU.min, ALU.max, "angle", n)
            last()
        for n, col in ((1, 1), (3, 3)):
            v.wait_ge(*V.at("sin", n))
            ts(rope[:, n, :], rope[:, n, :], C("cols")[:, col:col + 1], None, ALU.mult, None, "rope", n)
        ffn("c", 1.0, conv_up)
        norm("fin1", hk8, hk8, pcol[:, A_ROWS["fin1"]:])

        with Fori(V, v, "layer", LAYERS) as l:
            last()
            v.tensor_copy(cur[:, 0:L_NROWS], lcol[:, bass.ds(l * L_NROWS, L_NROWS)]).then_inc(*V.up())
            v.tensor_copy(cur[:, L_NROWS:L_NROWS + 8].rearrange("p (o a h) -> p o a h", o=1, a=2),
                          lbs[:, bass.ds(l, 1), :, :]).then_inc(*V.up())

            def g(name):
                return cur[:, L_ROWS[name]:]

            norm("f1", hk8, n8, g("ffn1"), xh, xl)
            ffn("f", 0.5, gated_up)
            norm("lm", hk8, n8, g("mix"), xh, xl)
            norm("q", [cq[:, i, :] for i in range(2)], [cq[:, i, :] for i in range(2)], g("q"), op_hi, op_lo)
            norm("kv", [ckv], [ckv], g("kv"), op_hi[:, 2:, :], op_lo[:, 2:, :])
            for n in range(NH + 1):
                x0 = qh[64:96, n, :] if n < NH else kh[64:96, 0, :]
                t0 = lprob[64:96, n % 2, :]
                v.wait_ge(*V.at("swapped", n))
                last()
                tt(t0, SC[n % 2][64:96, :], rope[64:96, 3, :], ALU.mult, "rot_used", n)
                tt(x0, x0, rope[64:96, 2, :], ALU.mult)
                last()
                tt(x0, x0, t0, ALU.add)
            last()
            for n in range(1, NH):
                v.tensor_copy(kh[64:96, n, :], kh[64:96, 0, :]).then_inc(*V.up(*(("k_rot",) if n == NH - 1 else ())))
            attention("ml", 2, None)
            for hh in range(NH):
                f = hS[:, hh, :]
                last()
                ts(f, f, cur[:, L_NROWS + 4 + hh:L_NROWS + 5 + hh], cur[:, L_NROWS + hh:L_NROWS + 1 + hh],
                   ALU.mult, ALU.add)
                last()
                ts(hk[:, hh, :], f, -1.0, 1.0, ALU.mult, ALU.add)
                ts(f, f, 2.0 ** -63, None, ALU.max, None, "forget", hh)
            v.wait_ge(*V.at("evac", "zv", 0))
            for i in range(TT):
                zi, st = zv[:, i, :], sgst[:, i, :]
                v.tensor_reduce(st[:, 0:1], zi, AX.X, ALU.add).then_inc(*V.up())
                last()
                ts(st[:, 0:1], st[:, 0:1], -1.0 / 256, None, ALU.mult, None)
                last()
                ts(zi, zi, st[:, 0:1], None, ALU.add, None)
                last()
                v.tensor_tensor_reduce(nrm[:, 2, 0:256], zi, zi, 1.0 / 256, 0.0, ALU.mult, ALU.add, st[:, 1:2])\
                    .then_inc(*V.up())
                last()
            ts(sgst[:, :, 2], sgst[:, :, 1], EPS, None, ALU.add, None, "sgvar")
            v.wait_ge(*V.at("sgroot"))
            newton(sgst[:, :, 2], sgst[:, :, 3], sgst[:, :, 4])
            for i in range(TT):
                ts(zv[:, i, :], zv[:, i, :], sgst[:, i, 3:4], None, ALU.mult, None, *(("zv_normed",) if i == TT - 1 else ()))
            v.wait_ge(*V.at("sgw_turned"))
            tt(sgwT, PT[:, :].rearrange("p (h t) -> p h t", h=NH), C("tril")[:, None, :].to_broadcast([P, NH, P]),
               ALU.mult, "sgwT")
            for c in range(2):
                y = lprobT[:, 1, :]
                v.wait_ge(*V.at("sgbb"))
                v.wait_ge(*V.at("sg_mixed", c))
                last()
                stt(y.rearrange("p (i t) -> p i t", i=TT), (PT if c == 0 else OB)[:, :].rearrange("p (i t) -> p i t", i=TT),
                    g("sg")[:, c:c + 1], sgbb[:, c:c + 1, :].to_broadcast([P, TT, P]), ALU.mult, ALU.add)
                last()
                tt(zu[:, c, :], zu[:, c, :], y, ALU.mult, "sg_out", c)

            for n in range(4):
                x0 = (rq, rk)[n // 2][:, n % 2, :]
                t0 = lprobT[:, n % 2, :]
                v.wait_ge(*V.at("ret_swap", n))
                last()
                tt(t0, SC[n % 2][:, :], rope[:, 1, :], ALU.mult)
                tt(x0, x0, rope[:, 0, :], ALU.mult)
                last()
                tt(x0, x0, t0, ALU.add, "ret_rot", n)

            def recurrence_start():
                last()
                v.memset(hQ, 0.0).then_inc(*V.up())
                v.memset(hK, 0.0).then_inc(*V.up())
                v.memset(scT, 0.0).then_inc(*V.up())
                tail(0)

            def tail(hh):
                f4 = hS[:, hh, :].rearrange("p (n m) -> p n m", n=TT)
                tt(hE[:, 0, :].rearrange("p (n m) -> p n m", n=TT), f4[:, :, P - 1:P].to_broadcast([P, TT, P]), f4,
                   ALU.subtract, "tail", hh)

            def group_out(tag, c, gain, gate, centred):
                if centred:
                    v.wait_ge(*V.at("gmean", tag, c))
                    last()
                    tt(gn[:, 0, :], gn[:, 0, :], PT[:, :], ALU.subtract, "gcentred", tag, c)
                    if c:
                        recurrence_start()
                rstd(PT[:, :], ("gms", tag, c), (tag, c))
                stt(gn[:, 1, :], gn[:, 0, :], gain[:, c:c + 1], nrm[:, 1, :], ALU.mult, ALU.mult)
                last()
                tt(gate[:, c, :], gate[:, c, :], gn[:, 1, :], ALU.mult, "gout", tag, c)

            for u in range(NH * TT):
                hh, j = u // TT, u % TT
                n = S - j * P
                v.wait_ge(*V.at("ret_score", u))
                tt(lprob[:, u % 2, 0:n], SC[u % 2][:, 0:n], decay[:, hh, 0:n], ALU.mult, "ret_w", u)
                if u in (2 * TT, 4 * TT - 1):
                    group_out("r", u // (3 * TT), g("ret"), rgate, True)
                if j == 1:
                    v.wait_ge(*V.at("logf", hh))
                    for i in range(TT):
                        f = hS[:, hh, i * P:i * P + P]
                        v.tensor_tensor_scan(f, f, f, 0.0, ALU.add, ALU.bypass).then_inc(*V.up())

            n = 0
            for hh in range(NH):
                f = hS[:, hh, :]
                f4 = f.rearrange("p (n m) -> p n m", n=TT)

                def split(a, m):
                    a = a.rearrange("p (n two m) -> p n two m", two=2, m=m)
                    return a[:, :, 0, :], a[:, :, 1, :]

                def distances(lv):
                    m = LEVELS[lv]
                    early, late = split(f, m)
                    e_early, e_late = split(hE[:, lv % 2, :], m)
                    ref = early[:, :, m - 1:m].to_broadcast([P, S // (2 * m), m])
                    last()
                    tt(e_late, late, ref, ALU.subtract)
                    tt(e_early, ref, early, ALU.subtract, "lvl_d", hh, lv)

                def masked(x):
                    lx = x % (len(LEVELS) + 1)
                    v.wait_ge(*V.at("lvl", x))
                    last()
                    v.memset(stat[:, 0, 3:4], 0.0).then_inc(*V.up())
                    m = levels[:, lx * P:lx * P + P][:, None, :].to_broadcast([P, TT, P])
                    v.copy_predicated(scT.rearrange("p (i t) -> p i t", i=TT), m,
                                      SC[x % 2][:, :].rearrange("p (i t) -> p i t", i=TT)).then_inc(*V.up("lvl_used", x))

                if hh:
                    last()
                    tail(hh)
                v.wait_ge(*V.at("head_exp", hh))
                if hh:
                    v.wait_ge(*V.at("off", hh - 1, 1))
                tt(qd, hq[:, hh, :], hE[:, 1, :], ALU.mult)
                tt(kd, hk[:, hh, :], hE[:, 0, :], ALU.mult)
                last()
                kvs = kv3.rearrange("p (c t) -> p c t", c=3)
                ts(kvs[:, 0, :], kd[:, 0:P], dend[:, 1:2], None, ALU.mult, None)
                ts(kvs[:, 1, :], kd[:, P:2 * P], dend[:, 2:3], None, ALU.mult, None)
                last()
                ts(kvs[:, 2, :], kvs[:, 0, :], dend[:, 2:3], None, ALU.mult, None, "kv3", hh)
                distances(0)
                for lv in range(len(LEVELS)):
                    if lv + 1 < len(LEVELS):
                        distances(lv + 1)
                    m = LEVELS[lv]
                    e_early, e_late = split(hE[:, lv % 2, :], m)
                    v.wait_ge(*V.at("lvl_e", hh, lv))
                    if n >= 2:
                        v.wait_ge(*V.at("lvl", n - 2))
                    last()
                    tt(split(hQ[:, lv % 2, :], m)[1], split(hq[:, hh, :], m)[1], e_late, ALU.mult)
                    tt(split(hK[:, lv % 2, :], m)[0], split(hk[:, hh, :], m)[0], e_early, ALU.mult, "lvl_k", hh, lv)
                    if lv:
                        masked(n - 1)
                    if (hh, lv) == (2, 2):
                        group_out("h", 0, g("hg"), hgate, False)
                    n += 1
                n += 1
                masked(n - 2)
                masked(n - 1)
            parts = (cq, zu, hgate, rgate)
            for i in (0, 1, 2, 3, 6, 7):
                rest("lout", i, parts[i // 2][:, i % 2, :], xh[:, i, :], xl[:, i, :])
            group_out("h", 1, g("hg"), hgate, False)
            for i in (4, 5):
                rest("lout", i, hgate[:, i % 2, :], xh[:, i, :], xl[:, i, :])
            v.memset(stat[:, 0, 3:4], 0.0).then_inc(*V.up())
            proj("lout")
            norm("f2", hk8, n8, g("ffn2"), xh, xl)
            ffn("g", 0.5, gated_up)
            norm("pl", hk8, n8, g("ple"), xh, xl)
            for c in range(2):
                v.wait_ge(*V.at("p_first", c))
                tt(op_lo[:, c, :], SC[c][:, :], op_hi[:, c, :].bitcast(F32), ALU.subtract, *(("p_split",) if c else ()))
            with Fori(V, v, "ple", DC // 4) as it:
                for j in range(2):
                    s = evac_start(("branch", "p", j))
                    v.wait_ge(*V.at("evac", "gate", "p", j))
                    for c in range(2):
                        a = sg8[:, 2 * j + c:2 * j + c + 1, :]
                        last()
                        tt(a, a, bank[2 * s + c][:, :].rearrange("p (c t) -> p c t", c=1), ALU.mult)
                        last()
                        hc = h[:, bass.ds(it * 4 + (2 * j + c), 1), :]
                        tt(hc, hc, a, ALU.add, *(("evac", "branch", "p", j) if c else ()))
        norm("fin", hk8, n8, pcol[:, A_ROWS["fin2"]:])


_INS = ["x", "norm_mix_g", "norm_ffn_g", "norm_final_g", "w_in", "fox_b_f", "t5_bias", "w_gate", "w_branch", "w_out",
        "w_up", "conv_w", "conv_b", "w_down", "p_2", "positions_2", "ffn1_norm_2", "ffn1_w_gate_2", "ffn1_w_up_2",
        "ffn1_w_down_2", "mix_norm_2", "w_in_2", "mla_q_norm_2", "mla_w_uq_2", "mla_kv_norm_2", "mla_w_ukv_2",
        "sg_ln_2", "sg_w_s_2", "sg_b_s_2", "hg_lb_logits_2", "hg_norm_2", "ret_norm_2", "w_out_2", "ffn2_norm_2",
        "ffn2_w_gate_2", "ffn2_w_up_2", "ffn2_w_down_2", "ple_norm_2", "ple_w_proj_2", "ple_w_gate_2",
        "final_norm_2"]


def build(nc, arrays, known=None):
    k = {n: nc.dram_tensor(f"in_{n}", a.shape, mybir.dt.from_np(a.dtype), kind="ExternalInput").ap()
         for n, a in arrays.items()}
    out = nc.dram_tensor("out_0", (1, S, D), F32, kind="ExternalOutput").ap()
    scratch = nc.dram_tensor("t5_by_distance", (8, 640), F32).ap()
    book = Book(known)
    program(nc, k["x"][0], out[0], k, scratch, book)
    return book


def kernel(**inputs):
    import concourse.bacc as bacc
    from concourse.bass_utils import run_bass_kernel_spmd

    arrays = {n: np.ascontiguousarray(inputs[n]) for n in _INS}
    arrays["const"] = np.concatenate(list(constants().values()), 1)
    arrays.update(first_constants())
    arrays["levels"] = level_masks()
    arrays["decay"] = decays()
    counted = build(bacc.Bacc("TRN2", target_bir_lowering=False, num_devices=1), arrays)
    nc = bacc.Bacc("TRN2", target_bir_lowering=False, num_devices=1)
    build(nc, arrays, counted)
    r = run_bass_kernel_spmd(nc, [{f"in_{n}": a for n, a in arrays.items()}], core_ids=[0])
    return r.results[0]["out_0"]
```
